# Optimizing a Trainium2 kernel written in Bass

```python
import math
import jax, jax.numpy as jnp
from jax import lax
import numpy as np

D_MODEL = 1024
BATCH = 1
SEQ = 2048
DEPTH = 1

HEAD_DIM = 64
ATTN_GROUPS = ((128, 1), (512, 4), (2048, 16))
N_ATTN_GROUPS = len(ATTN_GROUPS)
HEADS_PER_GROUP = 8
N_ATTN_HEADS = N_ATTN_GROUPS * HEADS_PER_GROUP
ATTN_OUT_WIDTH = HEADS_PER_GROUP * HEAD_DIM
QKV_WIDTH = 3 * N_ATTN_HEADS * HEAD_DIM
BLOCK = 128
REL_BUCKETS = 32
REL_MAX_DIST = 2048
SSM_WIDTH = D_MODEL // 2
SSM_GROUP = 16
SSM_GROUPS = SSM_WIDTH // SSM_GROUP
SSM_STATE = 64
IN_WIDTH = QKV_WIDTH + SSM_WIDTH + 2 * D_MODEL
N_EXPERTS = 32
TOP_K = 4
D_FF = D_MODEL
SWIGLU_LIMIT = 7.0
SWIGLU_ALPHA = 1.702
EPS = 1e-6

kernel_name = "hybrid_dilated_attn_s5_moe_block"

def rms_norm(x, g):
    xf = x.astype(jnp.float32)
    y = xf * lax.rsqrt(jnp.mean(xf * xf, axis=-1, keepdims=True) + EPS) * g.astype(jnp.float32)
    return y.astype(x.dtype)

def head_rms_norm(t, g):
    tf = t.astype(jnp.float32)
    return tf * lax.rsqrt(jnp.mean(tf * tf, axis=-1, keepdims=True) + EPS) * g.astype(jnp.float32)[:, None, :]

def rel_bucket_np(dist):
    max_exact = REL_BUCKETS // 2
    d = np.maximum(dist, 1).astype(np.float32)
    large = max_exact + (np.log(d / max_exact) / math.log(REL_MAX_DIST / max_exact)
                         * (REL_BUCKETS - max_exact)).astype(np.int32)
    large = np.minimum(large, REL_BUCKETS - 1)
    return np.where(dist < max_exact, dist, large).astype(np.int32)

def dilated_window_attention(q, k, v, bias_table, window, dilation):
    b, s, h, dh = q.shape
    span = window // dilation
    L = s // dilation
    blk = min(BLOCK, L)
    nblk = -(-L // blk)
    Lp = nblk * blk

    def to_blocks(t):
        t = t.reshape(b, L, dilation, h, dh).transpose(0, 2, 1, 3, 4).reshape(b * dilation, L, h, dh)
        t = jnp.pad(t, ((0, 0), (0, Lp - L), (0, 0), (0, 0)))
        return t.reshape(b * dilation, nblk, blk, h, dh)

    def with_prev(t):
        prev = jnp.pad(t, ((0, 0), (1, 0), (0, 0), (0, 0), (0, 0)))[:, :-1]
        return jnp.concatenate([prev, t], axis=2)

    qb = to_blocks(q)
    kc = with_prev(to_blocks(k))
    vc = with_prev(to_blocks(v))

    qi = np.arange(blk)[:, None]
    ki = np.arange(2 * blk)[None, :]
    steps = qi + blk - ki
    band = (steps >= 0) & (steps <= span)
    key_pos = np.arange(nblk)[:, None] * blk - blk + np.arange(2 * blk)[None, :]
    mask = band[None] & (key_pos >= 0)[:, None, :]
    bucket = rel_bucket_np(np.clip(steps, 0, None) * dilation)
    bias = jnp.transpose(bias_table[bucket], (2, 0, 1)).astype(jnp.float32)

    logits = jnp.einsum('nbqhd,nbkhd->nbhqk', qb, kc) + bias
    logits = jnp.where(mask[None, :, None], logits, -jnp.inf)
    m = jnp.max(logits, axis=-1, keepdims=True)
    p = jnp.exp(logits - m)
    den = jnp.sum(p, axis=-1)
    o = jnp.einsum('nbhqk,nbkhd->nbqhd', p, vc) / jnp.transpose(den, (0, 1, 3, 2))[..., None]
    lse = jnp.transpose(m[..., 0] + jnp.log(den), (0, 1, 3, 2))

    o = o.reshape(b, dilation, Lp, h, dh)[:, :, :L].transpose(0, 2, 1, 3, 4).reshape(b, s, h, dh)
    lse = lse.reshape(b, dilation, Lp, h)[:, :, :L].transpose(0, 2, 1, 3).reshape(b, s, h)
    return o, lse

def s5_ssm(u, a_re, a_im, log_dt, b_re, b_im, c_re, c_im, d_skip):
    bsz, s, _ = u.shape
    uf = u.astype(jnp.float32).reshape(bsz, s, SSM_GROUPS, SSM_GROUP)
    lam = lax.complex(a_re.astype(jnp.float32), a_im.astype(jnp.float32))
    dt = jnp.exp(log_dt.astype(jnp.float32))[:, None]
    a_bar = jnp.exp(lam * dt)
    b_mat = lax.complex(b_re.astype(jnp.float32), b_im.astype(jnp.float32))
    b_bar = ((a_bar - 1.0) / lam)[..., None] * b_mat
    bu = jnp.einsum('bsgc,gnc->bsgn', uf.astype(jnp.complex64), b_bar)
    a_full = jnp.broadcast_to(a_bar, bu.shape)

    def combine(earlier, later):
        a1, b1 = earlier
        a2, b2 = later
        return a2 * a1, a2 * b1 + b2

    _, states = lax.associative_scan(combine, (a_full, bu), axis=1)
    c_mat = lax.complex(c_re.astype(jnp.float32), c_im.astype(jnp.float32))
    y = jnp.einsum('bsgn,gcn->bsgc', states, c_mat).real
    y = y + d_skip.astype(jnp.float32).reshape(SSM_GROUPS, SSM_GROUP) * uf
    return y.reshape(bsz, s, SSM_WIDTH).astype(u.dtype)

def moe_ffn(h, w_router, b_router, w_gu, b_gu, w_down, b_down):
    b, s, d = h.shape
    t = h.reshape(-1, d)
    logits = (t @ w_router + b_router).astype(jnp.float32)
    top_v, top_i = lax.top_k(logits, TOP_K)
    gates = jax.nn.softmax(top_v, axis=-1)
    flat_e = top_i.reshape(-1)
    order = jnp.argsort(flat_e)
    e_sorted = flat_e[order]
    tok = order // TOP_K
    xs = t[tok]
    sizes = jnp.bincount(flat_e, length=N_EXPERTS).astype(jnp.int32)
    gu = lax.ragged_dot(xs, w_gu, sizes) + b_gu[e_sorted]
    x_glu = jnp.minimum(gu[:, :D_FF], SWIGLU_LIMIT)
    x_lin = jnp.clip(gu[:, D_FF:], -SWIGLU_LIMIT, SWIGLU_LIMIT)
    act = x_glu * jax.nn.sigmoid(SWIGLU_ALPHA * x_glu) * (x_lin + 1.0)
    out = lax.ragged_dot(act, w_down, sizes) + b_down[e_sorted]
    out = out * gates.reshape(-1)[order][:, None].astype(out.dtype)
    y = jnp.zeros_like(t).at[tok].add(out)
    return y.reshape(b, s, d)

def setup_inputs(seed: int = 0) -> dict:
    key = jax.random.key(seed)
    ks = jax.random.split(key, 26)
    f32 = jnp.float32
    L = DEPTH
    nrm = lambda k, shape, scale: jax.random.normal(k, shape, f32) * scale
    n_idx = jnp.arange(SSM_STATE, dtype=f32)
    return {
        "x": nrm(ks[0], (BATCH, SEQ, D_MODEL), 1.0),
        "g_mix": 1.0 + nrm(ks[1], (L, D_MODEL), 0.02),
        "w_in": nrm(ks[2], (L, D_MODEL, IN_WIDTH), D_MODEL ** -0.5),
        "q_gain": 1.0 + nrm(ks[3], (L, N_ATTN_GROUPS, HEAD_DIM), 0.02),
        "k_gain": 1.0 + nrm(ks[4], (L, N_ATTN_GROUPS, HEAD_DIM), 0.02),
        "rel_bias": nrm(ks[5], (REL_BUCKETS, N_ATTN_HEADS), 0.5),
        "ssm_a_re": -0.5 + nrm(ks[6], (L, SSM_GROUPS, SSM_STATE), 0.01),
        "ssm_a_im": math.pi * n_idx + nrm(ks[7], (L, SSM_GROUPS, SSM_STATE), 0.01),
        "ssm_log_dt": jax.random.uniform(ks[8], (L, SSM_GROUPS), f32, math.log(1e-3), math.log(1e-1)),
        "ssm_b_re": nrm(ks[9], (L, SSM_GROUPS, SSM_STATE, SSM_GROUP), (2 * SSM_GROUP) ** -0.5),
        "ssm_b_im": nrm(ks[10], (L, SSM_GROUPS, SSM_STATE, SSM_GROUP), (2 * SSM_GROUP) ** -0.5),
        "ssm_c_re": nrm(ks[11], (L, SSM_GROUPS, SSM_GROUP, SSM_STATE), (2 * SSM_STATE) ** -0.5),
        "ssm_c_im": nrm(ks[12], (L, SSM_GROUPS, SSM_GROUP, SSM_STATE), (2 * SSM_STATE) ** -0.5),
        "ssm_d": nrm(ks[13], (L, SSM_WIDTH), 1.0),
        "w_glu": nrm(ks[14], (L, SSM_WIDTH, SSM_WIDTH), SSM_WIDTH ** -0.5),
        "b_glu": nrm(ks[15], (L, SSM_WIDTH), 0.01),
        "w_attn_proj": nrm(ks[16], (L, ATTN_OUT_WIDTH, D_MODEL), ATTN_OUT_WIDTH ** -0.5),
        "w_ssm_proj": nrm(ks[17], (L, SSM_WIDTH, D_MODEL), SSM_WIDTH ** -0.5),
        "w_out": nrm(ks[18], (L, D_MODEL, D_MODEL), D_MODEL ** -0.5),
        "g_ffn": 1.0 + nrm(ks[19], (L, D_MODEL), 0.02),
        "w_router": nrm(ks[20], (L, D_MODEL, N_EXPERTS), D_MODEL ** -0.5),
        "b_router": nrm(ks[21], (L, N_EXPERTS), 0.01),
        "w_gate_up": nrm(ks[22], (L, N_EXPERTS, D_MODEL, 2 * D_FF), D_MODEL ** -0.5),
        "b_gate_up": nrm(ks[23], (L, N_EXPERTS, 2 * D_FF), 0.01),
        "w_down": nrm(ks[24], (L, N_EXPERTS, D_FF, D_MODEL), D_FF ** -0.5),
        "b_down": nrm(ks[25], (L, N_EXPERTS, D_MODEL), 0.01),
    }

def reference(x, g_mix, w_in, q_gain, k_gain, rel_bias, ssm_a_re, ssm_a_im, ssm_log_dt,
              ssm_b_re, ssm_b_im, ssm_c_re, ssm_c_im, ssm_d, w_glu, b_glu, w_attn_proj,
              w_ssm_proj, w_out, g_ffn, w_router, b_router, w_gate_up, b_gate_up, w_down, b_down):
    b, s, _ = x.shape
    for l in range(DEPTH):
        h = rms_norm(x, g_mix[l])
        proj = h @ w_in[l]
        qkv = proj[..., :QKV_WIDTH].reshape(b, s, 3, N_ATTN_GROUPS, HEADS_PER_GROUP, HEAD_DIM)
        u = proj[..., QKV_WIDTH:QKV_WIDTH + SSM_WIDTH]
        gate_a = proj[..., QKV_WIDTH + SSM_WIDTH:QKV_WIDTH + SSM_WIDTH + D_MODEL]
        gate_b = proj[..., QKV_WIDTH + SSM_WIDTH + D_MODEL:]

        q = head_rms_norm(qkv[:, :, 0], q_gain[l]) * (HEAD_DIM ** -0.5)
        k = head_rms_norm(qkv[:, :, 1], k_gain[l])
        v = qkv[:, :, 2].astype(jnp.float32)
        outs, lses = [], []
        for gi, (window, dilation) in enumerate(ATTN_GROUPS):
            table = rel_bias[:, gi * HEADS_PER_GROUP:(gi + 1) * HEADS_PER_GROUP]
            o_g, lse_g = dilated_window_attention(q[:, :, gi], k[:, :, gi], v[:, :, gi], table, window, dilation)
            outs.append(o_g)
            lses.append(lse_g)
        w_den = jax.nn.softmax(jnp.stack(lses, axis=0), axis=0)
        attn = jnp.einsum('gbsh,gbshd->bshd', w_den, jnp.stack(outs, axis=0))
        y_a = attn.reshape(b, s, ATTN_OUT_WIDTH).astype(x.dtype) @ w_attn_proj[l]

        y_s = s5_ssm(u, ssm_a_re[l], ssm_a_im[l], ssm_log_dt[l], ssm_b_re[l], ssm_b_im[l],
                     ssm_c_re[l], ssm_c_im[l], ssm_d[l])
        y_s = jax.nn.gelu(y_s)
        y_s = y_s * jax.nn.sigmoid(y_s @ w_glu[l] + b_glu[l])
        y_b = y_s @ w_ssm_proj[l]

        mixed = jax.nn.sigmoid(gate_a) * y_a + jax.nn.sigmoid(gate_b) * y_b
        x = x + mixed @ w_out[l]

        h2 = rms_norm(x, g_ffn[l])
        x = x + moe_ffn(h2, w_router[l], b_router[l], w_gate_up[l], b_gate_up[l], w_down[l], b_down[l])
    return x


_drawn_inputs = setup_inputs


def setup_inputs(seed=0):
    import zlib

    import numpy as np

    out = dict(_drawn_inputs(seed))
    spreads = {}
    factors = {'g_mix': 2.929,
     'q_gain': 4.985,
     'k_gain': 5.45,
     'ssm_a_re': 200.0,
     'b_glu': 26.072,
     'b_gate_up': 8.0,
     'b_down': 22.792,
     'ssm_a_im': 21.805,
     'ssm_log_dt': 22.867,
     'ssm_b_re': 28.334,
     'ssm_b_im': 31.744,
     'ssm_c_re': 32.056,
     'ssm_c_im': 31.592,
     'b_router': 4.238}
    for name, (base, spread) in spreads.items():
        noise = np.random.default_rng([zlib.crc32(name.encode()), seed]).standard_normal(out[name].shape)
        drawn = base * np.exp(spread * noise) if base else spread * noise
        out[name] = __import__('jax').numpy.asarray(drawn.astype(out[name].dtype))
    for name, factor in factors.items():
        out[name] = (out[name] * factor).astype(out[name].dtype)
    return out
```

```python
from contextlib import ExitStack

import numpy as np

import concourse.bass as bass
from concourse import mybir

ALU = mybir.AluOpType
ACT = mybir.ActivationFunctionType
AX = mybir.AxisListType
F32 = mybir.dt.float32
I32 = mybir.dt.int32
U32 = mybir.dt.uint32
ds = bass.ds

P = 128
D = 1024
KD = D // P
S = 2048
NT = S // P
DH = 64
GROUPS = ((128, 1), (512, 4), (2048, 16))
HG = 8
AW = HG * DH
NFT = AW // P
QKV = 3 * len(GROUPS) * AW
EPS = 1e-6
CH = 512
NCH = S // CH
NBLK = CH // P
MASKED = 1e30
BUCKETS, MAX_DIST = 32, 2048
STEPS_W = 384
RW = DH + 2
SW = 512
SG, SC, SN = 32, 16, 64
PAIRS = SG // 2
TS = 8
NC = S // TS
HC = NC // P
LEVELS = NC.bit_length() - 1
NE = 32
TOPK = 4
FF = 1024
NF = FF // P
CAP = 384
NGT = CAP // P
REGION = -(-S // CAP) * CAP
MAX_TILES = S * TOPK // CAP + NE
DUMP = S + CAP
LIMIT, ALPHA = 7.0, 1.702


class Tools:

    def __init__(self, nc, ctx, tag):
        self.nc, self.ctx, self.tag, self.taken = nc, ctx, tag, []
        ctx.callback(self.give_back)

    def sb(self, name, shape, dt=F32):
        return self.ctx.enter_context(self.nc.sbuf_tensor(f"{self.tag}_{name}", list(shape), dt))

    def ps(self, name, shape=(P, 512), dt=F32):
        return self.ctx.enter_context(self.nc.psum_tensor(f"{self.tag}_{name}", list(shape), dt))

    def sem(self, name):
        self.taken.append(self.nc.alloc_semaphore(f"{self.tag}_{name}"))
        return self.taken[-1]

    def give_back(self):
        if self.taken:
            with self.nc.Block() as block:
                @block.gpsimd
                def _(pool):
                    for sem in self.taken:
                        pool.sem_clear(sem)
            for sem in self.taken:
                self.nc.release_semaphore(sem)

    def sems(self, names):
        return [self.sem(n) for n in names.split()]


class Steps:

    def __init__(self, eng, sem, base=0):
        self.eng, self.sem, self.base, self.n = eng, sem, base, 0

    def __call__(self, ins):
        self.n += 1
        ins.then_inc(self.sem, 1)
        self.eng.wait_ge(self.sem, self.base + self.n)


def stop_until(eng, sem, value, tick):
    eng.wait_ge(sem, value)
    eng.sem_inc(tick, 1)


def on_rows(row, n):
    return row.rearrange("(a w) -> a w", a=1).to_broadcast([n, row.shape[0]])


def make_constants(nc, ident, jflip, upper, ones):
    with ExitStack() as ctx:
        t_ = Tools(nc, ctx, "cst")
        filled, made = t_.sems("filled made")
        with nc.Block() as block:
            @block.gpsimd
            def _(pool):
                pool.memset(ident[:, :], 0.0).then_inc(filled, 1)
                pool.memset(jflip[:, :], 0.0).then_inc(filled, 1)
                pool.memset(upper[:, :], 0.0).then_inc(filled, 1)
                pool.memset(ones[:, :], 1.0).then_inc(made, 1)
                pool.wait_ge(filled, 3)
                pool.affine_select(out=ident[:, :], in_=ident[:, :], compare_op=ALU.not_equal, fill=1.0, base=0,
                                   pattern=[[-1, P]], channel_multiplier=1).then_inc(made, 1)
                pool.affine_select(out=jflip[:, :], in_=jflip[:, :], compare_op=ALU.not_equal, fill=1.0,
                                   base=1 - P, pattern=[[1, P]], channel_multiplier=1).then_inc(made, 1)
                pool.affine_select(out=upper[:, :], in_=upper[:, :], compare_op=ALU.is_ge, fill=1.0, base=0,
                                   pattern=[[-1, P]], channel_multiplier=1).then_inc(made, 1)
                pool.wait_ge(made, 4)


def normalise_input(nc, x, g_row, hT, ident):
    with ExitStack() as ctx:
        t_ = Tools(nc, ctx, "nrm")
        xt = [t_.sb(f"x{s}", [P, D]) for s in range(2)]
        hh = [t_.sb(f"h{s}", [P, D]) for s in range(2)]
        gb = t_.sb("gb", [P, D])
        junk = t_.sb("junk", [P, D])
        ss, ms, rms, rstd = (t_.sb(n, [P, 2]) for n in ("ss", "ms", "rms", "rstd"))
        pt = [[t_.ps(f"pt{s}{h}") for h in range(2)] for s in range(2)]
        x_in = [t_.sem(f"x_in{s}") for s in range(2)]
        g_in, step, ms_ready, rms_ready, h_ready, t_ready, t_free = t_.sems(
            "g_in step ms_ready rms_ready h_ready t_ready t_free")
        with nc.Block() as block:
            @block.sync
            def _(sp):
                sp.dma_start(gb[:, :], on_rows(g_row, P)).then_inc(g_in, 16)
                with sp.Fori(0, NT // 2) as i:
                    for s in range(2):
                        sp.wait_ge(h_ready, 2 * i + s + 1)
                        sp.dma_start(xt[s][:, :], x[ds(i * (2 * P) + s * P, P), :]).then_inc(x_in[s], 16)

            @block.vector
            def _(dve):
                dve.sem_inc(h_ready, 2)
                dve.wait_ge(g_in, 16)
                with dve.Fori(0, NT // 2) as i:
                    chain = Steps(dve, step, 4 * i)
                    for s in range(2):
                        dve.wait_ge(x_in[s], 16 * i + 16)
                        chain(dve.tensor_tensor_reduce(junk[:, :], xt[s][:, :], xt[s][:, :], 1.0, 0.0, ALU.mult,
                                                       ALU.add, ss[:, s:s + 1]))
                        dve.tensor_scalar(ms[:, s:s + 1], ss[:, s:s + 1], 1.0 / D, EPS, ALU.mult,
                                          ALU.add).then_inc(ms_ready, 1)
                        dve.wait_ge(rms_ready, 2 * i + s + 1)
                        chain(dve.reciprocal(rstd[:, s:s + 1], rms[:, s:s + 1]))
                        dve.wait_ge(t_free, 4 * i + 2 * s + 2)
                        dve.scalar_tensor_tensor(hh[s][:, :], xt[s][:, :], rstd[:, s:s + 1], gb[:, :], ALU.mult,
                                                 ALU.mult).then_inc(h_ready, 1)

            @block.tensor
            def _(pe):
                with pe.Fori(0, NT // 2) as i:
                    for s in range(2):
                        pe.wait_ge(h_ready, 2 * i + s + 3)
                        for h in range(2):
                            for k in range(4):
                                last = pe.transpose(pt[s][h][:, k * P:(k + 1) * P],
                                                    hh[s][:, (4 * h + k) * P:(4 * h + k + 1) * P], ident[:, :])
                            last.then_inc(t_ready, 1)

            @block.scalar
            def _(act):
                act.sem_inc(t_free, 4)
                with act.Fori(0, NT // 2) as i:
                    for s in range(2):
                        act.wait_ge(ms_ready, 2 * i + s + 1)
                        act.activation(rms[:, s:s + 1], ms[:, s:s + 1], ACT.Sqrt).then_inc(rms_ready, 1)
                        for h in range(2):
                            act.wait_ge(t_ready, 4 * i + 2 * s + h + 1)
                            act.activation(hT[:, 4 * h:4 * h + 4, ds(i * (2 * P) + s * P, P)],
                                           pt[s][h][:, :].rearrange("p (k n) -> p k n", k=4),
                                           ACT.Copy).then_inc(t_free, 1)


def s5(nc, hT, ident, w_u, prm, y_out):
    a_re, a_im, log_dt, b_re, b_im, c_re, c_im, d_skip = prm
    NP9 = TS + 1
    LEAD = (TS - 1) * SC
    TWO_PI = 2 * np.pi
    C1 = 6.28125
    C2 = float(np.float32(np.round((TWO_PI - C1) * 2 ** 22) / 2 ** 22))
    C3 = float(np.float32(TWO_PI - C1 - C2))
    ROUND = 1.5 * 2.0 ** 23
    HALVINGS = 10
    with ExitStack() as ctx:
        t_ = Tools(nc, ctx, "s5")
        w = t_.sb("w", [P, KD, SW])
        tok = t_.sb("tok", [P, HC, TS, SW])
        yT = t_.sb("yT", [P, SW // P, S])
        lr, li, dt = (t_.sb(n, [P, PAIRS]) for n in ("lr", "li", "dt"))
        br0, bi0, cr, ci, br, bi = (t_.sb(n, [P, PAIRS, SC]) for n in ("br0", "bi0", "cr", "ci", "br", "bi"))
        d8 = t_.sb("d8", [P, SG])
        v = [t_.sb(f"v{n}", [P, PAIRS]) for n in range(12)]
        t16 = [t_.sb(f"t16{n}", [P, PAIRS, SC]) for n in range(2)]
        pr, pi, npi = (t_.sb(n, [P, PAIRS, NP9]) for n in ("pr", "pi", "npi"))
        rr, ri = (t_.sb(n, [P, PAIRS, TS]) for n in ("rr", "ri"))
        lar, lai, nlai = (t_.sb(n, [P, PAIRS, LEVELS]) for n in ("lar", "lai", "nlai"))
        ust = [t_.sb(f"ust{z}", [P, HC, 2, TS, SC]) for z in range(2)]
        bpad = [t_.sb(f"bpad{z}", [P, 2, 2 * LEAD + SC]) for z in range(2)]
        cpad = [t_.sb(f"cpad{z}", [P, 2, LEAD + NP9 * SC]) for z in range(2)]
        inm = [t_.sb(f"inm{z}", [P, 2, TS * SC]) for z in range(2)]
        tmp = [t_.sb(f"tmp{n}", [P, NP9 * SC]) for n in range(4)]
        u8 = [t_.sb(f"u8{z}", [P, 2 * NC]) for z in range(2)]
        inT = [t_.sb(f"inT{z}", [P, 2, P]) for z in range(2)]
        intra = [t_.sb(f"intra{z}", [P, 2, P]) for z in range(2)]
        st = [t_.sb(f"st{z}", [P, 2, NC + 1]) for z in range(2)]
        alt = t_.sb("alt", [P, 2, NC + 1])
        ps_u = [t_.ps(f"u{z}") for z in range(2)]
        ps_8, ps_in, ps_it0, ps_x = (t_.ps(n) for n in ("p8", "pin", "pit", "px"))
        ps_it = (ps_it0, ps_u[0])
        ps_y = [t_.ps(f"y{h}") for h in range(2)]
        (w_in, prm_in, dt_ready, chain_v, maps_ready, pads_ready, u_ready, u_saved, chain_p, staged, t8, tin, kin,
         acts, it_saved, x_ready, x_saved, scanned, y_ready, y_saved, chain_s, yt_ready, yt_saved, y_stored) = t_.sems(
            "w_in prm_in dt_ready chain_v maps_ready pads_ready u_ready u_saved chain_p staged t8 tin kin "
            "acts it_saved x_ready x_saved scanned y_ready y_saved chain_s yt_ready yt_saved y_stored")

        with nc.Block() as block:
            @block.sync
            def _(sp):
                sp.dma_start(w[:, :, :], w_u).then_inc(w_in, 16)
                n = 0
                for dst, src in ((lr, a_re), (li, a_im)):
                    sp.dma_start(dst[:, :], src).then_inc(prm_in, 16)
                    n += 1
                for h in range(2):
                    sp.dma_start(dt[SN * h:SN * (h + 1), :], on_rows(log_dt[h], SN)).then_inc(prm_in, 16)
                    n += 1
                for dst, src in ((br0, b_re), (bi0, b_im), (cr, c_re), (ci, c_im)):
                    sp.dma_start(dst[:, :, :], src).then_inc(prm_in, 16)
                    n += 1
                for s in range(TS):
                    sp.dma_start(d8[SC * s:SC * (s + 1), :], d_skip).then_inc(prm_in, 16)
                    n += 1
                sp.wait_ge(yt_saved, HC * TS)
                sp.dma_start(y_out, yT[:, :, :]).then_inc(y_stored, 16)
                sp.wait_ge(y_stored, 16)
            PRM = 16 * (8 + TS)

            @block.gpsimd
            def _(pool):
                for z in range(2):
                    pool.memset(bpad[z][:, :, :], 0.0)
                    last = pool.memset(cpad[z][:, :, :], 0.0)
                last.then_inc(pads_ready, 1)
                pool.wait_ge(pads_ready, 1)
                pool.wait_ge(maps_ready, 1)
                pool.wait_ge(u_saved, HC * TS)

                def build(p, z, free):
                    if free is not None:
                        pool.wait_ge(y_ready, free)
                    chain = Steps(pool, chain_p, 3 * p)
                    for k in range(HC):
                        pool.tensor_copy(ust[z][:, k, :, :, :],
                                         tok[:, k, :, ds(p * 2 * SC, 2 * SC)].rearrange("p j (h c) -> p h j c", h=2))
                    pool.tensor_copy(bpad[z][:, 0, LEAD:LEAD + SC], br[:, ds(p, 1), :].rearrange("p a c -> p (a c)"))
                    pool.tensor_copy(bpad[z][:, 1, LEAD:LEAD + SC], bi[:, ds(p, 1), :].rearrange("p a c -> p (a c)"))

                    def outer(dst, power, factor, n):
                        return pool.tensor_tensor(
                            dst[:, 0:n * SC].rearrange("p (j c) -> p j c", c=SC),
                            power[:, ds(p, 1), :].rearrange("p a j -> p (a j)").unsqueeze(2).to_broadcast([P, n, SC]),
                            factor[:, ds(p, 1), :].to_broadcast([P, n, SC]), ALU.mult)

                    for (a, b, c, d), dst, off, n, op in (
                            (((rr, br), (ri, bi), (rr, bi), (ri, br)), inm, 0, TS, (ALU.subtract, ALU.add)),
                            (((pr, cr), (npi, ci), (npi, cr), (pr, ci)), cpad, LEAD, NP9, (ALU.add, ALU.subtract))):
                        for t, (power, factor) in zip(tmp[:3], (a, b, c)):
                            outer(t, power, factor, n)
                        chain(outer(tmp[3], *d, n))
                        pool.tensor_tensor(dst[z][:, 0, off:off + n * SC], tmp[0][:, 0:n * SC], tmp[1][:, 0:n * SC], op[0])
                        last = pool.tensor_tensor(dst[z][:, 1, off:off + n * SC], tmp[2][:, 0:n * SC],
                                                  tmp[3][:, 0:n * SC], op[1])
                        if dst is inm:
                            chain(last)
                    last.then_inc(staged, 1)
                    pool.wait_ge(staged, p + 1)

                for p in range(2):
                    build(p, p, None)
                with pool.Fori(1, PAIRS // 2) as i:
                    for z in range(2):
                        build(2 * i + z, z, 2 * i + z - 1)

            @block.tensor
            def _(pe):
                pe.wait_ge(w_in, 16)
                for n in range(HC * TS):
                    k, j = divmod(n, TS)
                    if n >= 2:
                        pe.wait_ge(u_saved, n - 1)
                    for c in range(KD):
                        lhs = hT[:, c, k * P * TS + j:(k * P + P - 1) * TS + j + 1:TS]
                        last = pe.matmul(ps_u[n % 2][:, :], lhs, w[:, c, :], start=(c == 0), stop=(c == KD - 1))
                    last.then_inc(u_ready, 1)

                def inputs(p, z):
                    pe.wait_ge(staged, p + 1)
                    pe.wait_ge(acts, 2 * p + 1)
                    for h in range(2):
                        for k in range(HC):
                            last = pe.transpose(ps_8[:, h * NC + k * P:h * NC + (k + 1) * P],
                                                ust[z][:, k, h, :, :].rearrange("p j c -> p (j c)"), ident[:, :])
                    last.then_inc(t8, 1)
                    for r in range(2):
                        last = pe.transpose(ps_in[:, r * P:(r + 1) * P], inm[z][:, r, :], ident[:, :])
                    last.then_inc(tin, 1)
                    pe.wait_ge(it_saved, 2 * p + 2)
                    for h in range(2):
                        q = slice(SN * h, SN * (h + 1))
                        for s in range(TS):
                            for r in range(2):
                                last = pe.matmul(ps_it[h][:, 0:P], bpad[z][q, r, LEAD - SC * s:LEAD - SC * s + P],
                                                 cpad[z][q, r, LEAD - SC * s:LEAD - SC * s + P],
                                                 start=(s == 0 and r == 0), stop=(s == TS - 1 and r == 1))
                    last.then_inc(kin, 1)
                    pe.wait_ge(acts, 2 * p + 3)
                    pe.wait_ge(x_saved, p + 1)
                    for r in range(2):
                        for h in range(2):
                            last = pe.matmul(ps_x[SN * h:SN * (h + 1), r * NC:(r + 1) * NC],
                                             inT[z][:, r, SN * h:SN * (h + 1)], u8[z][:, h * NC:(h + 1) * NC],
                                             start=True, stop=True)
                    last.then_inc(x_ready, 1)

                def outputs(p, z):
                    pe.wait_ge(scanned, p + 1)
                    pe.wait_ge(y_saved, 4 * p + 4)
                    for h in range(2):
                        q = slice(SN * h, SN * (h + 1))
                        for k in range(HC):
                            out = ps_y[h][:, k * P:(k + 1) * P]
                            pe.matmul(out, u8[z][:, h * NC + k * P:h * NC + (k + 1) * P], intra[z][:, h, :],
                                      start=True, stop=False)
                            for r in range(2):
                                last = pe.matmul(out, st[z][q, r, k * P:(k + 1) * P], cpad[z][q, r, LEAD + SC:],
                                                 start=False, stop=(r == 1))
                    last.then_inc(y_ready, 1)

                inputs(0, 0)
                with pe.Fori(0, PAIRS // 2 - 1) as i:
                    inputs(2 * i + 1, 1)
                    outputs(2 * i, 0)
                    inputs(2 * i + 2, 0)
                    outputs(2 * i + 1, 1)
                inputs(PAIRS - 1, 1)
                outputs(PAIRS - 2, 0)
                outputs(PAIRS - 1, 1)
                pe.wait_ge(y_saved, 4 * PAIRS + 4)
                for n in range(HC * TS):
                    k, j = divmod(n, TS)
                    if n >= 2:
                        pe.wait_ge(yt_saved, n - 1)
                    for f in range(SW // P):
                        last = pe.transpose(ps_u[n % 2][:, f * P:(f + 1) * P], tok[:, k, j, f * P:(f + 1) * P], ident[:, :])
                    last.then_inc(yt_ready, 1)

            @block.scalar
            def _(act):
                act.sem_inc(acts, 1)
                act.sem_inc(y_saved, 4)
                act.wait_ge(prm_in, PRM)
                act.activation(dt[:, :], dt[:, :], ACT.Exp).then_inc(dt_ready, 1)
                for n in range(HC * TS):
                    k, j = divmod(n, TS)
                    act.wait_ge(u_ready, n + 1)
                    act.activation(tok[:, k, j, :], ps_u[n % 2][:, :], ACT.Copy).then_inc(u_saved, 1)

                def save_inputs(p, z):
                    act.wait_ge(t8, p + 1)
                    act.activation(u8[z][:, :], ps_8[:, :], ACT.Copy).then_inc(acts, 1)
                    act.wait_ge(tin, p + 1)
                    act.activation(inT[z][:, :, :], ps_in[:, 0:2 * P].rearrange("p (r n) -> p r n", r=2),
                                   ACT.Copy).then_inc(acts, 1)

                def save_outputs(p, z):
                    act.wait_ge(y_ready, p + 1)
                    for h in range(2):
                        for k in range(HC):
                            act.activation(tok[:, k, :, ds(p * 2 * SC + h * SC, SC)],
                                           ps_y[h][:, k * P:(k + 1) * P].rearrange(
                                               "p (j c) -> p j c", c=SC), ACT.Gelu_apprx_tanh).then_inc(y_saved, 1)

                save_inputs(0, 0)
                with act.Fori(0, PAIRS // 2 - 1) as i:
                    save_inputs(2 * i + 1, 1)
                    save_outputs(2 * i, 0)
                    save_inputs(2 * i + 2, 0)
                    save_outputs(2 * i + 1, 1)
                save_inputs(PAIRS - 1, 1)
                save_outputs(PAIRS - 2, 0)
                save_outputs(PAIRS - 1, 1)

            @block.vector
            def _(dve):
                for z in range(2):
                    dve.memset(st[z][:, :, 0:1], 0.0)
                dve.sem_inc(it_saved, 2)
                dve.sem_inc(x_saved, 1)
                go = Steps(dve, chain_v)
                tt, tsc, stt = dve.tensor_tensor, dve.tensor_scalar, dve.scalar_tensor_tensor

                def cmul(re, im, ar, ai, b_r, b_i, t):
                    tt(t[0], ar, b_r, ALU.mult)
                    tt(t[1], ai, b_i, ALU.mult)
                    tt(t[2], ar, b_i, ALU.mult)
                    go(tt(t[3], ai, b_r, ALU.mult))
                    tt(re, t[0], t[1], ALU.subtract)
                    go(tt(im, t[2], t[3], ALU.add))

                vv = [x[:, :] for x in v]
                t4 = vv[8:12]
                dve.wait_ge(dt_ready, 1)
                tt(vv[0], lr[:, :], dt[:, :], ALU.mult)
                go(tt(vv[1], li[:, :], dt[:, :], ALU.mult))
                go(tsc(vv[2], vv[1], 1.0 / TWO_PI, None, ALU.mult))
                go(tsc(vv[2], vv[2], ROUND, None, ALU.add))
                go(tsc(vv[2], vv[2], -ROUND, None, ALU.add))
                for c in (C1, C2, C3):
                    go(stt(vv[1], vv[2], -c, vv[1], ALU.mult, ALU.add))
                go(tsc(vv[0], vv[0], -110.0, 100.0, ALU.max, ALU.min))
                tsc(vv[0], vv[0], 0.5 ** HALVINGS, None, ALU.mult)
                go(tsc(vv[1], vv[1], 0.5 ** HALVINGS, None, ALU.mult))
                tsc(vv[2], vv[0], 1 / 6, 1.0, ALU.mult, ALU.add)
                go(tsc(vv[3], vv[1], 1 / 6, None, ALU.mult))
                for k in (5, 4, 3, 2):
                    cmul(vv[4], vv[5], vv[0], vv[1], vv[2], vv[3], t4)
                    tsc(vv[2], vv[4], 1 / k, 1.0, ALU.mult, ALU.add)
                    go(tsc(vv[3], vv[5], 1 / k, None, ALU.mult))
                cmul(vv[4], vv[5], vv[0], vv[1], vv[2], vv[3], t4)
                for _ in range(HALVINGS):
                    stt(t4[0], vv[4], 2.0, vv[4], ALU.add, ALU.mult)
                    tt(t4[1], vv[5], vv[5], ALU.mult)
                    go(stt(t4[2], vv[4], 1.0, vv[5], ALU.add, ALU.mult))
                    tt(vv[4], t4[0], t4[1], ALU.subtract)
                    go(tsc(vv[5], t4[2], 2.0, None, ALU.mult))
                er, ei = vv[4], vv[5]
                tsc(vv[6], li[:, :], -1.0, None, ALU.mult)
                tt(t4[0], lr[:, :], lr[:, :], ALU.mult)
                go(tt(t4[1], li[:, :], li[:, :], ALU.mult))
                go(tt(vv[7], t4[0], t4[1], ALU.add))
                go(dve.reciprocal(vv[7], vv[7]))
                cmul(vv[0], vv[1], er, ei, lr[:, :], vv[6], t4)
                tt(vv[2], vv[0], vv[7], ALU.mult)
                go(tt(vv[3], vv[1], vv[7], ALU.mult))
                fr, fi = (x.unsqueeze(2).to_broadcast([P, PAIRS, SC]) for x in (vv[2], vv[3]))
                for dst, (f0, b0), (f1, b1), op in ((br, (fr, br0), (fi, bi0), ALU.subtract),
                                                    (bi, (fr, bi0), (fi, br0), ALU.add)):
                    tt(t16[0][:, :, :], b0[:, :, :], f0, ALU.mult)
                    go(tt(t16[1][:, :, :], b1[:, :, :], f1, ALU.mult))
                    go(tt(dst[:, :, :], t16[0][:, :, :], t16[1][:, :, :], op))
                dve.memset(pr[:, :, 0:1], 1.0)
                dve.memset(pi[:, :, 0:1], 0.0)
                tsc(pr[:, :, 1], er, 1.0, None, ALU.add)
                go(dve.tensor_copy(pi[:, :, 1], ei))
                for j in range(2, NP9):
                    cmul(pr[:, :, j], pi[:, :, j], pr[:, :, j - 1], pi[:, :, j - 1], pr[:, :, 1], pi[:, :, 1], t4)
                tsc(npi[:, :, :], pi[:, :, :], -1.0, None, ALU.mult)
                for j in range(TS):
                    dve.tensor_copy(rr[:, :, j], pr[:, :, TS - 1 - j])
                    dve.tensor_copy(ri[:, :, j], pi[:, :, TS - 1 - j])
                dve.tensor_copy(lar[:, :, 0], pr[:, :, TS])
                go(dve.tensor_copy(lai[:, :, 0], pi[:, :, TS]))
                for l in range(1, LEVELS):
                    a, b = lar[:, :, l - 1], lai[:, :, l - 1]
                    cmul(lar[:, :, l], lai[:, :, l], a, b, a, b, t4)
                go(tsc(nlai[:, :, :], lai[:, :, :], -1.0, None, ALU.mult))
                dve.sem_inc(maps_ready, 1)

                def scan(p, z):
                    dve.wait_ge(kin, p + 1)
                    for h in range(2):
                        stt(intra[z][:, h, :], ident[:, :], d8[:, ds(2 * p + h, 1)], ps_it[h][:, 0:P],
                            ALU.mult, ALU.add).then_inc(it_saved, 1)
                    dve.wait_ge(x_ready, p + 1)
                    dve.tensor_copy(st[z][:, :, 1:], ps_x[:, :].rearrange("p (r n) -> p r n", r=2)).then_inc(x_saved, 1)
                    dve.wait_ge(x_saved, p + 2)
                    chain = Steps(dve, chain_s, (2 * LEVELS - 1) * p)
                    src, dst = st[z], alt
                    for l in range(LEVELS):
                        s = 1 << l
                        scalar = [x[:, ds(p, 1), l:l + 1].rearrange("p a b -> p (a b)") for x in (lar, nlai, lai)]
                        dve.tensor_copy(dst[:, :, 1:1 + s], src[:, :, 1:1 + s])
                        chain(stt(dst[:, :, 1 + s:], src[:, :, 1:NC + 1 - s], scalar[0], src[:, :, 1 + s:],
                                  ALU.mult, ALU.add))
                        stt(dst[:, 0, 1 + s:], src[:, 1, 1:NC + 1 - s], scalar[1], dst[:, 0, 1 + s:], ALU.mult, ALU.add)
                        last = stt(dst[:, 1, 1 + s:], src[:, 0, 1:NC + 1 - s], scalar[2], dst[:, 1, 1 + s:],
                                   ALU.mult, ALU.add)
                        if l < LEVELS - 1:
                            chain(last)
                        src, dst = dst, src
                    last.then_inc(scanned, 1)
                    dve.wait_ge(scanned, p + 1)

                with dve.Fori(0, PAIRS // 2) as i:
                    for z in range(2):
                        scan(2 * i + z, z)
                for n in range(HC * TS):
                    k, j = divmod(n, TS)
                    dve.wait_ge(yt_ready, n + 1)
                    first = k * P * TS + j
                    dve.tensor_copy(yT[:, :, first:first + (P - 1) * TS + 1:TS],
                                    ps_u[n % 2][:, :].rearrange("p (f n) -> p f n", f=SW // P)).then_inc(yt_saved, 1)


def bucket_onehot():
    hot = np.zeros((BUCKETS + 1, len(GROUPS), STEPS_W), np.float32)
    exact = BUCKETS // 2
    for g, (window, dilation) in enumerate(GROUPS):
        steps = 2 * P - 1 - np.arange(STEPS_W)
        inside = (steps >= 0) & (steps <= window // dilation)
        dist = np.clip(steps, 0, None) * dilation
        far = exact + (np.log(np.maximum(dist, 1).astype(np.float32) / exact) / np.log(MAX_DIST / exact)
                       * (BUCKETS - exact)).astype(np.int32)
        bucket = np.where(dist < exact, dist, np.minimum(far, BUCKETS - 1))
        hot[bucket[inside], g, np.nonzero(inside)[0]] = 1.0
        hot[BUCKETS, g] = np.where(inside, 0.0, MASKED)
    return hot


def bias_tables(nc, rel_bias, onehot, rows_d, bias, jflip):
    NG, NH = len(GROUPS), len(GROUPS) * HG
    with ExitStack() as ctx:
        t_ = Tools(nc, ctx, "bia")
        rel = t_.sb("rel", [BUCKETS + 1, NH])
        hot = t_.sb("hot", [BUCKETS + 1, NG, STEPS_W])
        rows = t_.sb("rows", [HG, NG, STEPS_W])
        hank = t_.sb("hank", [P, NH, 2 * P])
        pr = [t_.ps(f"pr{g}") for g in range(NG)]
        pf = [t_.ps(f"pf{n}") for n in range(4)]
        loaded, negated, rows_ready, rows_saved, rows_out, hank_in, flipped, saved = t_.sems(
            "loaded negated rows_ready rows_saved rows_out hank_in flipped saved")
        with nc.Block() as block:
            @block.sync
            def _(sp):
                sp.dma_start(rel[0:BUCKETS, :], rel_bias).then_inc(loaded, 16)
                sp.dma_start(hot[:, :, :], onehot).then_inc(loaded, 16)
                sp.wait_ge(rows_saved, NG)
                sp.dma_start(rows_d.rearrange("(g h) s -> h g s", g=NG), rows[:, :, :]).then_inc(rows_out, 16)
                sp.wait_ge(rows_out, 16)
                shifted = bass.AP(rows_d.tensor, rows_d.offset, [[1, P], [STEPS_W, NH], [1, 2 * P]])
                sp.dma_start(hank[:, :, :], shifted).then_inc(hank_in, 16)

            @block.vector
            def _(dve):
                dve.memset(rel[BUCKETS:BUCKETS + 1, :], 1.0)
                dve.wait_ge(loaded, 32)
                dve.tensor_scalar(rel[0:BUCKETS, :], rel[0:BUCKETS, :], -1.0, None, ALU.mult).then_inc(negated, 1)
                for g in range(NG):
                    dve.wait_ge(rows_ready, g + 1)
                    dve.tensor_copy(rows[:, g, :], pr[g][0:HG, 0:STEPS_W]).then_inc(rows_saved, 1)
                for n in range(NH // 2):
                    dve.wait_ge(flipped, n + 1)
                    dve.tensor_copy(bias[:, 2 * n:2 * n + 2, :],
                                    pf[n % 4][:, :].rearrange("p (h k) -> p h k", h=2)).then_inc(saved, 1)

            @block.tensor
            def _(pe):
                pe.wait_ge(negated, 1)
                for g in range(NG):
                    pe.matmul(pr[g][0:HG, 0:STEPS_W], rel[:, g * HG:(g + 1) * HG], hot[:, g, :], start=True,
                              stop=True).then_inc(rows_ready, 1)
                pe.wait_ge(hank_in, 16)
                for n in range(NH // 2):
                    if n >= 4:
                        pe.wait_ge(saved, n - 3)
                    pe.matmul(pf[n % 4][:, :], jflip[:, :],
                              hank[:, 2 * n:2 * n + 2, :].rearrange("p h k -> p (h k)"), start=True,
                              stop=True).then_inc(flipped, 1)


def attention(nc, hT, w_in, q_gain, k_gain, bias, ident, att_d):
    UN = NBLK * HG
    with ExitStack() as ctx:
        t_ = Tools(nc, ctx, "att")
        hc = t_.sb("hc", [P, KD, CH])
        w = [t_.sb(f"w{n}", [P, KD, AW]) for n in "qkv"]
        qT = t_.sb("qT", [P, NFT, CH])
        kT = t_.sb("kT", [P, NFT, P + CH])
        v = t_.sb("v", [P, 1 + NBLK, AW])
        same = t_.sb("same", [P, P])
        gains = [t_.sb(f"gain{n}", [P, len(GROUPS)]) for n in "qk"]
        eps = t_.sb("eps", [P, 1])
        tick = t_.sem("tick")
        sq = [t_.sb(f"sq{z}", [P, CH]) for z in range(2)]
        rt = [t_.sb(f"rt{z}", [P, CH]) for z in range(2)]
        sc = [t_.sb(f"sc{z}", [P, 2 * P]) for z in range(3)]
        pp = [t_.sb(f"pp{z}", [P, 2 * P]) for z in range(3)]
        ppT = [t_.sb(f"ppT{z}", [P, 2 * P]) for z in range(2)]
        ao = [t_.sb(f"ao{z}", [P, HG, RW]) for z in range(2)]
        bank = [t_.ps(f"b{n}") for n in range(8)]
        gm, ssq, sb, tb, ob = bank[0:2], bank[2], bank[0:4], bank[4:6], bank[6:8]
        w_sem = [t_.sem(f"w_in_{n}") for n in "qkv"]
        ao_out = [t_.sem(f"ao_out{z}") for z in range(2)]
        (gain_in, const, gain_ready, hc_ready, qk_mm, v_mm, qk_done, v_done, sq_ready, ssq_ready, root_ready, rec,
         s_ready, s_read, p_ready, t_ready, pt_ready, pv_done, o_saved) = t_.sems(
            "gain_in const gain_ready hc_ready qk_mm v_mm qk_done v_done sq_ready ssq_ready root_ready rec "
            "s_ready s_read p_ready t_ready pt_ready pv_done o_saved")

        def chunks(eng, g, body):
            first = g == 0
            if first:
                body(g, 0, 0, True)
            with eng.Fori(1 if first else 0, NCH) as c:
                body(g, c, c + NCH * g, False)

        def alone(g, b, opening):
            return g == 2 or (b == 0 and (g == 1 or opening))

        def in_group_order(ap, g, c):
            d = GROUPS[g][1]
            if d == 1:
                return ap[:, :, ds(c * CH, CH)].rearrange("p k (r a) -> p k r a", r=1)
            n = d // NCH
            return ap.rearrange("p k (a r) -> p k r a", r=d)[:, :, ds(c * n, n), :]

        def block_rows(g, c, b):
            rows = att_d[g]
            if g == 0:
                return rows[ds(c * CH + b * P, P), :]
            d = GROUPS[g][1]
            r, a = (c, b) if g == 1 else (c * NBLK + b, 0)
            return rows.rearrange("(a r) w -> r a w", r=d)[ds(r, 1), a * P:(a + 1) * P, :].rearrange("o a w -> (o a) w")

        with nc.Block() as block:
            @block.sync
            def _(sp):
                for h in range(2):
                    for dst, src in zip(gains, (q_gain, k_gain)):
                        sp.dma_start(dst[DH * h:DH * (h + 1), :], src).then_inc(gain_in, 16)
                def load(g, i):
                    col = (i * len(GROUPS) + g) * AW
                    sp.dma_start(w[i][:, :, :], w_in[:, col:col + AW].rearrange("(k p) n -> p k n", p=P)).then_inc(
                        w_sem[i], 16)

                def chunk(g, c, n, opening):
                    for b in range(NBLK):
                        sp.wait_ge(o_saved, NBLK * n + b + 1)
                        sp.dma_start(block_rows(g, c, b), ao[b % 2][:, :, :].rearrange("p h w -> p (h w)")).then_inc(
                            ao_out[b % 2], 16)

                for i in range(3):
                    load(0, i)
                chunk(0, 0, 0, True)
                for g in range(len(GROUPS)):
                    with sp.Fori(1 if g == 0 else 0, NCH - 1) as c:
                        chunk(g, c, c + NCH * g, False)
                    if g + 1 < len(GROUPS):
                        for i in range(2):
                            sp.wait_ge(qk_mm, 2 * NFT * (NCH * (g + 1) - 1) + NFT * (i + 1))
                            load(g + 1, i)
                        sp.wait_ge(v_mm, NBLK * NCH * (g + 1))
                        load(g + 1, 2)
                    chunk(g, NCH - 1, NCH * g + NCH - 1, False)
                for z in range(2):
                    sp.wait_ge(ao_out[z], 16 * (NBLK // 2) * NCH * len(GROUPS))

            @block.gpsimd
            def _(pool):
                pool.memset(same[:, :], 0.0).then_inc(const, 1)
                pool.memset(eps[:, :], EPS).then_inc(const, 1)
                pool.wait_ge(const, 2)
                for h in range(2):
                    pool.memset(same[DH * h:DH * (h + 1), DH * h:DH * (h + 1)], 1.0).then_inc(const, 1)

                pool.wait_ge(const, 4)

                def stage(g, c, n, opening):
                    if not opening:
                        pool.wait_ge(v_mm, NBLK * n)
                    src = in_group_order(hT[:, :, :], g, c)
                    pool.tensor_copy(hc[:, :, :].rearrange("p k (r a) -> p k r a", r=src.shape[2]),
                                     src).then_inc(hc_ready, 1)
                for g in range(len(GROUPS)):
                    chunks(pool, g, stage)

            @block.tensor
            def _(pe):
                pe.wait_ge(const, 4)

                def chunk(g, c, n, opening):
                    pe.wait_ge(hc_ready, n + 1)
                    if not opening:
                        pe.wait_ge(s_read, UN * n)

                    def square_sums(t):
                        pe.wait_ge(sq_ready, 2 * NFT * n + t + 1)
                        if t or not opening:
                            pe.wait_ge(root_ready, 2 * NFT * n + t)
                        pe.matmul(ssq[:, :], same[:, :], sq[t % 2][:, :], start=True, stop=True).then_inc(ssq_ready, 1)

                    for t in range(2 * NFT):
                        i, f = divmod(t, NFT)
                        if f == 0:
                            pe.wait_ge(w_sem[i], 16 * g + 16)
                        if t >= 2:
                            pe.wait_ge(qk_done, 2 * NFT * n + t - 1)
                        for k in range(KD):
                            last = pe.matmul(gm[t % 2][:, :], w[i][:, k, f * P:(f + 1) * P], hc[:, k, :],
                                             start=(k == 0), stop=(k == KD - 1))
                        last.then_inc(qk_mm, 1)
                        if t:
                            square_sums(t - 1)
                    pe.wait_ge(w_sem[2], 16 * g + 16)
                    for b in range(NBLK):
                        if b < 2:
                            pe.wait_ge(qk_done, 2 * NFT * (n + 1) - 1 + b)
                        else:
                            pe.wait_ge(v_done, NBLK * n + b - 1)
                        for k in range(KD):
                            last = pe.matmul(gm[b % 2][:, :], hc[:, k, b * P:(b + 1) * P], w[2][:, k, :],
                                             start=(k == 0), stop=(k == KD - 1))
                        last.then_inc(v_mm, 1)
                        if b == 0:
                            square_sums(2 * NFT - 1)
                    pe.wait_ge(v_done, NBLK * n + NBLK)

                    for step in range(UN + 3):
                        if step < UN:
                            b, h = divmod(step, HG)
                            off, rows = (P if alone(g, b, opening) else 0), slice(DH * (h % 2), DH * (h % 2) + DH)
                            if step >= 4:
                                pe.wait_ge(s_read, UN * n + step - 3)
                            pe.matmul(sb[step % 4][:, off:2 * P], qT[rows, h // 2, b * P:(b + 1) * P],
                                      kT[rows, h // 2, b * P + off:(b + 2) * P], start=True, stop=True).then_inc(s_ready, 1)
                        u = step - 2
                        if 0 <= u < UN:
                            b, h = divmod(u, HG)
                            pe.wait_ge(p_ready, UN * n + u + 1)
                            if u >= 2 or not opening:
                                pe.wait_ge(pt_ready, UN * n + u - 1)
                            for k in range(1 if alone(g, b, opening) else 0, 2):
                                last = pe.transpose(tb[u % 2][:, k * P:(k + 1) * P], pp[u % 3][:, k * P:(k + 1) * P],
                                                    ident[:, :])
                            last.then_inc(t_ready, 1)
                        u = step - 3
                        if 0 <= u < UN:
                            b, h = divmod(u, HG)
                            pe.wait_ge(pt_ready, UN * n + u + 1)
                            if h == 0 and (b >= 2 or not opening):
                                pe.wait_ge(o_saved, NBLK * n + b - 1)
                            k0 = 1 if alone(g, b, opening) else 0
                            for k in range(k0, 2):
                                last = pe.matmul(ob[b % 2][:, h * DH:(h + 1) * DH], ppT[u % 2][:, k * P:(k + 1) * P],
                                                 v[:, b + k, h * DH:(h + 1) * DH], start=(k == k0), stop=(k == 1))
                            last.then_inc(pv_done, 1)
                for g in range(len(GROUPS)):
                    chunks(pe, g, chunk)

            @block.scalar
            def _(act):
                act.wait_ge(const, 4)

                def chunk(g, c, n, opening):
                    def root(t):
                        act.wait_ge(ssq_ready, 2 * NFT * n + t + 1)
                        if t >= 2 or not opening:
                            act.wait_ge(qk_done, 2 * NFT * n + t - 1)
                        act.activation(rt[t % 2][:, :], ssq[:, :], ACT.Sqrt, bias=eps[:, :],
                                       scale=1.0 / DH).then_inc(root_ready, 1)

                    for t in range(2 * NFT):
                        act.wait_ge(qk_mm, 2 * NFT * n + t + 1)
                        act.activation(sq[t % 2][:, :], gm[t % 2][:, :], ACT.Square).then_inc(sq_ready, 1)
                        if t:
                            root(t - 1)
                    root(2 * NFT - 1)
                    if g == 0 and not opening:
                        act.wait_ge(pv_done, UN * n)
                        act.activation(v[:, 0, :], v[:, NBLK, :], ACT.Copy).then_inc(gain_ready, 1)
                        act.wait_ge(gain_ready, n + 1)
                    for b in range(NBLK):
                        act.wait_ge(v_mm, NBLK * n + b + 1)
                        if b == 0 and not opening:
                            act.wait_ge(pv_done, UN * n)
                        act.activation(v[:, 1 + b, :], gm[b % 2][:, :], ACT.Copy).then_inc(v_done, 1)

                    def save(b):
                        act.wait_ge(pv_done, UN * n + HG * (b + 1))
                        act.activation(ao[b % 2][:, :, 0:DH], ob[b % 2][:, :].rearrange("p (h d) -> p h d", h=HG),
                                       ACT.Copy).then_inc(o_saved, 1)

                    for u in range(UN):
                        b, h = divmod(u, HG)
                        off = P if alone(g, b, opening) else 0
                        act.wait_ge(s_read, UN * n + u + 1)
                        if u >= 3 or not opening:
                            act.wait_ge(t_ready, UN * n + u - 2)
                        act.activation(pp[u % 3][:, off:2 * P], sc[u % 3][:, off:2 * P], ACT.Exp,
                                       bias=ao[b % 2][:, h, DH:DH + 1], scale=-1.0,
                                       accum_out=ao[b % 2][:, h, DH + 1:DH + 2]).then_inc(p_ready, 1)
                        if h == 3 and b:
                            save(b - 1)
                    save(NBLK - 1)
                for g in range(len(GROUPS)):
                    chunks(act, g, chunk)

            @block.vector
            def _(dve):
                dve.wait_ge(gain_in, 64)
                dve.tensor_scalar(gains[0][:, :], gains[0][:, :], -(DH ** -0.5), None, ALU.mult).then_inc(gain_ready, 1)
                dve.wait_ge(gain_ready, 1)

                def chunk(g, c, n, opening):
                    if not opening:
                        dve.wait_ge(s_ready, UN * n)
                    if g == 0 and not opening:
                        dve.tensor_copy(kT[:, :, 0:P], kT[:, :, CH:CH + P]).then_inc(rec, 1)
                        dve.wait_ge(rec, (2 * NFT + 1) * n)
                    kept = n if g == 0 else NCH - 1
                    for t in range(2 * NFT):
                        i, f = divmod(t, NFT)
                        dve.wait_ge(root_ready, 2 * NFT * n + t + 1)
                        dve.reciprocal(rt[t % 2][:, :], rt[t % 2][:, :]).then_inc(rec, 1)
                        dve.wait_ge(rec, 2 * NFT * n + kept + t + 1)
                        dst = qT[:, f, :] if i == 0 else kT[:, f, P:P + CH]
                        dve.scalar_tensor_tensor(dst, gm[t % 2][:, :], gains[i][:, g:g + 1], rt[t % 2][:, :], ALU.mult,
                                                 ALU.mult).then_inc(qk_done, 1)
                    for step in range(UN + 2):
                        u = step
                        if u < UN:
                            b, h = divmod(u, HG)
                            off = P if alone(g, b, opening) else 0
                            dve.wait_ge(s_ready, UN * n + u + 1)
                            if u >= 3 or not opening:
                                dve.wait_ge(p_ready, UN * n + u - 2)
                            if h == 0 and (b >= 2 or not opening):
                                dve.wait_ge(ao_out[b % 2], 32 * n + 16 * (b // 2))
                            dve.sem_inc(tick, 1)
                            dve.tensor_tensor_reduce(sc[u % 3][:, off:2 * P], sb[u % 4][:, off:2 * P],
                                                     bias[:, HG * g + h, off:2 * P], 1.0, MASKED, ALU.add, ALU.min,
                                                     ao[b % 2][:, h, DH:DH + 1]).then_inc(s_read, 1)
                        u = step - 2
                        if 0 <= u < UN:
                            b = u // HG
                            off = P if alone(g, b, opening) else 0
                            dve.wait_ge(t_ready, UN * n + u + 1)
                            if u >= 2 or not opening:
                                dve.wait_ge(pv_done, UN * n + u - 1)
                            dve.tensor_copy(ppT[u % 2][:, off:2 * P], tb[u % 2][:, off:2 * P]).then_inc(pt_ready, 1)
                for g in range(len(GROUPS)):
                    chunks(dve, g, chunk)



def combine(nc, att_d, ident, attT_d):
    with ExitStack() as ctx:
        t_ = Tools(nc, ctx, "cmb")
        NG = len(GROUPS)
        a = [[t_.sb(f"a{z}{g}", [P, HG, RW]) for g in range(NG)] for z in range(2)]
        low, den, rden = (t_.sb(n, [P, HG]) for n in ("low", "den", "rden"))
        dif, wgt, part = (t_.sb(n, [P, NG, HG]) for n in ("dif", "wgt", "part"))
        mix = [t_.sb(f"mix{z}", [P, AW]) for z in range(2)]
        m1, m2 = (t_.sb(n, [P, AW]) for n in ("m1", "m2"))
        aT = t_.sb("aT", [P, NFT, S])
        pt = [t_.ps(f"pt{z}") for z in range(2)]
        a_in = [t_.sem(f"a_in{z}") for z in range(2)]
        step, added, dif_ready, w_ready, mixed, turned, saved, stored = t_.sems(
            "step added dif_ready w_ready mixed turned saved stored")
        with nc.Block() as block:
            @block.sync
            def _(sp):
                with sp.Fori(0, NT // 2) as i:
                    for z in range(2):
                        sp.wait_ge(mixed, 2 * i + z + 1)
                        for g in range(NG):
                            sp.dma_start(a[z][g][:, :, :].rearrange("p h w -> p (h w)"),
                                         att_d[g, ds(i * (2 * P) + z * P, P), :]).then_inc(a_in[z], 16)
                sp.wait_ge(saved, NT + 2)
                sp.dma_start(attT_d, aT[:, :, :]).then_inc(stored, 16)
                sp.wait_ge(stored, 16)

            @block.vector
            def _(dve):
                dve.sem_inc(mixed, 2)
                tt = dve.tensor_tensor
                PER = 8
                with dve.Fori(0, NT // 2) as i:
                    chain = Steps(dve, step, 2 * PER * i)
                    for z in range(2):
                        dve.wait_ge(a_in[z], 16 * NG * i + 16 * NG)
                        m = [x[:, :, DH] for x in a[z]]
                        chain(tt(low[:, :], m[0], m[1], ALU.min))
                        chain(tt(low[:, :], low[:, :], m[2], ALU.min))
                        for g in range(NG):
                            last = tt(dif[:, g, :], low[:, :], m[g], ALU.subtract)
                        last.then_inc(dif_ready, 1)
                        dve.wait_ge(w_ready, 2 * i + z + 1)
                        for g in range(NG):
                            last = tt(part[:, g, :], wgt[:, g, :], a[z][g][:, :, DH + 1], ALU.mult)
                        chain(last)
                        chain(tt(den[:, :], part[:, 0, :], part[:, 1, :], ALU.add))
                        chain(tt(den[:, :], den[:, :], part[:, 2, :], ALU.add))
                        chain(dve.reciprocal(rden[:, :], den[:, :]))
                        chain(tt(part[:, :, :], wgt[:, :, :], rden[:, :].unsqueeze(1).to_broadcast([P, NG, HG]), ALU.mult))
                        out = mix[z][:, :].rearrange("p (h d) -> p h d", h=HG)
                        view = [x[:, :].rearrange("p (h d) -> p h d", h=HG) for x in (m1, m2)]

                        def weighted(dst, g):
                            return tt(dst, a[z][g][:, :, 0:DH], part[:, g, :].unsqueeze(2).to_broadcast([P, HG, DH]),
                                      ALU.mult)
                        weighted(view[0], 0)
                        weighted(view[1], 1)
                        dve.wait_ge(turned, 2 * i + z + 1)
                        chain(weighted(out, 2))
                        tt(m1[:, :], m1[:, :], m2[:, :], ALU.add).then_inc(added, 1)
                        dve.wait_ge(added, 2 * i + z + 1)
                        tt(mix[z][:, :], mix[z][:, :], m1[:, :], ALU.add).then_inc(mixed, 1)
                        dve.wait_ge(mixed, 2 * i + z + 3)
                    assert chain.n == 2 * PER

            @block.scalar
            def _(act):
                act.sem_inc(saved, 2)
                with act.Fori(0, NT // 2) as i:
                    for z in range(2):
                        act.wait_ge(dif_ready, 2 * i + z + 1)
                        act.activation(wgt[:, :, :], dif[:, :, :], ACT.Exp).then_inc(w_ready, 1)
                        act.wait_ge(turned, 2 * i + z + 3)
                        act.activation(aT[:, :, ds(i * (2 * P) + z * P, P)],
                                       pt[z][:, :].rearrange("p (f n) -> p f n", f=NFT), ACT.Copy).then_inc(saved, 1)

            @block.tensor
            def _(pe):
                pe.sem_inc(turned, 2)
                with pe.Fori(0, NT // 2) as i:
                    for z in range(2):
                        pe.wait_ge(mixed, 2 * i + z + 3)
                        pe.wait_ge(saved, 2 * i + z + 1)
                        for f in range(NFT):
                            last = pe.transpose(pt[z][:, f * P:(f + 1) * P], mix[z][:, f * P:(f + 1) * P], ident[:, :])
                        last.then_inc(turned, 1)



def mix(nc, hT, yT_d, attT_d, w_glu, b_glu, w_tiles, mixed_d):
    KA = AW // P
    KW = 2 * KD + 2 * KA
    NO = D // P
    with ExitStack() as ctx:
        t_ = Tools(nc, ctx, "mix")
        glu = t_.sb("glu", [P, KA, SW])
        bg = t_.sb("bg", [P, KA])
        w = [t_.sb(f"w{z}", [P, KW, P]) for z in range(2)]
        at, y, sg, y2 = (t_.sb(n, [P, KA, CH]) for n in ("at", "y", "sg", "y2"))
        ga, gb, ta, tb = ([t_.sb(f"{n}{z}", [P, CH]) for z in range(2)] for n in ("ga", "gb", "ta", "tb"))
        mx = t_.sb("mx", [P, NO, CH])
        bank = [t_.ps(f"b{n}") for n in range(8)]
        pg = bank[4:8]
        w_sem = [t_.sem(f"w_in{z}") for z in range(2)]
        (glu_in, at_in, y_in, glu_mm, sig, y2_ready, mm, gates, m_a, m_b, mx_ready, mx_out) = t_.sems(
            "glu_in at_in y_in glu_mm sig y2_ready mm gates m_a m_b mx_ready mx_out")
        with nc.Block() as block:
            @block.sync
            def _(sp):
                sp.dma_start(glu[:, :, :], w_glu).then_inc(glu_in, 16)
                sp.dma_start(bg[:, :], b_glu).then_inc(glu_in, 16)
                with sp.Fori(0, NCH) as c:
                    sp.wait_ge(y2_ready, c * KA + 1)
                    sp.dma_start(y[:, :, :], yT_d[:, :, ds(c * CH, CH)]).then_inc(y_in, 16)
                    for o in range(NO):
                        sp.wait_ge(mm, c * (4 * NO) + 4 * o + 4)
                        sp.dma_start(w[o % 2][:, :, :], w_tiles[o]).then_inc(w_sem[o % 2], 16)
                        if o == 0:
                            sp.wait_ge(mm, c * (4 * NO) + 8)
                            sp.dma_start(at[:, :, :], attT_d[:, :, ds(c * CH, CH)]).then_inc(at_in, 16)
                sp.wait_ge(mx_out, 16 * NCH)

            @block.tensor
            def _(pe):
                pe.sem_inc(mm, 8)
                pe.wait_ge(glu_in, 32)
                with pe.Fori(0, NCH) as c:
                    pe.wait_ge(y_in, 16 * c + 16)
                    for f in range(KA):
                        pe.wait_ge(y2_ready, c * KA + 1)
                        for k in range(KA):
                            last = pe.matmul(pg[f][:, :], glu[:, k, f * P:(f + 1) * P], y[:, k, :], start=(k == 0),
                                             stop=(k == KA - 1))
                        last.then_inc(glu_mm, 1)
                    pe.wait_ge(at_in, 16 * c + 16)
                    for o in range(NO):
                        z = o % 2
                        t = c * NO + o
                        pe.wait_ge(w_sem[z], c * (16 * NO // 2) + 16 * (o // 2) + 16)
                        pe.wait_ge(gates, 2 * t + 1)
                        for j in range(2):
                            for k in range(KD):
                                last = pe.matmul(bank[j][:, :], w[z][:, j * KD + k, :], hT[:, k, ds(c * CH, CH)],
                                                 start=(k == 0), stop=(k == KD - 1))
                            last.then_inc(mm, 1)
                        if o == 0:
                            pe.wait_ge(y2_ready, c * KA + KA + 1)
                        pe.wait_ge(m_b, t + 2)
                        for j, src in enumerate((at, y2)):
                            for k in range(KA):
                                last = pe.matmul(bank[2 + j][:, :], w[z][:, 2 * KD + j * KA + k, :], src[:, k, :],
                                                 start=(k == 0), stop=(k == KA - 1))
                            last.then_inc(mm, 1)

            @block.scalar
            def _(act):
                act.sem_inc(gates, 1)
                act.wait_ge(glu_in, 32)
                with act.Fori(0, NCH) as c:
                    for f in range(KA):
                        act.wait_ge(glu_mm, c * KA + f + 1)
                        act.activation(sg[:, f, :], pg[f][:, :], ACT.Sigmoid, bias=bg[:, f:f + 1]).then_inc(sig, 1)
                    for o in range(NO):
                        t = c * NO + o
                        for j, dst in enumerate((ga, gb)):
                            act.wait_ge(mm, 4 * t + 8 + j + 1)
                            act.wait_ge(m_b, t + 1)
                            act.activation(dst[o % 2][:, :], bank[j][:, :], ACT.Sigmoid).then_inc(gates, 1)

            @block.vector
            def _(dve):
                dve.sem_inc(m_b, 2)
                dve.sem_inc(y2_ready, 1)
                with dve.Fori(0, NCH) as c:
                    for f in range(KA):
                        dve.wait_ge(sig, c * KA + f + 1)
                        dve.wait_ge(mm, c * (4 * NO) + 8)
                        dve.tensor_tensor(y2[:, f, :], y[:, f, :], sg[:, f, :], ALU.mult).then_inc(y2_ready, 1)
                    for o in range(NO):
                        t = c * NO + o
                        z = o % 2
                        dve.wait_ge(gates, 2 * t + 3)
                        dve.wait_ge(mm, 4 * t + 8 + 4)
                        dve.wait_ge(mx_ready, t + 1)
                        dve.tensor_tensor(ta[z][:, :], bank[2][:, :], ga[z][:, :], ALU.mult).then_inc(m_a, 1)
                        dve.tensor_tensor(tb[z][:, :], bank[3][:, :], gb[z][:, :], ALU.mult).then_inc(m_b, 1)

            @block.gpsimd
            def _(pool):
                pool.sem_inc(mx_ready, 2)
                with pool.Fori(0, NCH) as c:
                    for o in range(NO):
                        t = c * NO + o
                        pool.wait_ge(m_b, t + 3)
                        pool.tensor_tensor(mx[:, o, :], ta[o % 2][:, :], tb[o % 2][:, :], ALU.add).then_inc(mx_ready, 1)
                    pool.wait_ge(mx_ready, c * NO + NO + 2)
                    pool.dma_start(mixed_d[:, :, ds(c * CH, CH)], mx[:, :, :]).then_inc(mx_out, 16)
                    pool.wait_ge(mx_out, 16 * c + 16)


def route(nc, x, mixed_d, w_out, g_row, w_router, b_router, empty_slots, ident, upper, ones, acc_d, h2_d, slots_d,
          table_d):
    with ExitStack() as ctx:
        t_ = Tools(nc, ctx, "rt")
        w = t_.sb("w", [P, KD, D])
        gb = t_.sb("gb", [P, D])
        wr = t_.sb("wr", [P, KD, NE])
        br = t_.sb("br", [1, NE])
        xt, mt, x1, h2 = ([t_.sb(f"{n}{z}", [P, D]) for z in range(2)] for n in ("x", "m", "x1", "h2"))
        h2T = t_.sb("h2T", [P, KD, P])
        zero = t_.sb("zero", [P, D])
        junk = t_.sb("junk", [P, D])
        ss, ms, rms, rstd, top, nbest, esum, resum, tok = (t_.sb(n, [P, 1]) for n in (
            "ss", "ms", "rms", "rstd", "top", "nbest", "esum", "resum", "tok"))
        lg, mask, chosen = (t_.sb(n, [P, NE]) for n in ("lg", "mask", "chosen"))
        v8 = t_.sb("v8", [P, 8])
        i8 = t_.sb("i8", [P, 8], U32)
        idx, ex, rsel, slot = (t_.sb(n, [P, TOPK]) for n in ("idx", "ex", "rsel", "slot"))
        ecol = t_.sb("ecol", [P, NE])
        hot, rk = (t_.sb(n, [P, TOPK, NE]) for n in ("hot", "rk"))
        slot_i = [t_.sb(f"slot_i{z}", [P, TOPK], U32) for z in range(2)]
        pay = [t_.sb(f"pay{z}", [P, TOPK, 2], I32) for z in range(2)]
        cnt, tiles, upto, before = (t_.sb(n, [P, NE]) for n in ("cnt", "tiles", "upto", "before"))
        row, ei, last_c, tab = (t_.sb(n, [P, k]) for n, k in (("row", 1), ("ei", 1), ("last_c", 1), ("tab", 4)))
        tab_i = t_.sb("tab_i", [P, 4], I32)
        po = [[t_.ps(f"o{z}{h}") for h in range(2)] for z in range(2)]
        pt = [t_.ps(f"t{h}") for h in range(2)]
        pl, pr = t_.ps("l"), t_.ps("r")
        x_in = [t_.sem(f"x_in{z}") for z in range(2)]
        x1_out = [t_.sem(f"x1_out{z}") for z in range(2)]
        h2_out = [t_.sem(f"h2_out{z}") for z in range(2)]
        tick = t_.sem("tick")
        (c_in, pre, pad_out, iot, mm, x1_ready, step, ms_ready, rms_ready, h2_ready, turned, h2T_ready, lg_mm, ex_in,
         ex_ready, mask_ready, rank_mm, rank_read, pay_ready, pay_free, sc_out, cnt_mm, fin, tab_out) = t_.sems(
            "c_in pre pad_out iot mm x1_ready step ms_ready rms_ready h2_ready turned h2T_ready lg_mm ex_in "
            "ex_ready mask_ready rank_mm rank_read pay_ready pay_free sc_out cnt_mm fin tab_out")
        rows = lambda ap, t: ap[ds(t * P, P), :]
        with nc.Block() as block:
            @block.sync
            def _(sp):
                sp.dma_start(w[:, :, :], w_out).then_inc(c_in, 16)
                sp.dma_start(gb[:, :], on_rows(g_row, P)).then_inc(c_in, 16)
                sp.dma_start(wr[:, :, :], w_router).then_inc(c_in, 16)
                sp.dma_start(br[:, :], on_rows(b_router, 1)).then_inc(c_in, 16)
                sp.dma_start(slots_d, empty_slots).then_inc(pre, 16)
                with sp.Fori(0, NT // 2) as i:
                    for z in range(2):
                        t = 2 * i + z
                        sp.wait_ge(h2_ready, t + 1)
                        sp.dma_start(xt[z][:, :], rows(x, t)).then_inc(x_in[z], 16)
                        sp.dma_start(mt[z][:, :].rearrange("p (k n) -> p k n", k=KD),
                                     mixed_d[:, :, ds(t * P, P)]).then_inc(x_in[z], 16)

            @block.scalar
            def _(act):
                act.sem_inc(h2T_ready, 2)
                for z in range(2):
                    act.sem_inc(x1_out[z], 16)
                    act.sem_inc(h2_out[z], 16)
                act.wait_ge(pad_out, 1)
                for g in range(NGT):
                    act.dma_start(h2_d[S + g * P:S + (g + 1) * P, :], zero[:, :]).then_inc(pre, 16)
                    act.dma_start(acc_d[S + g * P:S + (g + 1) * P, :], zero[:, :]).then_inc(pre, 16)

                def tile(t, z):
                    act.wait_ge(ms_ready, t + 1)
                    act.activation(rms[:, :], ms[:, :], ACT.Sqrt).then_inc(rms_ready, 1)
                    act.dma_start(rows(acc_d, t), x1[z][:, :]).then_inc(x1_out[z], 16)
                    act.wait_ge(h2_ready, t + 3)
                    act.dma_start(rows(h2_d, t), h2[z][:, :]).then_inc(h2_out[z], 16)
                    for h in range(2):
                        act.wait_ge(turned, 2 * t + h + 3)
                        if h == 0:
                            act.wait_ge(lg_mm, t + 1)
                        act.activation(h2T[:, 4 * h:4 * h + 4, :], pt[h][:, :].rearrange("p (k n) -> p k n", k=4),
                                       ACT.Copy).then_inc(h2T_ready, 1)
                    act.wait_ge(ex_in, t + 2)
                    act.activation(ex[:, :], v8[:, 0:TOPK], ACT.Exp, bias=nbest[:, :],
                                   accum_out=esum[:, :]).then_inc(ex_ready, 1)
                with act.Fori(0, NT // 2) as i:
                    for z in range(2):
                        tile(2 * i + z, z)
                for z in range(2):
                    act.wait_ge(x1_out[z], 16 * (NT // 2) + 16)
                    act.wait_ge(h2_out[z], 16 * (NT // 2) + 16)
                act.wait_ge(fin, 1)
                act.dma_start(table_d, tab_i[:, :]).then_inc(tab_out, 16)
                act.wait_ge(tab_out, 16)

            @block.tensor
            def _(pe):
                pe.sem_inc(lg_mm, 1)
                pe.sem_inc(turned, 2)
                pe.wait_ge(c_in, 64)

                def project(t, z):
                    pe.wait_ge(x_in[z], (t - z) * 16 + 32)
                    pe.wait_ge(x1_ready, 2 * t + 2)
                    for h in range(2):
                        for k in range(KD):
                            last = pe.matmul(po[z][h][:, :], mt[z][:, k * P:(k + 1) * P], w[:, k, h * 512:(h + 1) * 512],
                                             start=(k == 0), stop=(k == KD - 1))
                        last.then_inc(mm, 1)

                def choose(t, z):
                    pe.wait_ge(h2_ready, t + 3)
                    for h in range(2):
                        if h == 0:
                            pe.wait_ge(h2T_ready, 2 * t + 2)
                        for k in range(4):
                            last = pe.transpose(pt[h][:, k * P:(k + 1) * P],
                                                h2[z][:, (4 * h + k) * P:(4 * h + k + 1) * P], ident[:, :])
                        last.then_inc(turned, 1)
                    pe.wait_ge(h2T_ready, 2 * t + 4)
                    pe.wait_ge(ex_in, t + 1)
                    for k in range(KD):
                        pe.matmul(pl[:, 0:NE], h2T[:, k, :], wr[:, k, :], start=(k == 0), stop=False)
                    pe.matmul(pl[:, 0:NE], ones[0:1, :], br[:, :], start=False, stop=True).then_inc(lg_mm, 1)
                    pe.wait_ge(mask_ready, t + 1)
                    pe.matmul(pr[:, 0:NE], upper[:, :], mask[:, :], start=True, stop=False)
                    pe.matmul(pr[:, 0:NE], ones[:, :], chosen[:, :], start=False, stop=True).then_inc(rank_mm, 1)

                project(0, 0)
                with pe.Fori(0, NT // 2 - 1) as i:
                    project(2 * i + 1, 1)
                    choose(2 * i, 0)
                    project(2 * i + 2, 0)
                    choose(2 * i + 1, 1)
                project(NT - 1, 1)
                choose(NT - 2, 0)
                choose(NT - 1, 1)
                pe.wait_ge(rank_read, NT)
                pe.matmul(pr[:, 0:NE], ones[:, :], chosen[:, :], start=True, stop=True).then_inc(cnt_mm, 1)

            @block.gpsimd
            def _(pool):
                pool.sem_inc(pay_free, 2)
                pool.memset(zero[:, :], 0.0).then_inc(pad_out, 1)
                pool.iota(ecol[:, :], [[1, NE]], base=0, channel_multiplier=0,
                          allow_small_or_imprecise_dtypes=True).then_inc(iot, 1)
                pool.iota(tok[:, :], [[1, 1]], base=0, channel_multiplier=1,
                          allow_small_or_imprecise_dtypes=True).then_inc(iot, 1)
                pool.iota(row[:, :], [[1, 1]], base=0, channel_multiplier=1,
                          allow_small_or_imprecise_dtypes=True).then_inc(iot, 1)
                pool.wait_ge(pre, 16 + 32 * NGT)
                with pool.Fori(0, NT // 2) as i:
                    for z in range(2):
                        stop_until(pool, pay_ready, 2 * i + z + 1, tick)
                        for s in range(TOPK):
                            pool.indirect_dma_start(
                                out=slots_d, out_offset=bass.IndirectOffsetOnAxis(ap=slot_i[z][:, s:s + 1], axis=0),
                                in_=pay[z][:, s, :], in_offset=None).then_inc(sc_out, 16)
                        pool.wait_ge(sc_out, 16 * TOPK * (2 * i + z + 1))
                        pool.sem_inc(pay_free, 1)

            @block.vector
            def _(dve):
                tt, tsc, stt = dve.tensor_tensor, dve.tensor_scalar, dve.scalar_tensor_tensor
                dve.sem_inc(x1_ready, 4)
                dve.sem_inc(h2_ready, 2)
                dve.sem_inc(ex_in, 1)
                dve.memset(chosen[:, :], 0.0)
                dve.wait_ge(c_in, 64)
                dve.wait_ge(iot, 3)
                PER = 13

                def tile(t, z, i):
                    chain = Steps(dve, step, PER * t)
                    dve.wait_ge(x1_out[z], 16 * i + 16)
                    dve.wait_ge(h2_out[z], 16 * i + 16)
                    dve.wait_ge(x_in[z], 32 * i + 32)
                    for h in range(2):
                        dve.wait_ge(mm, 2 * t + h + 1)
                        tt(x1[z][:, h * 512:(h + 1) * 512], po[z][h][:, :], xt[z][:, h * 512:(h + 1) * 512],
                           ALU.add).then_inc(x1_ready, 1)
                    dve.wait_ge(x1_ready, 2 * t + 6)
                    chain(dve.tensor_tensor_reduce(junk[:, :], x1[z][:, :], x1[z][:, :], 1.0, 0.0, ALU.mult, ALU.add,
                                                   ss[:, :]))
                    tsc(ms[:, :], ss[:, :], 1.0 / D, EPS, ALU.mult, ALU.add).then_inc(ms_ready, 1)
                    dve.wait_ge(rms_ready, t + 1)
                    chain(dve.reciprocal(rstd[:, :], rms[:, :]))
                    dve.wait_ge(turned, 2 * t + 2)
                    stt(h2[z][:, :], x1[z][:, :], rstd[:, :], gb[:, :], ALU.mult, ALU.mult).then_inc(h2_ready, 1)
                    dve.wait_ge(lg_mm, t + 2)
                    chain(dve.tensor_copy(lg[:, :], pl[:, 0:NE]))
                    dve.sem_inc(tick, 1)
                    chain(dve.max(v8[:, :], lg[:, :]))
                    dve.sem_inc(tick, 1)
                    dve.max_index(i8[:, :], v8[:, :], lg[:, :])
                    tsc(nbest[:, :], v8[:, 0:1], -1.0, None, ALU.mult).then_inc(ex_in, 1)
                    dve.wait_ge(ex_in, t + 2)
                    chain(dve.tensor_copy(idx[:, :], i8[:, 0:TOPK]))
                    chain(tt(hot[:, :, :], ecol[:, :].unsqueeze(1).to_broadcast([P, TOPK, NE]),
                             idx[:, :].unsqueeze(2).to_broadcast([P, TOPK, NE]), ALU.is_equal))
                    dve.tensor_reduce(mask[:, :], hot[:, :, :].rearrange("p s e -> p e s"), AX.X,
                                      ALU.add).then_inc(mask_ready, 1)
                    dve.wait_ge(ex_ready, t + 1)
                    chain(dve.reciprocal(resum[:, :], esum[:, :]))
                    dve.wait_ge(pay_free, t + 1)
                    chain(tsc(pay[z][:, :, 1].bitcast(F32), ex[:, :], resum[:, :], None, ALU.mult))
                    chain(dve.tensor_copy(pay[z][:, :, 0], tok[:, :].to_broadcast([P, TOPK])))
                    dve.wait_ge(rank_mm, t + 1)
                    chain(tt(rk[:, :, :], hot[:, :, :], pr[:, 0:NE].unsqueeze(1).to_broadcast([P, TOPK, NE]), ALU.mult))
                    tt(chosen[:, :], chosen[:, :], mask[:, :], ALU.add).then_inc(rank_read, 1)
                    chain(dve.tensor_reduce(rsel[:, :], rk[:, :, :], AX.X, ALU.add))
                    chain(stt(slot[:, :], idx[:, :], float(REGION), rsel[:, :], ALU.mult, ALU.add))
                    dve.tensor_copy(slot_i[z][:, :], slot[:, :]).then_inc(pay_ready, 1)
                    dve.wait_ge(pay_ready, t + 1)
                    chain(tsc(tok[:, :], tok[:, :], float(P), None, ALU.add))
                    assert chain.n == PER, chain.n
                with dve.Fori(0, NT // 2) as i:
                    for z in range(2):
                        tile(2 * i + z, z, i)
                chain = Steps(dve, step, PER * NT)
                dve.wait_ge(cnt_mm, 1)
                dve.memset(junk[:, 0:NE], 1.0)
                chain(dve.tensor_copy(cnt[:, :], pr[:, 0:NE]))
                chain(tsc(tiles[:, :], cnt[:, :], float(CAP), 1.0, ALU.is_gt, ALU.add))
                for j in range(2, REGION // CAP):
                    chain(stt(tiles[:, :], cnt[:, :], float(j * CAP), tiles[:, :], ALU.is_gt, ALU.add))
                chain(dve.tensor_tensor_scan(upto[:, :], junk[:, 0:NE], tiles[:, :], 0.0, ALU.mult, ALU.add))
                chain(tsc(before[:, :], upto[:, :], row[:, :], None, ALU.is_le))
                dve.tensor_reduce(ei[:, :], before[:, :], AX.X, ALU.add)
                chain(tt(before[:, :], before[:, :], upto[:, :], ALU.mult))
                chain(dve.tensor_reduce(last_c[:, :], before[:, :], AX.X, ALU.max))
                tsc(tab[:, 0:1], ei[:, :], float(NE - 1), None, ALU.min)
                chain(tt(last_c[:, :], row[:, :], last_c[:, :], ALU.subtract))
                chain(tsc(last_c[:, :], last_c[:, :], float(CAP), None, ALU.mult))
                chain(stt(tab[:, 1:2], ei[:, :], float(REGION), last_c[:, :], ALU.mult, ALU.add))
                chain(tsc(tab[:, 1:2], tab[:, 1:2], float(NE * REGION - CAP), None, ALU.min))
                chain(dve.tensor_copy(tab[:, 2:4], upto[:, NE - 1:NE].to_broadcast([P, 2])))
                dve.tensor_copy(tab_i[:, :], tab[:, :]).then_inc(fin, 1)


def experts(nc, ident, w_gu, b_gu, w_down, b_down, h2_d, acc_d, slots_d, table_d):
    with ExitStack() as ctx:
        t_ = Tools(nc, ctx, "ex")
        tab = t_.sb("tab", [1, P * 4], I32)
        wg = [t_.sb(f"wg{f}", [P, KD, 2, P]) for f in range(NF)]
        wd = [t_.sb(f"wd{f}", [P, D]) for f in range(NF)]
        nxt, cur = (t_.sb(n, [P, NGT, 2], I32) for n in ("nxt", "cur"))
        xg = t_.sb("xg", [P, NGT, D])
        xT = t_.sb("xT", [P, KD, CAP])
        bin_, bgu = (t_.sb(n, [P, 2 * NF]) for n in ("bin", "bgu"))
        bd = t_.sb("bd", [P, D])
        t1, sg, t2, t4, at = ([t_.sb(f"{n}{z}", [P, CAP]) for z in range(2)] for n in ("t1", "sg", "t2", "t4", "at"))
        y = t_.sb("y", [P, NGT, D])
        down = [t_.ps(f"d{n}") for n in range(2 * NGT)]
        gu = [t_.ps(f"g{j}") for j in range(2)]
        wg_in = [t_.sem(f"wg_in{f}") for f in range(NF)]
        wd_in = [t_.sem(f"wd_in{f}") for f in range(NF)]
        (tab_in, b_in, bd_in, gu_mm, down_mm, gu_read, act_ready, clip, sig, prod, turned, xT_ready, sl_in, g_in, moved,
         cur_ready, b_ready, y_ready, y_scaled, y_out, y_free) = t_.sems(
            "tab_in b_in bd_in gu_mm down_mm gu_read act_ready clip sig prod turned xT_ready sl_in g_in moved "
            "cur_ready b_ready y_ready y_scaled y_out y_free")
        tick = t_.sem("tick")
        NB = 2 * NGT

        def number(eng):
            eng.wait_ge(tab_in, 16)
            return eng.value_load(tab[0:1, 2:3], min_val=NE, max_val=MAX_TILES)

        with nc.Block() as block:
            @block.sync
            def _(sp):
                sp.dma_start(tab[:, :], table_d.rearrange("a b -> (a b)").rearrange("(o n) -> o n", o=1)).then_inc(tab_in, 16)
                with sp.Fori(0, number(sp)) as i:
                    e = sp.value_load(tab[0:1, ds(i * 4, 1)], min_val=0, max_val=NE - 1)
                    sp.wait_ge(b_ready, i + 1)
                    sp.dma_start(bin_[:, :], b_gu[ds(e, 1)].rearrange("o p n -> (o p) n")).then_inc(b_in, 16)
                    for f in range(NF):
                        sp.wait_ge(gu_mm, 2 * NF * i + 2 * f + 2)
                        sp.dma_start(wg[f][:, :, :, :], w_gu[ds(e, 1), f].rearrange("o p k j n -> (o p) k j n")).then_inc(
                            wg_in[f], 16)
                        sp.wait_ge(down_mm, NF * i + f + 1)
                        sp.dma_start(wd[f][:, :], w_down[ds(e, 1), f * P:(f + 1) * P, :].rearrange("o p n -> (o p) n")).then_inc(
                            wd_in[f], 16)
                    sp.wait_ge(y_ready, NB * i + NB)
                    sp.dma_start(bd[:, :], b_down[ds(e, 1), :].to_broadcast([P, D])).then_inc(bd_in, 16)

            @block.gpsimd
            def _(pool):
                pool.sem_inc(y_free, 1)
                n = number(pool)

                def fetch(i):
                    base = pool.value_load(tab[0:1, ds(i * 4 + 1, 1)], min_val=0, max_val=NE * REGION - CAP)
                    pool.dma_start(nxt[:, :, :], slots_d[ds(base, CAP), :].rearrange("(g p) w -> p g w", p=P)).then_inc(
                        sl_in, 16)
                    stop_until(pool, sl_in, 16 * i + 16, tick)
                    stop_until(pool, turned, NB * i + NB, tick)
                    for g in range(NGT):
                        pool.indirect_dma_start(
                            out=xg[:, g, :], out_offset=None, in_=h2_d,
                            in_offset=bass.IndirectOffsetOnAxis(ap=nxt[:, g, 0:1].bitcast(U32), axis=0)).then_inc(g_in, 16)

                fetch(0)
                with pool.Fori(0, n) as i:
                    stop_until(pool, g_in, 16 * NGT * i + 16 * NGT, tick)
                    pool.tensor_copy(cur[:, :, 0], nxt[:, :, 0])
                    pool.tensor_copy(cur[:, :, 1].bitcast(F32), nxt[:, :, 1].bitcast(F32)).then_inc(cur_ready, 1)
                    stop_until(pool, cur_ready, i + 1, tick)
                    fetch(i + 1)
                    for g in range(NGT):
                        stop_until(pool, y_ready, NB * i + NB + 2 * g + 2, tick)
                        pool.tensor_scalar(y[:, g, :], y[:, g, :], cur[:, g, 1:2].bitcast(F32), None,
                                           ALU.mult).then_inc(y_scaled, 1)
                        stop_until(pool, y_scaled, NGT * i + g + 1, tick)
                        pool.indirect_dma_start(
                            out=acc_d, out_offset=bass.IndirectOffsetOnAxis(ap=cur[:, g, 0:1].bitcast(U32), axis=0),
                            in_=y[:, g, :], in_offset=None, compute_op=ALU.add).then_inc(y_out, 16)
                    pool.wait_ge(y_out, 16 * NGT * i + 16 * NGT)
                    pool.sem_inc(y_free, 1)
                pool.wait_ge(g_in, n * (16 * NGT) + 16 * NGT)

            @block.tensor
            def _(pe):
                pe.sem_inc(gu_mm, 2 * NF)
                pe.sem_inc(down_mm, NF)
                pe.sem_inc(turned, NB)
                n = number(pe)

                def turn(i, first):
                    pe.wait_ge(g_in, 16 * NGT * i + 16 * NGT)
                    for b in range(NB):
                        g, h = divmod(b, 2)
                        if b >= 2:
                            pe.wait_ge(xT_ready, NB * i + b - 1)
                        elif not first:
                            pe.wait_ge(gu_read, NF * i)
                        for k in range(4):
                            last = pe.transpose(gu[b % 2][:, k * P:(k + 1) * P],
                                                xg[:, g, (4 * h + k) * P:(4 * h + k + 1) * P], ident[:, :])
                        last.then_inc(turned, 1)

                def gate_up(i, f):
                    pe.wait_ge(wg_in[f], 16 * i + 16)
                    if f == 0:
                        pe.wait_ge(xT_ready, NB * i + NB)
                    for j in range(2):
                        if f:
                            pe.wait_ge((clip, gu_read)[j], NF * i + f)
                        for k in range(KD):
                            last = pe.matmul(gu[j][:, 0:CAP], wg[f][:, k, j, :], xT[:, k, :], start=(k == 0),
                                             stop=(k == KD - 1))
                        last.then_inc(gu_mm, 1)

                def down_product(i, f):
                    pe.wait_ge(wd_in[f], 16 * i + 16)
                    pe.wait_ge(act_ready, NF * i + f + 1)
                    if f == 0:
                        pe.wait_ge(y_ready, NB * i + NB)
                    for g in range(NGT):
                        for h in range(2):
                            last = pe.matmul(down[2 * g + h][:, :], at[f % 2][:, g * P:(g + 1) * P],
                                             wd[f][:, h * 512:(h + 1) * 512], start=(f == 0), stop=(f == NF - 1))
                    last.then_inc(down_mm, 1)

                turn(0, True)
                with pe.Fori(0, n) as i:
                    gate_up(i, 0)
                    for f in range(1, NF):
                        gate_up(i, f)
                        down_product(i, f - 1)
                    turn(i + 1, False)
                    down_product(i, NF - 1)

            @block.scalar
            def _(act):
                n = number(act)

                def save_x(i):
                    for b in range(NB):
                        g, h = divmod(b, 2)
                        act.wait_ge(turned, NB * i + NB + b + 1)
                        act.activation(xT[:, 4 * h:4 * h + 4, g * P:(g + 1) * P],
                                       gu[b % 2][:, :].rearrange("p (k n) -> p k n", k=4), ACT.Copy).then_inc(xT_ready, 1)
                save_x(0)
                with act.Fori(0, n) as i:
                    for f in range(NF):
                        act.wait_ge(clip, NF * i + f + 1)
                        act.activation(sg[f % 2][:, :], t1[f % 2][:, :], ACT.Sigmoid, scale=ALPHA).then_inc(sig, 1)
                    save_x(i + 1)

            @block.vector
            def _(dve):
                tt, tsc, stt = dve.tensor_tensor, dve.tensor_scalar, dve.scalar_tensor_tensor
                dve.sem_inc(b_ready, 1)
                dve.sem_inc(y_ready, NB)
                n = number(dve)
                with dve.Fori(0, n) as i:
                    dve.wait_ge(b_in, 16 * i + 16)
                    dve.tensor_copy(bgu[:, 0:NF], bin_[:, 0:NF])
                    tsc(bgu[:, NF:], bin_[:, NF:], 1.0, None, ALU.add).then_inc(b_ready, 1)
                    dve.wait_ge(b_ready, i + 2)
                    for f in range(NF):
                        z = f % 2
                        dve.wait_ge(gu_mm, 2 * NF * (i + 1) + 2 * f + 1)
                        tsc(t1[z][:, :], gu[0][:, 0:CAP], bgu[:, f:f + 1], LIMIT, ALU.add, ALU.min).then_inc(clip, 1)
                        dve.wait_ge(gu_mm, 2 * NF * (i + 1) + 2 * f + 2)
                        tsc(t2[z][:, :], gu[1][:, 0:CAP], bgu[:, NF + f:NF + f + 1], LIMIT + 1.0, ALU.add,
                            ALU.min).then_inc(gu_read, 1)
                        dve.wait_ge(sig, NF * i + f + 1)
                        tt(t4[z][:, :], t1[z][:, :], sg[z][:, :], ALU.mult).then_inc(prod, 1)
                        dve.wait_ge(prod, NF * i + f + 1)
                        dve.wait_ge(down_mm, NF * i + NF + f - 1)
                        stt(at[z][:, :], t2[z][:, :], 1.0 - LIMIT, t4[z][:, :], ALU.max, ALU.mult).then_inc(act_ready, 1)
                    dve.wait_ge(bd_in, 16 * i + 16)
                    dve.wait_ge(y_free, i + 1)
                    dve.wait_ge(down_mm, NF * i + 2 * NF)
                    for b in range(NB):
                        g, h = divmod(b, 2)
                        tt(y[:, g, h * 512:(h + 1) * 512], down[b][:, :], bd[:, h * 512:(h + 1) * 512],
                           ALU.add).then_inc(y_ready, 1)


def store(nc, acc_d, out):
    with nc.semaphore("st_done") as done, nc.Block() as block:
        @block.sync
        def _(sp):
            sp.dma_start(out, acc_d[0:S, :]).then_inc(done, 16)
            sp.wait_ge(done, 16)


def hybrid_layer(nc, a, out):
    scratch = lambda name, shape, dt=F32: nc.dram_tensor(name, list(shape), dt, kind="Internal").ap()
    att_d = scratch("att_d", [len(GROUPS), S, HG * RW])
    yT_d = scratch("yT_d", [P, SW // P, S])
    attT_d = scratch("attT_d", [P, NFT, S])
    mixed_d = scratch("mixed_d", [P, KD, S])
    rows_d = scratch("rows_d", [len(GROUPS) * HG, STEPS_W])
    acc_d = scratch("acc_d", [DUMP, D])
    h2_d = scratch("h2_d", [DUMP, D])
    slots_d = scratch("slots_d", [NE * REGION, 2], I32)
    table_d = scratch("table_d", [P, 4], I32)
    with ExitStack() as outer:
        keep = Tools(nc, outer, "k")
        ident, jflip, upper, ones = (keep.sb(n, [P, P]) for n in ("ident", "jflip", "upper", "ones"))
        make_constants(nc, ident, jflip, upper, ones)
        with ExitStack() as ctx:
            hT = Tools(nc, ctx, "k").sb("hT", [P, KD, S])
            normalise_input(nc, a["x"], a["g_mix"], hT, ident)
            s5(nc, hT, ident, a["w_in"][:, QKV:QKV + SW].rearrange("(k p) n -> p k n", p=P),
               [a[k] for k in ("a_re", "a_im", "log_dt", "b_re", "b_im", "c_re", "c_im", "d_skip")], yT_d)
            with ExitStack() as inner:
                bias = Tools(nc, inner, "k").sb("bias", [P, len(GROUPS) * HG, 2 * P])
                bias_tables(nc, a["rel_bias"], a["onehot"], rows_d, bias, jflip)
                attention(nc, hT, a["w_in"], a["q_gain"], a["k_gain"], bias, ident, att_d)
            combine(nc, att_d, ident, attT_d)
            mix(nc, hT, yT_d, attT_d, a["w_glu"], a["b_glu"], a["mix_w"], mixed_d)
        route(nc, a["x"], mixed_d, a["w_out"], a["g_ffn"], a["w_router"], a["b_router"], a["empty_slots"], ident,
              upper, ones, acc_d, h2_d, slots_d, table_d)
        experts(nc, ident, a["w_gu"], a["b_gu"], a["w_down"], a["b_down"], h2_d, acc_d, slots_d, table_d)
        store(nc, acc_d, out)


def by_state(w):
    w = w.reshape(PAIRS, 2, SN, *w.shape[2:])
    return np.moveaxis(w, 0, 2).reshape(2 * SN, PAIRS, *w.shape[3:])


def out_tiles(w):
    return w.reshape(-1, P, w.shape[1] // P, P).transpose(2, 1, 0, 3)


def k_tiles(w):
    return w.reshape(-1, P, w.shape[1]).transpose(1, 0, 2)


def kernel(x, g_mix, w_in, q_gain, k_gain, rel_bias, ssm_a_re, ssm_a_im, ssm_log_dt, ssm_b_re, ssm_b_im, ssm_c_re,
           ssm_c_im, ssm_d, w_glu, b_glu, w_attn_proj, w_ssm_proj, w_out, g_ffn, w_router, b_router, w_gate_up,
           b_gate_up, w_down, b_down):
    import concourse.bacc as bacc
    from concourse.bass_utils import run_bass_kernel_spmd

    w_in0 = np.asarray(w_in)[0]
    gates = QKV + SW
    slots = np.zeros((NE * REGION, 2), np.int32)
    slots[:, 0] = S + np.arange(NE * REGION) % CAP
    arrays = {
        "x": np.asarray(x)[0], "g_mix": np.asarray(g_mix)[0], "w_in": w_in0,
        "q_gain": np.asarray(q_gain)[0].T, "k_gain": np.asarray(k_gain)[0].T,
        "rel_bias": np.asarray(rel_bias), "onehot": bucket_onehot(),
        "a_re": by_state(np.asarray(ssm_a_re)[0]), "a_im": by_state(np.asarray(ssm_a_im)[0]),
        "log_dt": np.asarray(ssm_log_dt)[0].reshape(PAIRS, 2).T,
        "b_re": by_state(np.asarray(ssm_b_re)[0]), "b_im": by_state(np.asarray(ssm_b_im)[0]),
        "c_re": by_state(np.asarray(ssm_c_re)[0].transpose(0, 2, 1)),
        "c_im": by_state(np.asarray(ssm_c_im)[0].transpose(0, 2, 1)),
        "d_skip": np.asarray(ssm_d)[0].reshape(SG, SC).T,
        "w_glu": k_tiles(np.asarray(w_glu)[0]), "b_glu": np.asarray(b_glu)[0].reshape(-1, P).T,
        "mix_w": np.concatenate([out_tiles(m) for m in (
            w_in0[:, gates:gates + D], w_in0[:, gates + D:], np.asarray(w_attn_proj)[0], np.asarray(w_ssm_proj)[0])],
            axis=2),
        "w_out": k_tiles(np.asarray(w_out)[0]), "g_ffn": np.asarray(g_ffn)[0],
        "w_router": k_tiles(np.asarray(w_router)[0]), "b_router": np.asarray(b_router)[0], "empty_slots": slots,
        "w_gu": np.asarray(w_gate_up)[0].reshape(NE, KD, P, 2, NF, P).transpose(0, 4, 2, 1, 3, 5),
        "b_gu": np.asarray(b_gate_up)[0].reshape(NE, 2 * NF, P).transpose(0, 2, 1),
        "w_down": np.asarray(w_down)[0], "b_down": np.asarray(b_down)[0],
    }
    arrays = {k: np.ascontiguousarray(v) for k, v in arrays.items()}
    nc = bacc.Bacc("TRN2", target_bir_lowering=False, num_devices=1)
    a = {k: nc.dram_tensor(f"in_{k}", v.shape, mybir.dt.from_np(v.dtype), kind="ExternalInput").ap()
         for k, v in arrays.items()}
    out = nc.dram_tensor("out", [S, D], F32, kind="ExternalOutput").ap()
    hybrid_layer(nc, a, out)
    r = run_bass_kernel_spmd(nc, [{f"in_{k}": v for k, v in arrays.items()}], core_ids=[0])
    return r.results[0]["out"].reshape(1, S, D)
```

```python
from contextlib import ExitStack

import numpy as np

import concourse.bass as bass
from concourse import mybir

ALU = mybir.AluOpType
ACT = mybir.ActivationFunctionType
AX = mybir.AxisListType
F32 = mybir.dt.float32
F32R = mybir.dt.float32r
I32 = mybir.dt.int32
U32 = mybir.dt.uint32
ds = bass.ds

P = 128
D = 1024
KD = D // P
S = 2048
NT = S // P
DH = 64
GROUPS = ((128, 1), (512, 4), (2048, 16))
HG = 8
AW = HG * DH
NFT = AW // P
QKV = 3 * len(GROUPS) * AW
EPS = 1e-6
CH = 512
NCH = S // CH
NBLK = CH // P
MASKED = 1e30
BUCKETS, MAX_DIST = 32, 2048
STEPS_W = 384
RW = DH + 2
SW = 512
SG, SC, SN = 32, 16, 64
PAIRS = SG // 2
TS = 8
NC = S // TS
HC = NC // P
LEVELS = NC.bit_length() - 1
NE = 32
TOPK = 4
FF = 1024
NF = FF // P
LARGE, SMALL = 384, 256
NGT = LARGE // P
REGION = -(-S // LARGE) * LARGE
SLOTS = NE * REGION + LARGE
DUMP = S + LARGE
LIMIT, ALPHA = 7.0, 1.702


class Tools:

    def __init__(self, nc, ctx, tag):
        self.nc, self.ctx, self.tag, self.taken = nc, ctx, tag, []
        ctx.callback(self.give_back)

    def sb(self, name, shape, dt=F32):
        return self.ctx.enter_context(self.nc.sbuf_tensor(f"{self.tag}_{name}", list(shape), dt))

    def ps(self, name, shape=(P, 512), dt=F32):
        return self.ctx.enter_context(self.nc.psum_tensor(f"{self.tag}_{name}", list(shape), dt))

    def sem(self, name):
        self.taken.append(self.nc.alloc_semaphore(f"{self.tag}_{name}"))
        return self.taken[-1]

    def give_back(self):
        if self.taken:
            with self.nc.Block() as block:
                @block.gpsimd
                def _(pool):
                    for sem in self.taken:
                        pool.sem_clear(sem)
            for sem in self.taken:
                self.nc.release_semaphore(sem)

    def sems(self, names):
        return [self.sem(n) for n in names.split()]


class Steps:

    def __init__(self, eng, sem, base=0):
        self.eng, self.sem, self.base, self.n = eng, sem, base, 0

    def __call__(self, ins):
        self.n += 1
        ins.then_inc(self.sem, 1)
        self.eng.wait_ge(self.sem, self.base + self.n)


def stop_until(eng, sem, value, tick):
    eng.wait_ge(sem, value)
    eng.sem_inc(tick, 1)


def on_rows(row, n):
    return row.rearrange("(a w) -> a w", a=1).to_broadcast([n, row.shape[0]])


def make_constants(nc, ident, jflip, upper, ones):
    with ExitStack() as ctx:
        t_ = Tools(nc, ctx, "cst")
        filled, made = t_.sems("filled made")
        with nc.Block() as block:
            @block.gpsimd
            def _(pool):
                pool.memset(ident[:, :], 0.0).then_inc(filled, 1)
                pool.memset(jflip[:, :], 0.0).then_inc(filled, 1)
                pool.memset(upper[:, :], 0.0).then_inc(filled, 1)
                pool.memset(ones[:, :], 1.0).then_inc(made, 1)
                pool.wait_ge(filled, 3)
                pool.affine_select(out=ident[:, :], in_=ident[:, :], compare_op=ALU.not_equal, fill=1.0, base=0,
                                   pattern=[[-1, P]], channel_multiplier=1).then_inc(made, 1)
                pool.affine_select(out=jflip[:, :], in_=jflip[:, :], compare_op=ALU.not_equal, fill=1.0,
                                   base=1 - P, pattern=[[1, P]], channel_multiplier=1).then_inc(made, 1)
                pool.affine_select(out=upper[:, :], in_=upper[:, :], compare_op=ALU.is_ge, fill=1.0, base=0,
                                   pattern=[[-1, P]], channel_multiplier=1).then_inc(made, 1)
                pool.wait_ge(made, 4)


def normalise_input(nc, x, g_row, hT, ident):
    with ExitStack() as ctx:
        t_ = Tools(nc, ctx, "nrm")
        xt = [t_.sb(f"x{s}", [P, D]) for s in range(2)]
        hh = [t_.sb(f"h{s}", [P, D]) for s in range(2)]
        gb = t_.sb("gb", [P, D])
        junk = t_.sb("junk", [P, D])
        ss, ms, rms, rstd = (t_.sb(n, [P, 2]) for n in ("ss", "ms", "rms", "rstd"))
        pt = [[t_.ps(f"pt{s}{h}") for h in range(2)] for s in range(2)]
        x_in = [t_.sem(f"x_in{s}") for s in range(2)]
        g_in, step, ms_ready, rms_ready, h_ready, t_ready, t_free = t_.sems(
            "g_in step ms_ready rms_ready h_ready t_ready t_free")
        with nc.Block() as block:
            @block.sync
            def _(sp):
                sp.dma_start(gb[:, :], on_rows(g_row, P)).then_inc(g_in, 16)
                with sp.Fori(0, NT // 2) as i:
                    for s in range(2):
                        sp.wait_ge(h_ready, 2 * i + s + 1)
                        sp.dma_start(xt[s][:, :], x[ds(i * (2 * P) + s * P, P), :]).then_inc(x_in[s], 16)

            @block.vector
            def _(dve):
                dve.sem_inc(h_ready, 2)
                dve.wait_ge(g_in, 16)
                with dve.Fori(0, NT // 2) as i:
                    chain = Steps(dve, step, 4 * i)
                    for s in range(2):
                        dve.wait_ge(x_in[s], 16 * i + 16)
                        chain(dve.tensor_tensor_reduce(junk[:, :], xt[s][:, :], xt[s][:, :], 1.0, 0.0, ALU.mult,
                                                       ALU.add, ss[:, s:s + 1]))
                        dve.tensor_scalar(ms[:, s:s + 1], ss[:, s:s + 1], 1.0 / D, EPS, ALU.mult,
                                          ALU.add).then_inc(ms_ready, 1)
                        dve.wait_ge(rms_ready, 2 * i + s + 1)
                        chain(dve.reciprocal(rstd[:, s:s + 1], rms[:, s:s + 1]))
                        dve.wait_ge(t_free, 4 * i + 2 * s + 2)
                        dve.scalar_tensor_tensor(hh[s][:, :], xt[s][:, :], rstd[:, s:s + 1], gb[:, :], ALU.mult,
                                                 ALU.mult).then_inc(h_ready, 1)

            @block.tensor
            def _(pe):
                with pe.Fori(0, NT // 2) as i:
                    for s in range(2):
                        pe.wait_ge(h_ready, 2 * i + s + 3)
                        for h in range(2):
                            for k in range(4):
                                last = pe.transpose(pt[s][h][:, k * P:(k + 1) * P],
                                                    hh[s][:, (4 * h + k) * P:(4 * h + k + 1) * P], ident[:, :])
                            last.then_inc(t_ready, 1)

            @block.scalar
            def _(act):
                act.sem_inc(t_free, 4)
                with act.Fori(0, NT // 2) as i:
                    for s in range(2):
                        act.wait_ge(ms_ready, 2 * i + s + 1)
                        act.activation(rms[:, s:s + 1], ms[:, s:s + 1], ACT.Sqrt).then_inc(rms_ready, 1)
                        for h in range(2):
                            act.wait_ge(t_ready, 4 * i + 2 * s + h + 1)
                            act.activation(hT[:, 4 * h:4 * h + 4, ds(i * (2 * P) + s * P, P)],
                                           pt[s][h][:, :].rearrange("p (k n) -> p k n", k=4),
                                           ACT.Copy).then_inc(t_free, 1)


def s5(nc, hT, ident, w_u, prm, y_out):
    a_re, a_im, log_dt, b_re, b_im, c_re, c_im, d_skip = prm
    NP9 = TS + 1
    LEAD = (TS - 1) * SC
    TWO_PI = 2 * np.pi
    C1 = 6.28125
    C2 = float(np.float32(np.round((TWO_PI - C1) * 2 ** 22) / 2 ** 22))
    C3 = float(np.float32(TWO_PI - C1 - C2))
    ROUND = 1.5 * 2.0 ** 23
    HALVINGS = 10
    with ExitStack() as ctx:
        t_ = Tools(nc, ctx, "s5")
        w = t_.sb("w", [P, KD, SW])
        tok = t_.sb("tok", [P, HC, TS, SW])
        yT = t_.sb("yT", [P, SW // P, S])
        lr, li, dt = (t_.sb(n, [P, PAIRS]) for n in ("lr", "li", "dt"))
        br0, bi0, cr, ci, br, bi = (t_.sb(n, [P, PAIRS, SC]) for n in ("br0", "bi0", "cr", "ci", "br", "bi"))
        d8 = t_.sb("d8", [P, SG])
        v = [t_.sb(f"v{n}", [P, PAIRS]) for n in range(12)]
        t16 = [t_.sb(f"t16{n}", [P, PAIRS, SC]) for n in range(2)]
        pr, pi, npi = (t_.sb(n, [P, PAIRS, NP9]) for n in ("pr", "pi", "npi"))
        rr, ri = (t_.sb(n, [P, PAIRS, TS]) for n in ("rr", "ri"))
        lar, lai, nlai = (t_.sb(n, [P, PAIRS, LEVELS]) for n in ("lar", "lai", "nlai"))
        ust = [t_.sb(f"ust{z}", [P, HC, 2, TS, SC]) for z in range(2)]
        bpad = [t_.sb(f"bpad{z}", [P, 2, 2 * LEAD + SC]) for z in range(2)]
        cpad = [t_.sb(f"cpad{z}", [P, 2, LEAD + NP9 * SC]) for z in range(2)]
        inm = [t_.sb(f"inm{z}", [P, 2, TS * SC]) for z in range(2)]
        tmp = [t_.sb(f"tmp{n}", [P, NP9 * SC]) for n in range(4)]
        u8 = [t_.sb(f"u8{z}", [P, 2 * NC]) for z in range(2)]
        inT = [t_.sb(f"inT{z}", [P, 2, P]) for z in range(2)]
        intra = [t_.sb(f"intra{z}", [P, 2, P]) for z in range(2)]
        st = [t_.sb(f"st{z}", [P, 2, NC + 1]) for z in range(2)]
        alt = t_.sb("alt", [P, 2, NC + 1])
        ps_u = [t_.ps(f"u{z}") for z in range(2)]
        ps_8, ps_in, ps_it0, ps_x = (t_.ps(n) for n in ("p8", "pin", "pit", "px"))
        ps_it = (ps_it0, ps_u[0])
        ps_y = [t_.ps(f"y{h}") for h in range(2)]
        (w_in, prm_in, dt_ready, chain_v, maps_ready, pads_ready, u_ready, u_saved, chain_p, staged, t8, tin, kin,
         acts, it_saved, x_ready, x_saved, scanned, y_ready, y_saved, chain_s, yt_ready, yt_saved, y_stored) = t_.sems(
            "w_in prm_in dt_ready chain_v maps_ready pads_ready u_ready u_saved chain_p staged t8 tin kin "
            "acts it_saved x_ready x_saved scanned y_ready y_saved chain_s yt_ready yt_saved y_stored")

        with nc.Block() as block:
            @block.sync
            def _(sp):
                sp.dma_start(w[:, :, :], w_u).then_inc(w_in, 16)
                n = 0
                for dst, src in ((lr, a_re), (li, a_im)):
                    sp.dma_start(dst[:, :], src).then_inc(prm_in, 16)
                    n += 1
                for h in range(2):
                    sp.dma_start(dt[SN * h:SN * (h + 1), :], on_rows(log_dt[h], SN)).then_inc(prm_in, 16)
                    n += 1
                for dst, src in ((br0, b_re), (bi0, b_im), (cr, c_re), (ci, c_im)):
                    sp.dma_start(dst[:, :, :], src).then_inc(prm_in, 16)
                    n += 1
                for s in range(TS):
                    sp.dma_start(d8[SC * s:SC * (s + 1), :], d_skip).then_inc(prm_in, 16)
                    n += 1
                sp.wait_ge(yt_saved, HC * TS)
                sp.dma_start(y_out, yT[:, :, :]).then_inc(y_stored, 16)
                sp.wait_ge(y_stored, 16)
            PRM = 16 * (8 + TS)

            @block.gpsimd
            def _(pool):
                for z in range(2):
                    pool.memset(bpad[z][:, :, :], 0.0)
                    last = pool.memset(cpad[z][:, :, :], 0.0)
                last.then_inc(pads_ready, 1)
                pool.wait_ge(pads_ready, 1)
                pool.wait_ge(maps_ready, 1)
                pool.wait_ge(u_saved, HC * TS)

                def build(p, z, free):
                    if free is not None:
                        pool.wait_ge(y_ready, free)
                    chain = Steps(pool, chain_p, 3 * p)
                    for k in range(HC):
                        pool.tensor_copy(ust[z][:, k, :, :, :],
                                         tok[:, k, :, ds(p * 2 * SC, 2 * SC)].rearrange("p j (h c) -> p h j c", h=2))
                    pool.tensor_copy(bpad[z][:, 0, LEAD:LEAD + SC], br[:, ds(p, 1), :].rearrange("p a c -> p (a c)"))
                    pool.tensor_copy(bpad[z][:, 1, LEAD:LEAD + SC], bi[:, ds(p, 1), :].rearrange("p a c -> p (a c)"))

                    def outer(dst, power, factor, n):
                        return pool.tensor_tensor(
                            dst[:, 0:n * SC].rearrange("p (j c) -> p j c", c=SC),
                            power[:, ds(p, 1), :].rearrange("p a j -> p (a j)").unsqueeze(2).to_broadcast([P, n, SC]),
                            factor[:, ds(p, 1), :].to_broadcast([P, n, SC]), ALU.mult)

                    for (a, b, c, d), dst, off, n, op in (
                            (((rr, br), (ri, bi), (rr, bi), (ri, br)), inm, 0, TS, (ALU.subtract, ALU.add)),
                            (((pr, cr), (npi, ci), (npi, cr), (pr, ci)), cpad, LEAD, NP9, (ALU.add, ALU.subtract))):
                        for t, (power, factor) in zip(tmp[:3], (a, b, c)):
                            outer(t, power, factor, n)
                        chain(outer(tmp[3], *d, n))
                        pool.tensor_tensor(dst[z][:, 0, off:off + n * SC], tmp[0][:, 0:n * SC], tmp[1][:, 0:n * SC], op[0])
                        last = pool.tensor_tensor(dst[z][:, 1, off:off + n * SC], tmp[2][:, 0:n * SC],
                                                  tmp[3][:, 0:n * SC], op[1])
                        if dst is inm:
                            chain(last)
                    last.then_inc(staged, 1)
                    pool.wait_ge(staged, p + 1)

                for p in range(2):
                    build(p, p, None)
                with pool.Fori(1, PAIRS // 2) as i:
                    for z in range(2):
                        build(2 * i + z, z, 2 * i + z - 1)

            @block.tensor
            def _(pe):
                pe.wait_ge(w_in, 16)
                for n in range(HC * TS):
                    k, j = divmod(n, TS)
                    if n >= 2:
                        pe.wait_ge(u_saved, n - 1)
                    for c in range(KD):
                        lhs = hT[:, c, k * P * TS + j:(k * P + P - 1) * TS + j + 1:TS]
                        last = pe.matmul(ps_u[n % 2][:, :], lhs, w[:, c, :], start=(c == 0), stop=(c == KD - 1))
                    last.then_inc(u_ready, 1)

                def inputs(p, z):
                    pe.wait_ge(staged, p + 1)
                    pe.wait_ge(acts, 2 * p + 1)
                    for h in range(2):
                        for k in range(HC):
                            last = pe.transpose(ps_8[:, h * NC + k * P:h * NC + (k + 1) * P],
                                                ust[z][:, k, h, :, :].rearrange("p j c -> p (j c)"), ident[:, :])
                    last.then_inc(t8, 1)
                    for r in range(2):
                        last = pe.transpose(ps_in[:, r * P:(r + 1) * P], inm[z][:, r, :], ident[:, :])
                    last.then_inc(tin, 1)
                    pe.wait_ge(it_saved, 2 * p + 2)
                    for h in range(2):
                        q = slice(SN * h, SN * (h + 1))
                        for s in range(TS):
                            for r in range(2):
                                last = pe.matmul(ps_it[h][:, 0:P], bpad[z][q, r, LEAD - SC * s:LEAD - SC * s + P],
                                                 cpad[z][q, r, LEAD - SC * s:LEAD - SC * s + P],
                                                 start=(s == 0 and r == 0), stop=(s == TS - 1 and r == 1))
                    last.then_inc(kin, 1)
                    pe.wait_ge(acts, 2 * p + 3)
                    pe.wait_ge(x_saved, p + 1)
                    for r in range(2):
                        for h in range(2):
                            last = pe.matmul(ps_x[SN * h:SN * (h + 1), r * NC:(r + 1) * NC],
                                             inT[z][:, r, SN * h:SN * (h + 1)], u8[z][:, h * NC:(h + 1) * NC],
                                             start=True, stop=True)
                    last.then_inc(x_ready, 1)

                def outputs(p, z):
                    pe.wait_ge(scanned, p + 1)
                    pe.wait_ge(y_saved, 4 * p + 4)
                    for h in range(2):
                        q = slice(SN * h, SN * (h + 1))
                        for k in range(HC):
                            out = ps_y[h][:, k * P:(k + 1) * P]
                            pe.matmul(out, u8[z][:, h * NC + k * P:h * NC + (k + 1) * P], intra[z][:, h, :],
                                      start=True, stop=False)
                            for r in range(2):
                                last = pe.matmul(out, st[z][q, r, k * P:(k + 1) * P], cpad[z][q, r, LEAD + SC:],
                                                 start=False, stop=(r == 1))
                    last.then_inc(y_ready, 1)

                inputs(0, 0)
                with pe.Fori(0, PAIRS // 2 - 1) as i:
                    inputs(2 * i + 1, 1)
                    outputs(2 * i, 0)
                    inputs(2 * i + 2, 0)
                    outputs(2 * i + 1, 1)
                inputs(PAIRS - 1, 1)
                outputs(PAIRS - 2, 0)
                outputs(PAIRS - 1, 1)
                pe.wait_ge(y_saved, 4 * PAIRS + 4)
                for n in range(HC * TS):
                    k, j = divmod(n, TS)
                    if n >= 2:
                        pe.wait_ge(yt_saved, n - 1)
                    for f in range(SW // P):
                        last = pe.transpose(ps_u[n % 2][:, f * P:(f + 1) * P], tok[:, k, j, f * P:(f + 1) * P], ident[:, :])
                    last.then_inc(yt_ready, 1)

            @block.scalar
            def _(act):
                act.sem_inc(acts, 1)
                act.sem_inc(y_saved, 4)
                act.wait_ge(prm_in, PRM)
                act.activation(dt[:, :], dt[:, :], ACT.Exp).then_inc(dt_ready, 1)
                for n in range(HC * TS):
                    k, j = divmod(n, TS)
                    act.wait_ge(u_ready, n + 1)
                    act.activation(tok[:, k, j, :], ps_u[n % 2][:, :], ACT.Copy).then_inc(u_saved, 1)

                def save_inputs(p, z):
                    act.wait_ge(t8, p + 1)
                    act.activation(u8[z][:, :], ps_8[:, :], ACT.Copy).then_inc(acts, 1)
                    act.wait_ge(tin, p + 1)
                    act.activation(inT[z][:, :, :], ps_in[:, 0:2 * P].rearrange("p (r n) -> p r n", r=2),
                                   ACT.Copy).then_inc(acts, 1)

                def save_outputs(p, z):
                    act.wait_ge(y_ready, p + 1)
                    for h in range(2):
                        for k in range(HC):
                            act.activation(tok[:, k, :, ds(p * 2 * SC + h * SC, SC)],
                                           ps_y[h][:, k * P:(k + 1) * P].rearrange(
                                               "p (j c) -> p j c", c=SC), ACT.Gelu_apprx_tanh).then_inc(y_saved, 1)

                save_inputs(0, 0)
                with act.Fori(0, PAIRS // 2 - 1) as i:
                    save_inputs(2 * i + 1, 1)
                    save_outputs(2 * i, 0)
                    save_inputs(2 * i + 2, 0)
                    save_outputs(2 * i + 1, 1)
                save_inputs(PAIRS - 1, 1)
                save_outputs(PAIRS - 2, 0)
                save_outputs(PAIRS - 1, 1)

            @block.vector
            def _(dve):
                for z in range(2):
                    dve.memset(st[z][:, :, 0:1], 0.0)
                dve.sem_inc(it_saved, 2)
                dve.sem_inc(x_saved, 1)
                go = Steps(dve, chain_v)
                tt, tsc, stt = dve.tensor_tensor, dve.tensor_scalar, dve.scalar_tensor_tensor

                def cmul(re, im, ar, ai, b_r, b_i, t):
                    tt(t[0], ar, b_r, ALU.mult)
                    tt(t[1], ai, b_i, ALU.mult)
                    tt(t[2], ar, b_i, ALU.mult)
                    go(tt(t[3], ai, b_r, ALU.mult))
                    tt(re, t[0], t[1], ALU.subtract)
                    go(tt(im, t[2], t[3], ALU.add))

                vv = [x[:, :] for x in v]
                t4 = vv[8:12]
                dve.wait_ge(dt_ready, 1)
                tt(vv[0], lr[:, :], dt[:, :], ALU.mult)
                go(tt(vv[1], li[:, :], dt[:, :], ALU.mult))
                go(tsc(vv[2], vv[1], 1.0 / TWO_PI, None, ALU.mult))
                go(tsc(vv[2], vv[2], ROUND, None, ALU.add))
                go(tsc(vv[2], vv[2], -ROUND, None, ALU.add))
                for c in (C1, C2, C3):
                    go(stt(vv[1], vv[2], -c, vv[1], ALU.mult, ALU.add))
                go(tsc(vv[0], vv[0], -110.0, 100.0, ALU.max, ALU.min))
                tsc(vv[0], vv[0], 0.5 ** HALVINGS, None, ALU.mult)
                go(tsc(vv[1], vv[1], 0.5 ** HALVINGS, None, ALU.mult))
                tsc(vv[2], vv[0], 1 / 6, 1.0, ALU.mult, ALU.add)
                go(tsc(vv[3], vv[1], 1 / 6, None, ALU.mult))
                for k in (5, 4, 3, 2):
                    cmul(vv[4], vv[5], vv[0], vv[1], vv[2], vv[3], t4)
                    tsc(vv[2], vv[4], 1 / k, 1.0, ALU.mult, ALU.add)
                    go(tsc(vv[3], vv[5], 1 / k, None, ALU.mult))
                cmul(vv[4], vv[5], vv[0], vv[1], vv[2], vv[3], t4)
                for _ in range(HALVINGS):
                    stt(t4[0], vv[4], 2.0, vv[4], ALU.add, ALU.mult)
                    tt(t4[1], vv[5], vv[5], ALU.mult)
                    go(stt(t4[2], vv[4], 1.0, vv[5], ALU.add, ALU.mult))
                    tt(vv[4], t4[0], t4[1], ALU.subtract)
                    go(tsc(vv[5], t4[2], 2.0, None, ALU.mult))
                er, ei = vv[4], vv[5]
                tsc(vv[6], li[:, :], -1.0, None, ALU.mult)
                tt(t4[0], lr[:, :], lr[:, :], ALU.mult)
                go(tt(t4[1], li[:, :], li[:, :], ALU.mult))
                go(tt(vv[7], t4[0], t4[1], ALU.add))
                go(dve.reciprocal(vv[7], vv[7]))
                cmul(vv[0], vv[1], er, ei, lr[:, :], vv[6], t4)
                tt(vv[2], vv[0], vv[7], ALU.mult)
                go(tt(vv[3], vv[1], vv[7], ALU.mult))
                fr, fi = (x.unsqueeze(2).to_broadcast([P, PAIRS, SC]) for x in (vv[2], vv[3]))
                for dst, (f0, b0), (f1, b1), op in ((br, (fr, br0), (fi, bi0), ALU.subtract),
                                                    (bi, (fr, bi0), (fi, br0), ALU.add)):
                    tt(t16[0][:, :, :], b0[:, :, :], f0, ALU.mult)
                    go(tt(t16[1][:, :, :], b1[:, :, :], f1, ALU.mult))
                    go(tt(dst[:, :, :], t16[0][:, :, :], t16[1][:, :, :], op))
                dve.memset(pr[:, :, 0:1], 1.0)
                dve.memset(pi[:, :, 0:1], 0.0)
                tsc(pr[:, :, 1], er, 1.0, None, ALU.add)
                go(dve.tensor_copy(pi[:, :, 1], ei))
                for j in range(2, NP9):
                    cmul(pr[:, :, j], pi[:, :, j], pr[:, :, j - 1], pi[:, :, j - 1], pr[:, :, 1], pi[:, :, 1], t4)
                tsc(npi[:, :, :], pi[:, :, :], -1.0, None, ALU.mult)
                for j in range(TS):
                    dve.tensor_copy(rr[:, :, j], pr[:, :, TS - 1 - j])
                    dve.tensor_copy(ri[:, :, j], pi[:, :, TS - 1 - j])
                dve.tensor_copy(lar[:, :, 0], pr[:, :, TS])
                go(dve.tensor_copy(lai[:, :, 0], pi[:, :, TS]))
                for l in range(1, LEVELS):
                    a, b = lar[:, :, l - 1], lai[:, :, l - 1]
                    cmul(lar[:, :, l], lai[:, :, l], a, b, a, b, t4)
                go(tsc(nlai[:, :, :], lai[:, :, :], -1.0, None, ALU.mult))
                dve.sem_inc(maps_ready, 1)

                def scan(p, z):
                    dve.wait_ge(kin, p + 1)
                    for h in range(2):
                        stt(intra[z][:, h, :], ident[:, :], d8[:, ds(2 * p + h, 1)], ps_it[h][:, 0:P],
                            ALU.mult, ALU.add).then_inc(it_saved, 1)
                    dve.wait_ge(x_ready, p + 1)
                    dve.tensor_copy(st[z][:, :, 1:], ps_x[:, :].rearrange("p (r n) -> p r n", r=2)).then_inc(x_saved, 1)
                    dve.wait_ge(x_saved, p + 2)
                    chain = Steps(dve, chain_s, (2 * LEVELS - 1) * p)
                    src, dst = st[z], alt
                    for l in range(LEVELS):
                        s = 1 << l
                        scalar = [x[:, ds(p, 1), l:l + 1].rearrange("p a b -> p (a b)") for x in (lar, nlai, lai)]
                        dve.tensor_copy(dst[:, :, 1:1 + s], src[:, :, 1:1 + s])
                        chain(stt(dst[:, :, 1 + s:], src[:, :, 1:NC + 1 - s], scalar[0], src[:, :, 1 + s:],
                                  ALU.mult, ALU.add))
                        stt(dst[:, 0, 1 + s:], src[:, 1, 1:NC + 1 - s], scalar[1], dst[:, 0, 1 + s:], ALU.mult, ALU.add)
                        last = stt(dst[:, 1, 1 + s:], src[:, 0, 1:NC + 1 - s], scalar[2], dst[:, 1, 1 + s:],
                                   ALU.mult, ALU.add)
                        if l < LEVELS - 1:
                            chain(last)
                        src, dst = dst, src
                    last.then_inc(scanned, 1)
                    dve.wait_ge(scanned, p + 1)

                with dve.Fori(0, PAIRS // 2) as i:
                    for z in range(2):
                        scan(2 * i + z, z)
                for n in range(HC * TS):
                    k, j = divmod(n, TS)
                    dve.wait_ge(yt_ready, n + 1)
                    first = k * P * TS + j
                    dve.tensor_copy(yT[:, :, first:first + (P - 1) * TS + 1:TS],
                                    ps_u[n % 2][:, :].rearrange("p (f n) -> p f n", f=SW // P)).then_inc(yt_saved, 1)


def bucket_onehot():
    hot = np.zeros((BUCKETS + 1, len(GROUPS), STEPS_W), np.float32)
    exact = BUCKETS // 2
    for g, (window, dilation) in enumerate(GROUPS):
        steps = 2 * P - 1 - np.arange(STEPS_W)
        inside = (steps >= 0) & (steps <= window // dilation)
        dist = np.clip(steps, 0, None) * dilation
        far = exact + (np.log(np.maximum(dist, 1).astype(np.float32) / exact) / np.log(MAX_DIST / exact)
                       * (BUCKETS - exact)).astype(np.int32)
        bucket = np.where(dist < exact, dist, np.minimum(far, BUCKETS - 1))
        hot[bucket[inside], g, np.nonzero(inside)[0]] = 1.0
        hot[BUCKETS, g] = np.where(inside, 0.0, MASKED)
    return hot


def bias_tables(nc, rel_bias, onehot, rows_d, bias, jflip):
    NG, NH = len(GROUPS), len(GROUPS) * HG
    with ExitStack() as ctx:
        t_ = Tools(nc, ctx, "bia")
        rel = t_.sb("rel", [BUCKETS + 1, NH])
        hot = t_.sb("hot", [BUCKETS + 1, NG, STEPS_W])
        rows = t_.sb("rows", [HG, NG, STEPS_W])
        hank = t_.sb("hank", [P, NH, 2 * P])
        pr = [t_.ps(f"pr{g}") for g in range(NG)]
        pf = [t_.ps(f"pf{n}") for n in range(4)]
        loaded, negated, rows_ready, rows_saved, rows_out, hank_in, flipped, saved = t_.sems(
            "loaded negated rows_ready rows_saved rows_out hank_in flipped saved")
        with nc.Block() as block:
            @block.sync
            def _(sp):
                sp.dma_start(rel[0:BUCKETS, :], rel_bias).then_inc(loaded, 16)
                sp.dma_start(hot[:, :, :], onehot).then_inc(loaded, 16)
                sp.wait_ge(rows_saved, NG)
                sp.dma_start(rows_d.rearrange("(g h) s -> h g s", g=NG), rows[:, :, :]).then_inc(rows_out, 16)
                sp.wait_ge(rows_out, 16)
                shifted = bass.AP(rows_d.tensor, rows_d.offset, [[1, P], [STEPS_W, NH], [1, 2 * P]])
                sp.dma_start(hank[:, :, :], shifted).then_inc(hank_in, 16)

            @block.vector
            def _(dve):
                dve.memset(rel[BUCKETS:BUCKETS + 1, :], 1.0)
                dve.wait_ge(loaded, 32)
                dve.tensor_scalar(rel[0:BUCKETS, :], rel[0:BUCKETS, :], -1.0, None, ALU.mult).then_inc(negated, 1)
                for g in range(NG):
                    dve.wait_ge(rows_ready, g + 1)
                    dve.tensor_copy(rows[:, g, :], pr[g][0:HG, 0:STEPS_W]).then_inc(rows_saved, 1)
                for n in range(NH // 2):
                    dve.wait_ge(flipped, n + 1)
                    dve.tensor_copy(bias[:, 2 * n:2 * n + 2, :],
                                    pf[n % 4][:, :].rearrange("p (h k) -> p h k", h=2)).then_inc(saved, 1)

            @block.tensor
            def _(pe):
                pe.wait_ge(negated, 1)
                for g in range(NG):
                    pe.matmul(pr[g][0:HG, 0:STEPS_W], rel[:, g * HG:(g + 1) * HG], hot[:, g, :], start=True,
                              stop=True).then_inc(rows_ready, 1)
                pe.wait_ge(hank_in, 16)
                for n in range(NH // 2):
                    if n >= 4:
                        pe.wait_ge(saved, n - 3)
                    pe.matmul(pf[n % 4][:, :], jflip[:, :],
                              hank[:, 2 * n:2 * n + 2, :].rearrange("p h k -> p (h k)"), start=True,
                              stop=True).then_inc(flipped, 1)


def attention(nc, hT, w_in, q_gain, k_gain, bias, ident, att_d):
    UN = NBLK * HG
    with ExitStack() as ctx:
        t_ = Tools(nc, ctx, "att")
        hc = t_.sb("hc", [P, KD, CH])
        w = [t_.sb(f"w{n}", [P, KD, AW]) for n in "qkv"]
        qT = t_.sb("qT", [P, NFT, CH])
        kT = t_.sb("kT", [P, NFT, P + CH])
        v = t_.sb("v", [P, 1 + NBLK, AW])
        same = t_.sb("same", [P, P])
        gains = [t_.sb(f"gain{n}", [P, len(GROUPS)]) for n in "qk"]
        eps = t_.sb("eps", [P, 1])
        tick = t_.sem("tick")
        rt = [t_.sb(f"rt{z}", [P, CH]) for z in range(2)]
        sc = [t_.sb(f"sc{z}", [P, 2 * P]) for z in range(3)]
        probs = t_.sb("probs", [P, 4 * 2 * P])
        pp = [probs[:, z * 2 * P:(z + 1) * 2 * P] for z in range(4)]
        sq = [probs[:, z * CH:(z + 1) * CH] for z in range(2)]
        ppT = [t_.sb(f"ppT{z}", [P, 2 * P]) for z in range(3)]
        ao = [t_.sb(f"ao{z}", [P, HG, RW]) for z in range(NBLK)]
        bank = [t_.ps(f"b{n}") for n in range(8)]
        gm, ssq, tb, ob = (bank[0], bank[1], bank[3], bank[4]), bank[2], bank[4:6], bank[6:8]
        vb = (bank[0], bank[1], bank[3], bank[7])
        sb = (bank[2], bank[0], bank[1], bank[3])
        w_sem = [t_.sem(f"w_in_{n}") for n in "qkv"]
        ao_out = [t_.sem(f"ao_out{z}") for z in range(NBLK)]
        (gain_in, const, gain_ready, hc_ready, qk_mm, v_mm, qk_done, v_done, sq_ready, ssq_ready, root_ready, rec,
         s_ready, s_read, p_ready, t_ready, pt_ready, pv_done, o_saved) = t_.sems(
            "gain_in const gain_ready hc_ready qk_mm v_mm qk_done v_done sq_ready ssq_ready root_ready rec "
            "s_ready s_read p_ready t_ready pt_ready pv_done o_saved")

        def chunks(eng, g, body):
            first = g == 0
            if first:
                body(g, 0, 0, True)
            with eng.Fori(1 if first else 0, NCH) as c:
                body(g, c, c + NCH * g, False)

        def alone(g, b, opening):
            return g == 2 or (b == 0 and (g == 1 or opening))

        def in_group_order(ap, g, c):
            d = GROUPS[g][1]
            if d == 1:
                return ap[:, :, ds(c * CH, CH)].rearrange("p k (r a) -> p k r a", r=1)
            n = d // NCH
            return ap.rearrange("p k (a r) -> p k r a", r=d)[:, :, ds(c * n, n), :]

        def block_rows(g, c, b):
            rows = att_d[g]
            if g == 0:
                return rows[ds(c * CH + b * P, P), :]
            d = GROUPS[g][1]
            r, a = (c, b) if g == 1 else (c * NBLK + b, 0)
            return rows.rearrange("(a r) w -> r a w", r=d)[ds(r, 1), a * P:(a + 1) * P, :].rearrange("o a w -> (o a) w")

        with nc.Block() as block:
            @block.sync
            def _(sp):
                for h in range(2):
                    for dst, src in zip(gains, (q_gain, k_gain)):
                        sp.dma_start(dst[DH * h:DH * (h + 1), :], src).then_inc(gain_in, 16)
                def load(g, i):
                    col = (i * len(GROUPS) + g) * AW
                    sp.dma_start(w[i][:, :, :], w_in[:, col:col + AW].rearrange("(k p) n -> p k n", p=P)).then_inc(
                        w_sem[i], 16)

                def chunk(g, c, n, opening):
                    for b in range(NBLK):
                        sp.wait_ge(o_saved, NBLK * n + b + 1)
                        sp.dma_start(block_rows(g, c, b), ao[b][:, :, :].rearrange("p h w -> p (h w)")).then_inc(
                            ao_out[b], 16)

                for i in range(3):
                    load(0, i)
                chunk(0, 0, 0, True)
                for g in range(len(GROUPS)):
                    with sp.Fori(1 if g == 0 else 0, NCH - 1) as c:
                        chunk(g, c, c + NCH * g, False)
                    if g + 1 < len(GROUPS):
                        for i in range(2):
                            sp.wait_ge(qk_mm, 2 * NFT * (NCH * (g + 1) - 1) + NFT * (i + 1))
                            load(g + 1, i)
                        sp.wait_ge(v_mm, NBLK * NCH * (g + 1))
                        load(g + 1, 2)
                    chunk(g, NCH - 1, NCH * g + NCH - 1, False)
                for z in range(NBLK):
                    sp.wait_ge(ao_out[z], 16 * NCH * len(GROUPS))

            @block.gpsimd
            def _(pool):
                pool.memset(same[:, :], 0.0).then_inc(const, 1)
                pool.memset(eps[:, :], EPS).then_inc(const, 1)
                pool.wait_ge(const, 2)
                for h in range(2):
                    pool.memset(same[DH * h:DH * (h + 1), DH * h:DH * (h + 1)], 1.0).then_inc(const, 1)

                pool.wait_ge(const, 4)

                def stage(g, c, n, opening):
                    if not opening:
                        pool.wait_ge(v_mm, NBLK * n)
                    src = in_group_order(hT[:, :, :], g, c)
                    pool.tensor_copy(hc[:, :, :].rearrange("p k (r a) -> p k r a", r=src.shape[2]),
                                     src).then_inc(hc_ready, 1)
                for g in range(len(GROUPS)):
                    chunks(pool, g, stage)

            @block.tensor
            def _(pe):
                pe.wait_ge(const, 4)

                def chunk(g, c, n, opening):
                    pe.wait_ge(hc_ready, n + 1)
                    if not opening:
                        pe.wait_ge(s_read, UN * n)

                    def square_sums(t):
                        pe.wait_ge(sq_ready, 2 * NFT * n + t + 1)
                        if t or not opening:
                            pe.wait_ge(root_ready, 2 * NFT * n + t)
                        pe.matmul(ssq[:, :], same[:, :], sq[t % 2][:, :], start=True, stop=True).then_inc(ssq_ready, 1)

                    for t in range(2 * NFT):
                        i, f = divmod(t, NFT)
                        if f == 0:
                            pe.wait_ge(w_sem[i], 16 * g + 16)
                        if t >= 4:
                            pe.wait_ge(qk_done, 2 * NFT * n + t - 3)
                        for k in range(KD):
                            last = pe.matmul(gm[t % 4][:, :], w[i][:, k, f * P:(f + 1) * P], hc[:, k, :],
                                             start=(k == 0), stop=(k == KD - 1))
                        last.then_inc(qk_mm, 1)
                        if t:
                            square_sums(t - 1)
                    pe.wait_ge(w_sem[2], 16 * g + 16)

                    def scores(u):
                        b, h = divmod(u, HG)
                        off, rows = (P if alone(g, b, opening) else 0), slice(DH * (h % 2), DH * (h % 2) + DH)
                        pe.matmul(sb[u % 4][:, off:2 * P], qT[rows, h // 2, b * P:(b + 1) * P],
                                  kT[rows, h // 2, b * P + off:(b + 2) * P], start=True, stop=True).then_inc(s_ready, 1)

                    for b in range(NBLK):
                        if b < 3:
                            pe.wait_ge(qk_done, 2 * NFT * n + 2 * NFT - 3 + b)
                        else:
                            pe.wait_ge(qk_done, 2 * NFT * (n + 1))
                            scores(0)
                            pe.wait_ge(v_done, NBLK * n + 1)
                            scores(1)
                            if not opening:
                                pe.wait_ge(o_saved, NBLK * n)
                        for k in range(KD):
                            last = pe.matmul(vb[b][:, :], hc[:, k, b * P:(b + 1) * P], w[2][:, k, :],
                                             start=(k == 0), stop=(k == KD - 1))
                        last.then_inc(v_mm, 1)
                        if b == 0:
                            square_sums(2 * NFT - 1)

                    for step in range(2, UN + 5):
                        if step < UN:
                            if step < 4:
                                pe.wait_ge(v_done, NBLK * n + step)
                            else:
                                pe.wait_ge(s_read, UN * n + step - 3)
                            scores(step)
                        u = step - 3
                        if 0 <= u < UN:
                            b, h = divmod(u, HG)
                            pe.wait_ge(p_ready, UN * n + u + 1)
                            if u >= 2 or not opening:
                                pe.wait_ge(pt_ready, UN * n + u - 1)
                            for k in range(1 if alone(g, b, opening) else 0, 2):
                                last = pe.transpose(tb[u % 2][:, k * P:(k + 1) * P], pp[u % 4][:, k * P:(k + 1) * P],
                                                    ident[:, :])
                            last.then_inc(t_ready, 1)
                        u = step - 5
                        if 0 <= u < UN:
                            b, h = divmod(u, HG)
                            pe.wait_ge(pt_ready, UN * n + u + 1)
                            if u == 0:
                                pe.wait_ge(v_done, NBLK * n + NBLK)
                            if h == 0 and (b >= 2 or not opening):
                                pe.wait_ge(o_saved, NBLK * n + b - 1)
                            k0 = 1 if alone(g, b, opening) else 0
                            for k in range(k0, 2):
                                last = pe.matmul(ob[b % 2][:, h * DH:(h + 1) * DH], ppT[u % 3][:, k * P:(k + 1) * P],
                                                 v[:, b + k, h * DH:(h + 1) * DH], start=(k == k0), stop=(k == 1))
                            last.then_inc(pv_done, 1)
                for g in range(len(GROUPS)):
                    chunks(pe, g, chunk)

            @block.scalar
            def _(act):
                act.wait_ge(const, 4)

                def chunk(g, c, n, opening):
                    def root(t):
                        act.wait_ge(ssq_ready, 2 * NFT * n + t + 1)
                        if t >= 2 or not opening:
                            act.wait_ge(qk_done, 2 * NFT * n + t - 1)
                        act.activation(rt[t % 2][:, :], ssq[:, :], ACT.Sqrt, bias=eps[:, :],
                                       scale=1.0 / DH).then_inc(root_ready, 1)

                    for t in range(2 * NFT):
                        act.wait_ge(qk_mm, 2 * NFT * n + t + 1)
                        act.activation(sq[t % 2][:, :], gm[t % 4][:, :], ACT.Square).then_inc(sq_ready, 1)
                        if t:
                            root(t - 1)
                    root(2 * NFT - 1)
                    if g == 0 and not opening:
                        act.wait_ge(pv_done, UN * n)
                        act.activation(v[:, 0, :], v[:, NBLK, :], ACT.Copy).then_inc(gain_ready, 1)
                        act.wait_ge(gain_ready, n + 1)
                    for b in range(NBLK):
                        act.wait_ge(v_mm, NBLK * n + b + 1)
                        if b == 0 and not opening:
                            act.wait_ge(pv_done, UN * n)
                        act.activation(v[:, 1 + b, :], vb[b][:, :], ACT.Copy).then_inc(v_done, 1)

                    def save(b):
                        act.wait_ge(pv_done, UN * n + HG * (b + 1))
                        act.activation(ao[b][:, :, 0:DH], ob[b % 2][:, :].rearrange("p (h d) -> p h d", h=HG),
                                       ACT.Copy).then_inc(o_saved, 1)

                    for u in range(UN):
                        b, h = divmod(u, HG)
                        off = P if alone(g, b, opening) else 0
                        act.wait_ge(s_read, UN * n + u + 1)
                        if u >= 4 or not opening:
                            act.wait_ge(t_ready, UN * n + u - 3)
                        act.activation(pp[u % 4][:, off:2 * P], sc[u % 3][:, off:2 * P], ACT.Exp,
                                       bias=ao[b][:, h, DH:DH + 1], scale=-1.0,
                                       accum_out=ao[b][:, h, DH + 1:DH + 2]).then_inc(p_ready, 1)
                        if h == 5 and b:
                            save(b - 1)
                    save(NBLK - 1)
                for g in range(len(GROUPS)):
                    chunks(act, g, chunk)

            @block.vector
            def _(dve):
                dve.wait_ge(gain_in, 64)
                dve.tensor_scalar(gains[0][:, :], gains[0][:, :], -(DH ** -0.5), None, ALU.mult).then_inc(gain_ready, 1)
                dve.wait_ge(gain_ready, 1)

                def chunk(g, c, n, opening):
                    if not opening:
                        dve.wait_ge(s_ready, UN * n)
                    if g == 0 and not opening:
                        dve.tensor_copy(kT[:, :, 0:P], kT[:, :, CH:CH + P]).then_inc(rec, 1)
                        dve.wait_ge(rec, (2 * NFT + 1) * n)
                    kept = n if g == 0 else NCH - 1
                    for t in range(2 * NFT):
                        i, f = divmod(t, NFT)
                        dve.wait_ge(root_ready, 2 * NFT * n + t + 1)
                        dve.reciprocal(rt[t % 2][:, :], rt[t % 2][:, :]).then_inc(rec, 1)
                        dve.wait_ge(rec, 2 * NFT * n + kept + t + 1)
                        dst = qT[:, f, :] if i == 0 else kT[:, f, P:P + CH]
                        dve.scalar_tensor_tensor(dst, gm[t % 4][:, :], gains[i][:, g:g + 1], rt[t % 2][:, :], ALU.mult,
                                                 ALU.mult).then_inc(qk_done, 1)
                    for step in range(UN + 3):
                        u = step
                        if u < UN:
                            b, h = divmod(u, HG)
                            off = P if alone(g, b, opening) else 0
                            dve.wait_ge(s_ready, UN * n + u + 1)
                            if u >= 3 or not opening:
                                dve.wait_ge(p_ready, UN * n + u - 2)
                            if h == 0 and not opening:
                                dve.wait_ge(ao_out[b], 16 * n)
                            dve.sem_inc(tick, 1)
                            dve.tensor_tensor_reduce(sc[u % 3][:, off:2 * P], sb[u % 4][:, off:2 * P],
                                                     bias[:, HG * g + h, off:2 * P], 1.0, MASKED, ALU.add, ALU.min,
                                                     ao[b][:, h, DH:DH + 1]).then_inc(s_read, 1)
                        u = step - 3
                        if 0 <= u < UN:
                            b = u // HG
                            off = P if alone(g, b, opening) else 0
                            dve.wait_ge(t_ready, UN * n + u + 1)
                            if u >= 3 or not opening:
                                dve.wait_ge(pv_done, UN * n + u - 2)
                            dve.tensor_copy(ppT[u % 3][:, off:2 * P], tb[u % 2][:, off:2 * P]).then_inc(pt_ready, 1)
                for g in range(len(GROUPS)):
                    chunks(dve, g, chunk)



def combine(nc, att_d, ident, attT_d):
    with ExitStack() as ctx:
        t_ = Tools(nc, ctx, "cmb")
        NG = len(GROUPS)
        a = [[t_.sb(f"a{z}{g}", [P, HG, RW]) for g in range(NG)] for z in range(2)]
        low, den, rden = (t_.sb(n, [P, HG]) for n in ("low", "den", "rden"))
        dif, wgt, part = (t_.sb(n, [P, NG, HG]) for n in ("dif", "wgt", "part"))
        mix = [t_.sb(f"mix{z}", [P, AW]) for z in range(2)]
        m1, m2 = (t_.sb(n, [P, AW]) for n in ("m1", "m2"))
        aT = t_.sb("aT", [P, NFT, S])
        pt = [t_.ps(f"pt{z}") for z in range(2)]
        a_in = [t_.sem(f"a_in{z}") for z in range(2)]
        step, added, dif_ready, w_ready, mixed, turned, saved, stored = t_.sems(
            "step added dif_ready w_ready mixed turned saved stored")
        with nc.Block() as block:
            @block.sync
            def _(sp):
                with sp.Fori(0, NT // 2) as i:
                    for z in range(2):
                        sp.wait_ge(mixed, 2 * i + z + 1)
                        for g in range(NG):
                            sp.dma_start(a[z][g][:, :, :].rearrange("p h w -> p (h w)"),
                                         att_d[g, ds(i * (2 * P) + z * P, P), :]).then_inc(a_in[z], 16)
                sp.wait_ge(saved, NT + 2)
                sp.dma_start(attT_d, aT[:, :, :]).then_inc(stored, 16)
                sp.wait_ge(stored, 16)

            @block.vector
            def _(dve):
                dve.sem_inc(mixed, 2)
                tt = dve.tensor_tensor
                PER = 8
                with dve.Fori(0, NT // 2) as i:
                    chain = Steps(dve, step, 2 * PER * i)
                    for z in range(2):
                        dve.wait_ge(a_in[z], 16 * NG * i + 16 * NG)
                        m = [x[:, :, DH] for x in a[z]]
                        chain(tt(low[:, :], m[0], m[1], ALU.min))
                        chain(tt(low[:, :], low[:, :], m[2], ALU.min))
                        for g in range(NG):
                            last = tt(dif[:, g, :], low[:, :], m[g], ALU.subtract)
                        last.then_inc(dif_ready, 1)
                        dve.wait_ge(w_ready, 2 * i + z + 1)
                        for g in range(NG):
                            last = tt(part[:, g, :], wgt[:, g, :], a[z][g][:, :, DH + 1], ALU.mult)
                        chain(last)
                        chain(tt(den[:, :], part[:, 0, :], part[:, 1, :], ALU.add))
                        chain(tt(den[:, :], den[:, :], part[:, 2, :], ALU.add))
                        chain(dve.reciprocal(rden[:, :], den[:, :]))
                        chain(tt(part[:, :, :], wgt[:, :, :], rden[:, :].unsqueeze(1).to_broadcast([P, NG, HG]), ALU.mult))
                        out = mix[z][:, :].rearrange("p (h d) -> p h d", h=HG)
                        view = [x[:, :].rearrange("p (h d) -> p h d", h=HG) for x in (m1, m2)]

                        def weighted(dst, g):
                            return tt(dst, a[z][g][:, :, 0:DH], part[:, g, :].unsqueeze(2).to_broadcast([P, HG, DH]),
                                      ALU.mult)
                        weighted(view[0], 0)
                        weighted(view[1], 1)
                        dve.wait_ge(turned, 2 * i + z + 1)
                        chain(weighted(out, 2))
                        tt(m1[:, :], m1[:, :], m2[:, :], ALU.add).then_inc(added, 1)
                        dve.wait_ge(added, 2 * i + z + 1)
                        tt(mix[z][:, :], mix[z][:, :], m1[:, :], ALU.add).then_inc(mixed, 1)
                        dve.wait_ge(mixed, 2 * i + z + 3)
                    assert chain.n == 2 * PER

            @block.scalar
            def _(act):
                act.sem_inc(saved, 2)
                with act.Fori(0, NT // 2) as i:
                    for z in range(2):
                        act.wait_ge(dif_ready, 2 * i + z + 1)
                        act.activation(wgt[:, :, :], dif[:, :, :], ACT.Exp).then_inc(w_ready, 1)
                        act.wait_ge(turned, 2 * i + z + 3)
                        act.activation(aT[:, :, ds(i * (2 * P) + z * P, P)],
                                       pt[z][:, :].rearrange("p (f n) -> p f n", f=NFT), ACT.Copy).then_inc(saved, 1)

            @block.tensor
            def _(pe):
                pe.sem_inc(turned, 2)
                with pe.Fori(0, NT // 2) as i:
                    for z in range(2):
                        pe.wait_ge(mixed, 2 * i + z + 3)
                        pe.wait_ge(saved, 2 * i + z + 1)
                        for f in range(NFT):
                            last = pe.transpose(pt[z][:, f * P:(f + 1) * P], mix[z][:, f * P:(f + 1) * P], ident[:, :])
                        last.then_inc(turned, 1)



def mix(nc, hT, yT_d, attT_d, w_glu, b_glu, w_tiles, mixed_d):
    KA = AW // P
    KW = 2 * KD + 2 * KA
    NO = D // P
    with ExitStack() as ctx:
        t_ = Tools(nc, ctx, "mix")
        glu = t_.sb("glu", [P, KA, SW])
        bg = t_.sb("bg", [P, KA])
        w = [t_.sb(f"w{z}", [P, KW, P]) for z in range(2)]
        at, y, sg, y2 = (t_.sb(n, [P, KA, CH]) for n in ("at", "y", "sg", "y2"))
        ga, gb, ta, tb = ([t_.sb(f"{n}{z}", [P, CH]) for z in range(2)] for n in ("ga", "gb", "ta", "tb"))
        mx = t_.sb("mx", [P, NO, CH])
        bank = [t_.ps(f"b{n}") for n in range(8)]
        pg = bank[4:8]
        w_sem = [t_.sem(f"w_in{z}") for z in range(2)]
        (glu_in, at_in, y_in, glu_mm, sig, y2_ready, mm, gates, m_a, m_b, mx_ready, mx_out) = t_.sems(
            "glu_in at_in y_in glu_mm sig y2_ready mm gates m_a m_b mx_ready mx_out")
        with nc.Block() as block:
            @block.sync
            def _(sp):
                sp.dma_start(glu[:, :, :], w_glu).then_inc(glu_in, 16)
                sp.dma_start(bg[:, :], b_glu).then_inc(glu_in, 16)
                with sp.Fori(0, NCH) as c:
                    sp.wait_ge(y2_ready, c * KA + 1)
                    sp.dma_start(y[:, :, :], yT_d[:, :, ds(c * CH, CH)]).then_inc(y_in, 16)
                    for o in range(NO):
                        sp.wait_ge(mm, c * (4 * NO) + 4 * o + 4)
                        sp.dma_start(w[o % 2][:, :, :], w_tiles[o]).then_inc(w_sem[o % 2], 16)
                        if o == 0:
                            sp.wait_ge(mm, c * (4 * NO) + 8)
                            sp.dma_start(at[:, :, :], attT_d[:, :, ds(c * CH, CH)]).then_inc(at_in, 16)
                sp.wait_ge(mx_out, 16 * NCH)

            @block.tensor
            def _(pe):
                pe.sem_inc(mm, 8)
                pe.wait_ge(glu_in, 32)
                with pe.Fori(0, NCH) as c:
                    pe.wait_ge(y_in, 16 * c + 16)
                    for f in range(KA):
                        pe.wait_ge(y2_ready, c * KA + 1)
                        for k in range(KA):
                            last = pe.matmul(pg[f][:, :], glu[:, k, f * P:(f + 1) * P], y[:, k, :], start=(k == 0),
                                             stop=(k == KA - 1))
                        last.then_inc(glu_mm, 1)
                    pe.wait_ge(at_in, 16 * c + 16)
                    for o in range(NO):
                        z = o % 2
                        t = c * NO + o
                        pe.wait_ge(w_sem[z], c * (16 * NO // 2) + 16 * (o // 2) + 16)
                        pe.wait_ge(gates, 2 * t + 1)
                        for j in range(2):
                            for k in range(KD):
                                last = pe.matmul(bank[j][:, :], w[z][:, j * KD + k, :], hT[:, k, ds(c * CH, CH)],
                                                 start=(k == 0), stop=(k == KD - 1))
                            last.then_inc(mm, 1)
                        if o == 0:
                            pe.wait_ge(y2_ready, c * KA + KA + 1)
                        pe.wait_ge(m_b, t + 2)
                        for j, src in enumerate((at, y2)):
                            for k in range(KA):
                                last = pe.matmul(bank[2 + j][:, :], w[z][:, 2 * KD + j * KA + k, :], src[:, k, :],
                                                 start=(k == 0), stop=(k == KA - 1))
                            last.then_inc(mm, 1)

            @block.scalar
            def _(act):
                act.sem_inc(gates, 1)
                act.wait_ge(glu_in, 32)
                with act.Fori(0, NCH) as c:
                    for f in range(KA):
                        act.wait_ge(glu_mm, c * KA + f + 1)
                        act.activation(sg[:, f, :], pg[f][:, :], ACT.Sigmoid, bias=bg[:, f:f + 1]).then_inc(sig, 1)
                    for o in range(NO):
                        t = c * NO + o
                        for j, dst in enumerate((ga, gb)):
                            act.wait_ge(mm, 4 * t + 8 + j + 1)
                            act.wait_ge(m_b, t + 1)
                            act.activation(dst[o % 2][:, :], bank[j][:, :], ACT.Sigmoid).then_inc(gates, 1)

            @block.vector
            def _(dve):
                dve.sem_inc(m_b, 2)
                dve.sem_inc(y2_ready, 1)
                with dve.Fori(0, NCH) as c:
                    for f in range(KA):
                        dve.wait_ge(sig, c * KA + f + 1)
                        dve.wait_ge(mm, c * (4 * NO) + 8)
                        dve.tensor_tensor(y2[:, f, :], y[:, f, :], sg[:, f, :], ALU.mult).then_inc(y2_ready, 1)
                    for o in range(NO):
                        t = c * NO + o
                        z = o % 2
                        dve.wait_ge(gates, 2 * t + 3)
                        dve.wait_ge(mm, 4 * t + 8 + 4)
                        dve.wait_ge(mx_ready, t + 1)
                        dve.tensor_tensor(ta[z][:, :], bank[2][:, :], ga[z][:, :], ALU.mult).then_inc(m_a, 1)
                        dve.tensor_tensor(tb[z][:, :], bank[3][:, :], gb[z][:, :], ALU.mult).then_inc(m_b, 1)

            @block.gpsimd
            def _(pool):
                pool.sem_inc(mx_ready, 2)
                with pool.Fori(0, NCH) as c:
                    for o in range(NO):
                        t = c * NO + o
                        pool.wait_ge(m_b, t + 3)
                        pool.tensor_tensor(mx[:, o, :], ta[o % 2][:, :], tb[o % 2][:, :], ALU.add).then_inc(mx_ready, 1)
                    pool.wait_ge(mx_ready, c * NO + NO + 2)
                    pool.dma_start(mixed_d[:, :, ds(c * CH, CH)], mx[:, :, :]).then_inc(mx_out, 16)
                    pool.wait_ge(mx_out, 16 * c + 16)


def route(nc, x, mixed_d, w_out, g_row, w_router, b_router, empty_slots, ident, upper, ones, acc_d, h2_d, slots_d,
          table_d):
    with ExitStack() as ctx:
        t_ = Tools(nc, ctx, "rt")
        w = t_.sb("w", [P, KD, D])
        gb = t_.sb("gb", [P, D])
        wr = t_.sb("wr", [P, KD, NE])
        br = t_.sb("br", [1, NE])
        xt, mt, x1, h2 = ([t_.sb(f"{n}{z}", [P, D]) for z in range(2)] for n in ("x", "m", "x1", "h2"))
        h2T = t_.sb("h2T", [P, KD, P])
        zero = t_.sb("zero", [P, D])
        junk = t_.sb("junk", [P, D])
        ss, ms, rms, rstd, top, nbest, esum, resum, tok = (t_.sb(n, [P, 1]) for n in (
            "ss", "ms", "rms", "rstd", "top", "nbest", "esum", "resum", "tok"))
        lg, mask, chosen = (t_.sb(n, [P, NE]) for n in ("lg", "mask", "chosen"))
        v8 = t_.sb("v8", [P, 8])
        i8 = t_.sb("i8", [P, 8], U32)
        idx, ex, rsel, slot = (t_.sb(n, [P, TOPK]) for n in ("idx", "ex", "rsel", "slot"))
        ecol = t_.sb("ecol", [P, NE])
        hot, rk = (t_.sb(n, [P, TOPK, NE]) for n in ("hot", "rk"))
        slot_i = [t_.sb(f"slot_i{z}", [P, TOPK], U32) for z in range(2)]
        pay = [t_.sb(f"pay{z}", [P, TOPK, 2], I32) for z in range(2)]
        cnt, full, part, upto, before = (t_.sb(n, [P, NE]) for n in ("cnt", "full", "part", "upto", "before"))
        row, ei, nth = (t_.sb(n, [P, 1]) for n in ("row", "ei", "nth"))
        tab = t_.sb("tab", [P, 2, 4])
        tab_i = t_.sb("tab_i", [P, 2, 4], I32)
        po = [[t_.ps(f"o{z}{h}") for h in range(2)] for z in range(2)]
        pt = [t_.ps(f"t{h}") for h in range(2)]
        pl, pr = t_.ps("l"), t_.ps("r")
        x_in = [t_.sem(f"x_in{z}") for z in range(2)]
        x1_out = [t_.sem(f"x1_out{z}") for z in range(2)]
        h2_out = [t_.sem(f"h2_out{z}") for z in range(2)]
        tick = t_.sem("tick")
        (c_in, pre, pad_out, iot, mm, x1_ready, step, ms_ready, rms_ready, h2_ready, turned, h2T_ready, lg_mm, ex_in,
         ex_ready, mask_ready, rank_mm, rank_read, pay_ready, pay_free, sc_out, cnt_mm, fin, tab_out) = t_.sems(
            "c_in pre pad_out iot mm x1_ready step ms_ready rms_ready h2_ready turned h2T_ready lg_mm ex_in "
            "ex_ready mask_ready rank_mm rank_read pay_ready pay_free sc_out cnt_mm fin tab_out")
        rows = lambda ap, t: ap[ds(t * P, P), :]
        with nc.Block() as block:
            @block.sync
            def _(sp):
                sp.dma_start(w[:, :, :], w_out).then_inc(c_in, 16)
                sp.dma_start(gb[:, :], on_rows(g_row, P)).then_inc(c_in, 16)
                sp.dma_start(wr[:, :, :], w_router).then_inc(c_in, 16)
                sp.dma_start(br[:, :], on_rows(b_router, 1)).then_inc(c_in, 16)
                sp.dma_start(slots_d, empty_slots).then_inc(pre, 16)
                with sp.Fori(0, NT // 2) as i:
                    for z in range(2):
                        t = 2 * i + z
                        sp.wait_ge(h2_ready, t + 1)
                        sp.dma_start(xt[z][:, :], rows(x, t)).then_inc(x_in[z], 16)
                        sp.dma_start(mt[z][:, :].rearrange("p (k n) -> p k n", k=KD),
                                     mixed_d[:, :, ds(t * P, P)]).then_inc(x_in[z], 16)

            @block.scalar
            def _(act):
                act.sem_inc(h2T_ready, 2)
                for z in range(2):
                    act.sem_inc(x1_out[z], 16)
                    act.sem_inc(h2_out[z], 16)
                act.wait_ge(pad_out, 1)
                for g in range(NGT):
                    act.dma_start(h2_d[S + g * P:S + (g + 1) * P, :], zero[:, :]).then_inc(pre, 16)
                    act.dma_start(acc_d[S + g * P:S + (g + 1) * P, :], zero[:, :]).then_inc(pre, 16)

                def tile(t, z):
                    act.wait_ge(ms_ready, t + 1)
                    act.activation(rms[:, :], ms[:, :], ACT.Sqrt).then_inc(rms_ready, 1)
                    act.dma_start(rows(acc_d, t), x1[z][:, :]).then_inc(x1_out[z], 16)
                    act.wait_ge(h2_ready, t + 3)
                    act.dma_start(rows(h2_d, t), h2[z][:, :]).then_inc(h2_out[z], 16)
                    for h in range(2):
                        act.wait_ge(turned, 2 * t + h + 3)
                        if h == 0:
                            act.wait_ge(lg_mm, t + 1)
                        act.activation(h2T[:, 4 * h:4 * h + 4, :], pt[h][:, :].rearrange("p (k n) -> p k n", k=4),
                                       ACT.Copy).then_inc(h2T_ready, 1)
                    act.wait_ge(ex_in, t + 2)
                    act.activation(ex[:, :], v8[:, 0:TOPK], ACT.Exp, bias=nbest[:, :],
                                   accum_out=esum[:, :]).then_inc(ex_ready, 1)
                with act.Fori(0, NT // 2) as i:
                    for z in range(2):
                        tile(2 * i + z, z)
                for z in range(2):
                    act.wait_ge(x1_out[z], 16 * (NT // 2) + 16)
                    act.wait_ge(h2_out[z], 16 * (NT // 2) + 16)
                act.wait_ge(fin, 1)
                act.dma_start(table_d.rearrange("k p c -> p k c"), tab_i[:, :, :]).then_inc(tab_out, 16)
                act.wait_ge(tab_out, 16)

            @block.tensor
            def _(pe):
                pe.sem_inc(lg_mm, 1)
                pe.sem_inc(turned, 2)
                pe.wait_ge(c_in, 64)

                def project(t, z):
                    pe.wait_ge(x_in[z], (t - z) * 16 + 32)
                    pe.wait_ge(x1_ready, 2 * t + 2)
                    for h in range(2):
                        for k in range(KD):
                            last = pe.matmul(po[z][h][:, :], mt[z][:, k * P:(k + 1) * P], w[:, k, h * 512:(h + 1) * 512],
                                             start=(k == 0), stop=(k == KD - 1))
                        last.then_inc(mm, 1)

                def choose(t, z):
                    pe.wait_ge(h2_ready, t + 3)
                    for h in range(2):
                        if h == 0:
                            pe.wait_ge(h2T_ready, 2 * t + 2)
                        for k in range(4):
                            last = pe.transpose(pt[h][:, k * P:(k + 1) * P],
                                                h2[z][:, (4 * h + k) * P:(4 * h + k + 1) * P], ident[:, :])
                        last.then_inc(turned, 1)
                    pe.wait_ge(h2T_ready, 2 * t + 4)
                    pe.wait_ge(ex_in, t + 1)
                    for k in range(KD):
                        pe.matmul(pl[:, 0:NE], h2T[:, k, :], wr[:, k, :], start=(k == 0), stop=False)
                    pe.matmul(pl[:, 0:NE], ones[0:1, :], br[:, :], start=False, stop=True).then_inc(lg_mm, 1)
                    pe.wait_ge(mask_ready, t + 1)
                    pe.matmul(pr[:, 0:NE], upper[:, :], mask[:, :], start=True, stop=False)
                    pe.matmul(pr[:, 0:NE], ones[:, :], chosen[:, :], start=False, stop=True).then_inc(rank_mm, 1)

                project(0, 0)
                with pe.Fori(0, NT // 2 - 1) as i:
                    project(2 * i + 1, 1)
                    choose(2 * i, 0)
                    project(2 * i + 2, 0)
                    choose(2 * i + 1, 1)
                project(NT - 1, 1)
                choose(NT - 2, 0)
                choose(NT - 1, 1)
                pe.wait_ge(rank_read, NT)
                pe.matmul(pr[:, 0:NE], ones[:, :], chosen[:, :], start=True, stop=True).then_inc(cnt_mm, 1)

            @block.gpsimd
            def _(pool):
                pool.sem_inc(pay_free, 2)
                pool.memset(zero[:, :], 0.0).then_inc(pad_out, 1)
                pool.iota(ecol[:, :], [[1, NE]], base=0, channel_multiplier=0,
                          allow_small_or_imprecise_dtypes=True).then_inc(iot, 1)
                pool.iota(tok[:, :], [[1, 1]], base=0, channel_multiplier=1,
                          allow_small_or_imprecise_dtypes=True).then_inc(iot, 1)
                pool.iota(row[:, :], [[1, 1]], base=0, channel_multiplier=1,
                          allow_small_or_imprecise_dtypes=True).then_inc(iot, 1)
                pool.wait_ge(pre, 16 + 32 * NGT)
                with pool.Fori(0, NT // 2) as i:
                    for z in range(2):
                        stop_until(pool, pay_ready, 2 * i + z + 1, tick)
                        for s in range(TOPK):
                            pool.indirect_dma_start(
                                out=slots_d, out_offset=bass.IndirectOffsetOnAxis(ap=slot_i[z][:, s:s + 1], axis=0),
                                in_=pay[z][:, s, :], in_offset=None).then_inc(sc_out, 16)
                        pool.wait_ge(sc_out, 16 * TOPK * (2 * i + z + 1))
                        pool.sem_inc(pay_free, 1)

            @block.vector
            def _(dve):
                tt, tsc, stt = dve.tensor_tensor, dve.tensor_scalar, dve.scalar_tensor_tensor
                dve.sem_inc(x1_ready, 4)
                dve.sem_inc(h2_ready, 2)
                dve.sem_inc(ex_in, 1)
                dve.memset(chosen[:, :], 0.0)
                dve.wait_ge(c_in, 64)
                dve.wait_ge(iot, 3)
                PER = 13

                def tile(t, z, i):
                    chain = Steps(dve, step, PER * t)
                    dve.wait_ge(x1_out[z], 16 * i + 16)
                    dve.wait_ge(h2_out[z], 16 * i + 16)
                    dve.wait_ge(x_in[z], 32 * i + 32)
                    for h in range(2):
                        dve.wait_ge(mm, 2 * t + h + 1)
                        tt(x1[z][:, h * 512:(h + 1) * 512], po[z][h][:, :], xt[z][:, h * 512:(h + 1) * 512],
                           ALU.add).then_inc(x1_ready, 1)
                    dve.wait_ge(x1_ready, 2 * t + 6)
                    chain(dve.tensor_tensor_reduce(junk[:, :], x1[z][:, :], x1[z][:, :], 1.0, 0.0, ALU.mult, ALU.add,
                                                   ss[:, :]))
                    tsc(ms[:, :], ss[:, :], 1.0 / D, EPS, ALU.mult, ALU.add).then_inc(ms_ready, 1)
                    dve.wait_ge(rms_ready, t + 1)
                    chain(dve.reciprocal(rstd[:, :], rms[:, :]))
                    dve.wait_ge(turned, 2 * t + 2)
                    stt(h2[z][:, :], x1[z][:, :], rstd[:, :], gb[:, :], ALU.mult, ALU.mult).then_inc(h2_ready, 1)
                    dve.wait_ge(lg_mm, t + 2)
                    chain(dve.tensor_copy(lg[:, :], pl[:, 0:NE]))
                    dve.sem_inc(tick, 1)
                    chain(dve.max(v8[:, :], lg[:, :]))
                    dve.sem_inc(tick, 1)
                    dve.max_index(i8[:, :], v8[:, :], lg[:, :])
                    tsc(nbest[:, :], v8[:, 0:1], -1.0, None, ALU.mult).then_inc(ex_in, 1)
                    dve.wait_ge(ex_in, t + 2)
                    chain(dve.tensor_copy(idx[:, :], i8[:, 0:TOPK]))
                    chain(tt(hot[:, :, :], ecol[:, :].unsqueeze(1).to_broadcast([P, TOPK, NE]),
                             idx[:, :].unsqueeze(2).to_broadcast([P, TOPK, NE]), ALU.is_equal))
                    dve.tensor_reduce(mask[:, :], hot[:, :, :].rearrange("p s e -> p e s"), AX.X,
                                      ALU.add).then_inc(mask_ready, 1)
                    dve.wait_ge(ex_ready, t + 1)
                    chain(dve.reciprocal(resum[:, :], esum[:, :]))
                    dve.wait_ge(pay_free, t + 1)
                    chain(tsc(pay[z][:, :, 1].bitcast(F32), ex[:, :], resum[:, :], None, ALU.mult))
                    chain(dve.tensor_copy(pay[z][:, :, 0], tok[:, :].to_broadcast([P, TOPK])))
                    dve.wait_ge(rank_mm, t + 1)
                    chain(tt(rk[:, :, :], hot[:, :, :], pr[:, 0:NE].unsqueeze(1).to_broadcast([P, TOPK, NE]), ALU.mult))
                    tt(chosen[:, :], chosen[:, :], mask[:, :], ALU.add).then_inc(rank_read, 1)
                    chain(dve.tensor_reduce(rsel[:, :], rk[:, :, :], AX.X, ALU.add))
                    chain(stt(slot[:, :], idx[:, :], float(REGION), rsel[:, :], ALU.mult, ALU.add))
                    dve.tensor_copy(slot_i[z][:, :], slot[:, :]).then_inc(pay_ready, 1)
                    dve.wait_ge(pay_ready, t + 1)
                    chain(tsc(tok[:, :], tok[:, :], float(P), None, ALU.add))
                    assert chain.n == PER, chain.n
                with dve.Fori(0, NT // 2) as i:
                    for z in range(2):
                        tile(2 * i + z, z, i)
                chain = Steps(dve, step, PER * NT)
                dve.wait_ge(cnt_mm, 1)
                dve.memset(junk[:, 0:NE], 1.0)
                chain(dve.tensor_copy(cnt[:, :], pr[:, 0:NE]))
                chain(tsc(full[:, :], cnt[:, :], float(SMALL), None, ALU.is_gt))
                for j in range(1, REGION // LARGE):
                    chain(stt(full[:, :], cnt[:, :], float(SMALL + j * LARGE), full[:, :], ALU.is_gt, ALU.add))
                chain(stt(part[:, :], full[:, :], -float(LARGE), cnt[:, :], ALU.mult, ALU.add))
                chain(tsc(part[:, :], part[:, :], 0.0, None, ALU.is_gt))
                for kind, tiles in enumerate((full, part)):
                    chain(dve.tensor_tensor_scan(upto[:, :], junk[:, 0:NE], tiles[:, :], 0.0, ALU.mult, ALU.add))
                    chain(tsc(before[:, :], upto[:, :], row[:, :], None, ALU.is_le))
                    chain(dve.tensor_reduce(ei[:, :], before[:, :], AX.X, ALU.add))
                    if kind == 0:
                        chain(tt(before[:, :], before[:, :], upto[:, :], ALU.mult))
                        chain(dve.tensor_reduce(nth[:, :], before[:, :], AX.X, ALU.max))
                        chain(tt(nth[:, :], row[:, :], nth[:, :], ALU.subtract))
                    else:
                        chain(tsc(before[:, :], ecol[:, :], ei[:, :], None, ALU.is_equal))
                        chain(tt(before[:, :], before[:, :], full[:, :], ALU.mult))
                        chain(dve.tensor_reduce(nth[:, :], before[:, :], AX.X, ALU.add))
                    tsc(tab[:, kind, 0:1], ei[:, :], float(NE - 1), None, ALU.min)
                    chain(tsc(nth[:, :], nth[:, :], float(LARGE), None, ALU.mult))
                    chain(stt(tab[:, kind, 1:2], ei[:, :], float(REGION), nth[:, :], ALU.mult, ALU.add))
                    chain(tsc(tab[:, kind, 1:2], tab[:, kind, 1:2], float(NE * REGION), None, ALU.min))
                    chain(tsc(tab[:, kind, 2:4], upto[:, NE - 1:NE].to_broadcast([P, 2]), 1.0, None, ALU.max))
                dve.tensor_copy(tab_i[:, :, :], tab[:, :, :]).then_inc(fin, 1)


def experts(nc, size, ident, w_gu, b_gu, w_down, b_down, h2_d, acc_d, slots_d, table_d):
    RAW = 4
    NG = size // P
    NB = 2 * NG
    with ExitStack() as ctx:
        t_ = Tools(nc, ctx, f"ex{size}")
        tab = t_.sb("tab", [1, P * 4], I32)
        wg = [t_.sb(f"wg{r}", [P, KD, 2, P]) for r in range(RAW)]
        wd = [t_.sb(f"wd{r}", [P, D]) for r in range(RAW)]
        wgh, wgl = ([t_.sb(f"{n}{z}", [P, KD, 2, P], F32R) for z in range(2)] for n in ("wgh", "wgl"))
        wdh, wdl = ([t_.sb(f"{n}{z}", [P, D], F32R) for z in range(2)] for n in ("wdh", "wdl"))
        nxt, cur = (t_.sb(n, [P, NG, 2], I32) for n in ("nxt", "cur"))
        xg = t_.sb("xg", [P, NG, D])
        xh, xl = (t_.sb(n, [P, KD, size], F32R) for n in ("xh", "xl"))
        bin_, bgu = (t_.sb(n, [P, 2 * NF]) for n in ("bin", "bgu"))
        bd = t_.sb("bd", [P, D])
        t1, sg, t2, t4, at = ([t_.sb(f"{n}{z}", [P, size]) for z in range(2)] for n in ("t1", "sg", "t2", "t4", "at"))
        ath, atl = ([t_.sb(f"{n}{z}", [P, size], F32R) for z in range(2)] for n in ("ath", "atl"))
        y = t_.sb("y", [P, NG, D])
        down = [t_.ps(f"d{n}") for n in range(NB)]
        gu = [t_.ps(f"g{j}") for j in range(2)]
        wg_in = [t_.sem(f"wg_in{r}") for r in range(RAW)]
        wd_in = [t_.sem(f"wd_in{r}") for r in range(RAW)]
        (tab_in, b_in, bd_in, wgh_ready, wgl_ready, wdh_ready, wdl_ready, gu_mm, down_mm, gu_read, act_ready, clip, sig,
         prod, at_step, turned, xh_ready, xl_ready, sl_in, g_in, cur_ready, b_ready, y_ready, y_scaled, y_out,
         y_free) = t_.sems(
            "tab_in b_in bd_in wgh_ready wgl_ready wdh_ready wdl_ready gu_mm down_mm gu_read act_ready clip sig "
            "prod at_step turned xh_ready xl_ready sl_in g_in cur_ready b_ready y_ready y_scaled y_out "
            "y_free")
        tick = t_.sem("tick")

        def number(eng):
            eng.wait_ge(tab_in, 16)
            return eng.value_load(tab[0:1, 2:3], min_val=1, max_val=NE)

        def flat(w):
            return w if len(w.shape) == 2 else w.rearrange("p k j n -> p (k j n)")

        with nc.Block() as block:
            @block.sync
            def _(sp):
                def expert(i):
                    return sp.value_load(tab[0:1, ds(i * 4, 1)], min_val=0, max_val=NE - 1)

                def weights(e, f):
                    r = f % RAW
                    sp.dma_start(wg[r][:, :, :, :], w_gu[ds(e, 1), f].rearrange("o p k j n -> (o p) k j n")).then_inc(
                        wg_in[r], 16)
                    sp.dma_start(wd[r][:, :], w_down[ds(e, 1), f * P:(f + 1) * P, :].rearrange("o p n -> (o p) n")).then_inc(
                        wd_in[r], 16)

                def biases(e):
                    sp.dma_start(bin_[:, :], b_gu[ds(e, 1)].rearrange("o p n -> (o p) n")).then_inc(b_in, 16)

                sp.dma_start(tab[:, :], table_d.rearrange("a b -> (a b)").rearrange("(o n) -> o n", o=1)).then_inc(tab_in, 16)
                n = number(sp)
                e = expert(0)
                for f in range(RAW):
                    weights(e, f)
                biases(e)
                with sp.Fori(0, n) as i:
                    e = expert(i)
                    for f in range(NF - RAW):
                        sp.wait_ge(wgl_ready, NF * i + f + 1)
                        sp.wait_ge(wdl_ready, NF * i + f + 1)
                        weights(e, f + RAW)
                    sp.wait_ge(y_ready, NB * i + NB)
                    sp.dma_start(bd[:, :], b_down[ds(e, 1), :].to_broadcast([P, D])).then_inc(bd_in, 16)
                    e = expert(i + 1)
                    sp.wait_ge(b_ready, i + 1)
                    biases(e)
                    for f in range(RAW):
                        sp.wait_ge(wgl_ready, NF * i + NF - RAW + f + 1)
                        sp.wait_ge(wdl_ready, NF * i + NF - RAW + f + 1)
                        weights(e, f)
                for r in range(RAW):
                    sp.wait_ge(wg_in[r], n * (16 * NF // RAW) + 16)
                    sp.wait_ge(wd_in[r], n * (16 * NF // RAW) + 16)
                stop_until(sp, b_in, n * 16 + 16, tick)

            @block.gpsimd
            def _(pool):
                pool.sem_inc(y_free, 1)
                n = number(pool)

                def fetch(i, first=False):
                    base = pool.value_load(tab[0:1, ds(i * 4 + 1, 1)], min_val=0, max_val=NE * REGION)
                    pool.dma_start(nxt[:, :, :], slots_d[ds(base, size), :].rearrange("(g p) w -> p g w", p=P)).then_inc(
                        sl_in, 16)
                    stop_until(pool, sl_in, 16 * i + 16, tick)
                    if not first:
                        stop_until(pool, turned, NB * i, tick)
                    for g in range(NG):
                        pool.indirect_dma_start(
                            out=xg[:, g, :], out_offset=None, in_=h2_d,
                            in_offset=bass.IndirectOffsetOnAxis(ap=nxt[:, g, 0:1].bitcast(U32), axis=0)).then_inc(g_in, 16)

                def split_down(s, z, r):
                    stop_until(pool, wdh_ready, s + 1, tick)
                    pool.tensor_tensor(wdl[z][:, :], wd[r][:, :], wdh[z][:, :].bitcast(F32),
                                       ALU.subtract).then_inc(wdl_ready, 1)

                fetch(0, True)
                split_down(0, 0, 0)
                with pool.Fori(0, n) as i:
                    stop_until(pool, g_in, 16 * NG * i + 16 * NG, tick)
                    pool.tensor_copy(cur[:, :, 0], nxt[:, :, 0])
                    pool.tensor_copy(cur[:, :, 1].bitcast(F32), nxt[:, :, 1].bitcast(F32)).then_inc(cur_ready, 1)
                    for f in range(NF):
                        split_down(NF * i + f + 1, (f + 1) % 2, (f + 1) % RAW)
                        if f == 0:
                            stop_until(pool, cur_ready, i + 1, tick)
                            fetch(i + 1)
                    for g in range(NG):
                        stop_until(pool, y_ready, NB * i + NB + 2 * g + 2, tick)
                        pool.tensor_scalar(y[:, g, :], y[:, g, :], cur[:, g, 1:2].bitcast(F32), None,
                                           ALU.mult).then_inc(y_scaled, 1)
                        stop_until(pool, y_scaled, NG * i + g + 1, tick)
                        pool.indirect_dma_start(
                            out=acc_d, out_offset=bass.IndirectOffsetOnAxis(ap=cur[:, g, 0:1].bitcast(U32), axis=0),
                            in_=y[:, g, :], in_offset=None, compute_op=ALU.add).then_inc(y_out, 16)
                    pool.wait_ge(y_out, 16 * NG * i + 16 * NG)
                    pool.sem_inc(y_free, 1)
                pool.wait_ge(g_in, n * (16 * NG) + 16 * NG)

            @block.tensor
            def _(pe):
                pe.sem_inc(down_mm, 1)
                n = number(pe)

                def turn(i, b):
                    g, h = divmod(b, 2)
                    if b >= 2:
                        pe.wait_ge(xl_ready, NB * i + b - 1)
                    for k in range(4):
                        last = pe.transpose(gu[b % 2][:, k * P:(k + 1) * P],
                                            xg[:, g, (4 * h + k) * P:(4 * h + k + 1) * P], ident[:, :])
                    last.then_inc(turned, 1)

                def gate_up(i, f):
                    pe.wait_ge(wgl_ready, NF * i + f + 1)
                    if f == 0:
                        pe.wait_ge(xl_ready, NB * i + NB)
                    h, l = wgh[f % 2], wgl[f % 2]
                    for j in range(2):
                        if f:
                            pe.wait_ge((clip, gu_read)[j], NF * i + f)
                        for k in range(KD):
                            for w, x in ((h, xh), (h, xl), (l, xh)):
                                last = pe.matmul(gu[j][:, 0:size], w[:, k, j, :], x[:, k, :], start=(k == 0 and x is xh and w is h),
                                                 stop=(k == KD - 1 and w is l))
                        last.then_inc(gu_mm, 1)

                def down_product(i, f, g):
                    if g == 0:
                        pe.wait_ge(wdl_ready, NF * i + f + 1)
                        pe.wait_ge(act_ready, NF * i + f + 1)
                        if f == 0:
                            pe.wait_ge(y_ready, NB * i + NB)
                    z = f % 2
                    for h in range(2):
                        for a, w in ((ath, wdh), (ath, wdl), (atl, wdh)):
                            last = pe.matmul(down[2 * g + h][:, :], a[z][:, g * P:(g + 1) * P],
                                             w[z][:, h * 512:(h + 1) * 512], start=(f == 0 and a is ath and w is wdh),
                                             stop=(f == NF - 1 and a is atl))
                    if g == NG - 1:
                        last.then_inc(down_mm, 1)

                pe.wait_ge(g_in, 16 * NG)
                for b in range(NB):
                    turn(0, b)
                with pe.Fori(0, n) as i:
                    gate_up(i, 0)
                    for f in range(1, NF):
                        gate_up(i, f)
                        for g in range(NG):
                            down_product(i, f - 1, g)
                    pe.wait_ge(g_in, 16 * NG * i + 32 * NG)
                    pe.wait_ge(gu_read, NF * i + NF)
                    for g in range(NG):
                        turn(i + 1, 2 * g)
                        turn(i + 1, 2 * g + 1)
                        down_product(i, NF - 1, g)

            @block.scalar
            def _(act):
                n = number(act)

                def split_gate_up(i, f, free=None):
                    if free is not None:
                        act.wait_ge(gu_mm, free)
                    act.wait_ge(wg_in[f % RAW], 16 * (NF // RAW) * i + 16 * (f // RAW) + 16)
                    act.activation(flat(wgh[f % 2][:, :, :, :]), flat(wg[f % RAW][:, :, :, :]), ACT.Copy).then_inc(
                        wgh_ready, 1)

                def split_down(i, f, free=None):
                    if free is not None:
                        act.wait_ge(down_mm, free)
                    act.wait_ge(wd_in[f % RAW], 16 * (NF // RAW) * i + 16 * (f // RAW) + 16)
                    act.activation(wdh[f % 2][:, :], wd[f % RAW][:, :], ACT.Copy).then_inc(wdh_ready, 1)

                def save_x(i):
                    for b in range(NB):
                        g, h = divmod(b, 2)
                        act.wait_ge(turned, NB * i + b + 1)
                        act.activation(xh[:, 4 * h:4 * h + 4, g * P:(g + 1) * P],
                                       gu[b % 2][:, :].rearrange("p (k n) -> p k n", k=4), ACT.Copy).then_inc(xh_ready, 1)
                split_gate_up(0, 0)
                split_gate_up(0, 1)
                split_down(0, 0)
                save_x(0)
                with act.Fori(0, n) as i:
                    for f in range(NF):
                        act.wait_ge(clip, NF * i + f + 1)
                        act.activation(sg[f % 2][:, :], t1[f % 2][:, :], ACT.Sigmoid, scale=ALPHA).then_inc(sig, 1)
                        if f == NF - 1:
                            save_x(i + 1)
                        di, nf = divmod(f + 2, NF)
                        split_gate_up(i + di, nf, 2 * NF * i + 2 * f + 2)
                        di, nf = divmod(f + 1, NF)
                        split_down(i + di, nf, NF * i + f + 1)

            @block.vector
            def _(dve):
                tt, tsc, stt = dve.tensor_tensor, dve.tensor_scalar, dve.scalar_tensor_tensor
                dve.sem_inc(y_ready, NB)
                n = number(dve)

                def split_gate_up(s, z, r):
                    dve.wait_ge(wgh_ready, s + 1)
                    tt(flat(wgl[z][:, :, :, :]), flat(wg[r][:, :, :, :]), flat(wgh[z][:, :, :, :]).bitcast(F32),
                       ALU.subtract).then_inc(wgl_ready, 1)

                def save_x(i):
                    for b in range(NB):
                        g, h = divmod(b, 2)
                        part = (slice(None), slice(4 * h, 4 * h + 4), slice(g * P, (g + 1) * P))
                        dve.wait_ge(xh_ready, NB * i + b + 1)
                        tt(xl[part], gu[b % 2][:, :].rearrange("p (k n) -> p k n", k=4), xh[part].bitcast(F32),
                           ALU.subtract).then_inc(xl_ready, 1)
                split_gate_up(0, 0, 0)
                split_gate_up(1, 1, 1)
                save_x(0)
                with dve.Fori(0, n) as i:
                    chain = Steps(dve, at_step, 2 * NF * i)
                    dve.wait_ge(b_in, 16 * i + 16)
                    dve.tensor_copy(bgu[:, 0:NF], bin_[:, 0:NF])
                    tsc(bgu[:, NF:], bin_[:, NF:], 1.0, None, ALU.add).then_inc(b_ready, 1)
                    dve.wait_ge(b_ready, i + 1)
                    for f in range(NF):
                        z = f % 2
                        dve.wait_ge(gu_mm, 2 * NF * i + 2 * f + 1)
                        tsc(t1[z][:, :], gu[0][:, 0:size], bgu[:, f:f + 1], LIMIT, ALU.add, ALU.min).then_inc(clip, 1)
                        dve.wait_ge(gu_mm, 2 * NF * i + 2 * f + 2)
                        tsc(t2[z][:, :], gu[1][:, 0:size], bgu[:, NF + f:NF + f + 1], LIMIT + 1.0, ALU.add,
                            ALU.min).then_inc(gu_read, 1)
                        dve.wait_ge(sig, NF * i + f + 1)
                        tt(t4[z][:, :], t1[z][:, :], sg[z][:, :], ALU.mult).then_inc(prod, 1)
                        dve.wait_ge(prod, NF * i + f + 1)
                        chain(stt(at[z][:, :], t2[z][:, :], 1.0 - LIMIT, t4[z][:, :], ALU.max, ALU.mult))
                        if f:
                            dve.wait_ge(down_mm, NF * i + f)
                        chain(dve.tensor_copy(ath[z][:, :], at[z][:, :]))
                        tt(atl[z][:, :], at[z][:, :], ath[z][:, :].bitcast(F32), ALU.subtract).then_inc(act_ready, 1)
                        if f == NF - 1:
                            save_x(i + 1)
                        split_gate_up(NF * i + f + 2, z, (f + 2) % RAW)
                    dve.wait_ge(bd_in, 16 * i + 16)
                    dve.wait_ge(y_free, i + 1)
                    dve.wait_ge(down_mm, NF * i + NF + 1)
                    for b in range(NB):
                        g, h = divmod(b, 2)
                        tt(y[:, g, h * 512:(h + 1) * 512], down[b][:, :], bd[:, h * 512:(h + 1) * 512],
                           ALU.add).then_inc(y_ready, 1)


def store(nc, acc_d, out):
    with nc.semaphore("st_done") as done, nc.Block() as block:
        @block.sync
        def _(sp):
            sp.dma_start(out, acc_d[0:S, :]).then_inc(done, 16)
            sp.wait_ge(done, 16)


def hybrid_layer(nc, a, out):
    scratch = lambda name, shape, dt=F32: nc.dram_tensor(name, list(shape), dt, kind="Internal").ap()
    att_d = scratch("att_d", [len(GROUPS), S, HG * RW])
    yT_d = scratch("yT_d", [P, SW // P, S])
    attT_d = scratch("attT_d", [P, NFT, S])
    mixed_d = scratch("mixed_d", [P, KD, S])
    rows_d = scratch("rows_d", [len(GROUPS) * HG, STEPS_W])
    acc_d = scratch("acc_d", [DUMP, D])
    h2_d = scratch("h2_d", [DUMP, D])
    slots_d = scratch("slots_d", [SLOTS, 2], I32)
    table_d = scratch("table_d", [2, P, 4], I32)
    with ExitStack() as outer:
        keep = Tools(nc, outer, "k")
        ident, jflip, upper, ones = (keep.sb(n, [P, P]) for n in ("ident", "jflip", "upper", "ones"))
        make_constants(nc, ident, jflip, upper, ones)
        with ExitStack() as ctx:
            hT = Tools(nc, ctx, "k").sb("hT", [P, KD, S])
            normalise_input(nc, a["x"], a["g_mix"], hT, ident)
            s5(nc, hT, ident, a["w_in"][:, QKV:QKV + SW].rearrange("(k p) n -> p k n", p=P),
               [a[k] for k in ("a_re", "a_im", "log_dt", "b_re", "b_im", "c_re", "c_im", "d_skip")], yT_d)
            with ExitStack() as inner:
                bias = Tools(nc, inner, "k").sb("bias", [P, len(GROUPS) * HG, 2 * P])
                bias_tables(nc, a["rel_bias"], a["onehot"], rows_d, bias, jflip)
                attention(nc, hT, a["w_in"], a["q_gain"], a["k_gain"], bias, ident, att_d)
            combine(nc, att_d, ident, attT_d)
            mix(nc, hT, yT_d, attT_d, a["w_glu"], a["b_glu"], a["mix_w"], mixed_d)
        route(nc, a["x"], mixed_d, a["w_out"], a["g_ffn"], a["w_router"], a["b_router"], a["empty_slots"], ident,
              upper, ones, acc_d, h2_d, slots_d, table_d)
        for kind, size in enumerate((LARGE, SMALL)):
            experts(nc, size, ident, a["w_gu"], a["b_gu"], a["w_down"], a["b_down"], h2_d, acc_d, slots_d,
                    table_d[kind])
        store(nc, acc_d, out)


def by_state(w):
    w = w.reshape(PAIRS, 2, SN, *w.shape[2:])
    return np.moveaxis(w, 0, 2).reshape(2 * SN, PAIRS, *w.shape[3:])


def out_tiles(w):
    return w.reshape(-1, P, w.shape[1] // P, P).transpose(2, 1, 0, 3)


def k_tiles(w):
    return w.reshape(-1, P, w.shape[1]).transpose(1, 0, 2)


def kernel(x, g_mix, w_in, q_gain, k_gain, rel_bias, ssm_a_re, ssm_a_im, ssm_log_dt, ssm_b_re, ssm_b_im, ssm_c_re,
           ssm_c_im, ssm_d, w_glu, b_glu, w_attn_proj, w_ssm_proj, w_out, g_ffn, w_router, b_router, w_gate_up,
           b_gate_up, w_down, b_down):
    import concourse.bacc as bacc
    from concourse.bass_utils import run_bass_kernel_spmd

    w_in0 = np.asarray(w_in)[0]
    gates = QKV + SW
    slots = np.zeros((SLOTS, 2), np.int32)
    slots[:, 0] = S + np.arange(SLOTS) % LARGE
    arrays = {
        "x": np.asarray(x)[0], "g_mix": np.asarray(g_mix)[0], "w_in": w_in0,
        "q_gain": np.asarray(q_gain)[0].T, "k_gain": np.asarray(k_gain)[0].T,
        "rel_bias": np.asarray(rel_bias), "onehot": bucket_onehot(),
        "a_re": by_state(np.asarray(ssm_a_re)[0]), "a_im": by_state(np.asarray(ssm_a_im)[0]),
        "log_dt": np.asarray(ssm_log_dt)[0].reshape(PAIRS, 2).T,
        "b_re": by_state(np.asarray(ssm_b_re)[0]), "b_im": by_state(np.asarray(ssm_b_im)[0]),
        "c_re": by_state(np.asarray(ssm_c_re)[0].transpose(0, 2, 1)),
        "c_im": by_state(np.asarray(ssm_c_im)[0].transpose(0, 2, 1)),
        "d_skip": np.asarray(ssm_d)[0].reshape(SG, SC).T,
        "w_glu": k_tiles(np.asarray(w_glu)[0]), "b_glu": np.asarray(b_glu)[0].reshape(-1, P).T,
        "mix_w": np.concatenate([out_tiles(m) for m in (
            w_in0[:, gates:gates + D], w_in0[:, gates + D:], np.asarray(w_attn_proj)[0], np.asarray(w_ssm_proj)[0])],
            axis=2),
        "w_out": k_tiles(np.asarray(w_out)[0]), "g_ffn": np.asarray(g_ffn)[0],
        "w_router": k_tiles(np.asarray(w_router)[0]), "b_router": np.asarray(b_router)[0], "empty_slots": slots,
        "w_gu": np.asarray(w_gate_up)[0].reshape(NE, KD, P, 2, NF, P).transpose(0, 4, 2, 1, 3, 5),
        "b_gu": np.asarray(b_gate_up)[0].reshape(NE, 2 * NF, P).transpose(0, 2, 1),
        "w_down": np.asarray(w_down)[0], "b_down": np.asarray(b_down)[0],
    }
    arrays = {k: np.ascontiguousarray(v) for k, v in arrays.items()}
    nc = bacc.Bacc("TRN2", target_bir_lowering=False, num_devices=1)
    a = {k: nc.dram_tensor(f"in_{k}", v.shape, mybir.dt.from_np(v.dtype), kind="ExternalInput").ap()
         for k, v in arrays.items()}
    out = nc.dram_tensor("out", [S, D], F32, kind="ExternalOutput").ap()
    hybrid_layer(nc, a, out)
    r = run_bass_kernel_spmd(nc, [{f"in_{k}": v for k, v in arrays.items()}], core_ids=[0])
    return r.results[0]["out"].reshape(1, S, D)
```

```python
from contextlib import ExitStack

import numpy as np

import concourse.bass as bass
from concourse import mybir

ALU = mybir.AluOpType
ACT = mybir.ActivationFunctionType
AX = mybir.AxisListType
F32 = mybir.dt.float32
F32R = mybir.dt.float32r
I32 = mybir.dt.int32
U32 = mybir.dt.uint32
ds = bass.ds

P = 128
D = 1024
KD = D // P
S = 2048
NT = S // P
DH = 64
GROUPS = ((128, 1), (512, 4), (2048, 16))
HG = 8
AW = HG * DH
NFT = AW // P
QKV = 3 * len(GROUPS) * AW
EPS = 1e-6
CH = 512
NCH = S // CH
NBLK = CH // P
MASKED = 1e30
BUCKETS, MAX_DIST = 32, 2048
STEPS_W = 384
RW = DH + 2
SW = 512
SG, SC, SN = 32, 16, 64
PAIRS = SG // 2
TS = 8
NC = S // TS
HC = NC // P
LEVELS = NC.bit_length() - 1
NE = 32
TOPK = 4
FF = 1024
NF = FF // P
LARGE, SMALL = 384, 256
NGT = LARGE // P
REGION = -(-S // LARGE) * LARGE
SLOTS = NE * REGION + LARGE
DUMP = S + LARGE
LIMIT, ALPHA = 7.0, 1.702


class Tools:

    def __init__(self, nc, ctx, tag):
        self.nc, self.ctx, self.tag, self.taken = nc, ctx, tag, []
        ctx.callback(self.give_back)

    def sb(self, name, shape, dt=F32):
        return self.ctx.enter_context(self.nc.sbuf_tensor(f"{self.tag}_{name}", list(shape), dt))

    def ps(self, name, shape=(P, 512), dt=F32):
        return self.ctx.enter_context(self.nc.psum_tensor(f"{self.tag}_{name}", list(shape), dt))

    def sem(self, name):
        self.taken.append(self.nc.alloc_semaphore(f"{self.tag}_{name}"))
        return self.taken[-1]

    def give_back(self):
        if self.taken:
            with self.nc.Block() as block:
                @block.gpsimd
                def _(pool):
                    for sem in self.taken:
                        pool.sem_clear(sem)
            for sem in self.taken:
                self.nc.release_semaphore(sem)

    def sems(self, names):
        return [self.sem(n) for n in names.split()]


class Steps:

    def __init__(self, eng, sem, base=0):
        self.eng, self.sem, self.base, self.n = eng, sem, base, 0

    def __call__(self, ins):
        self.n += 1
        ins.then_inc(self.sem, 1)
        self.eng.wait_ge(self.sem, self.base + self.n)


def stop_until(eng, sem, value, tick):
    eng.wait_ge(sem, value)
    eng.sem_inc(tick, 1)


def on_rows(row, n):
    return row.rearrange("(a w) -> a w", a=1).to_broadcast([n, row.shape[0]])


def make_constants(nc, ident, jflip, upper, ones):
    with ExitStack() as ctx:
        t_ = Tools(nc, ctx, "cst")
        filled, made = t_.sems("filled made")
        with nc.Block() as block:
            @block.gpsimd
            def _(pool):
                pool.memset(ident[:, :], 0.0).then_inc(filled, 1)
                pool.memset(jflip[:, :], 0.0).then_inc(filled, 1)
                pool.memset(upper[:, :], 0.0).then_inc(filled, 1)
                pool.memset(ones[:, :], 1.0).then_inc(made, 1)
                pool.wait_ge(filled, 3)
                pool.affine_select(out=ident[:, :], in_=ident[:, :], compare_op=ALU.not_equal, fill=1.0, base=0,
                                   pattern=[[-1, P]], channel_multiplier=1).then_inc(made, 1)
                pool.affine_select(out=jflip[:, :], in_=jflip[:, :], compare_op=ALU.not_equal, fill=1.0,
                                   base=1 - P, pattern=[[1, P]], channel_multiplier=1).then_inc(made, 1)
                pool.affine_select(out=upper[:, :], in_=upper[:, :], compare_op=ALU.is_ge, fill=1.0, base=0,
                                   pattern=[[-1, P]], channel_multiplier=1).then_inc(made, 1)
                pool.wait_ge(made, 4)


def normalise_input(nc, x, g_row, hT, ident):
    XR = 4
    with ExitStack() as ctx:
        t_ = Tools(nc, ctx, "nrm")
        xt = [t_.sb(f"x{r}", [P, D]) for r in range(XR)]
        hh = [t_.sb(f"h{s}", [P, D]) for s in range(2)]
        gb = t_.sb("gb", [P, D])
        junk = t_.sb("junk", [P, D])
        ss, ms, rms, rstd = (t_.sb(n, [P, 2]) for n in ("ss", "ms", "rms", "rstd"))
        pt = [[t_.ps(f"pt{s}{h}") for h in range(2)] for s in range(2)]
        x_in = [t_.sem(f"x_in{r}") for r in range(XR)]
        g_in, step, ms_ready, rms_ready, h_ready, t_ready, t_free = t_.sems(
            "g_in step ms_ready rms_ready h_ready t_ready t_free")
        with nc.Block() as block:
            @block.sync
            def _(sp):
                with sp.Fori(0, NT // XR) as i:
                    for r in range(XR):
                        sp.wait_ge(h_ready, XR * i + r + 1)
                        sp.dma_start(xt[r][:, :], x[ds(i * (XR * P) + r * P, P), :]).then_inc(x_in[r], 16)

            @block.vector
            def _(dve):
                dve.sem_inc(h_ready, XR)
                with dve.Fori(0, NT // XR) as i:
                    chain = Steps(dve, step, 2 * XR * i)
                    for r0 in range(0, XR, 2):
                        for s in range(2):
                            dve.wait_ge(x_in[r0 + s], 16 * i + 16)
                            chain(dve.tensor_tensor_reduce(junk[:, :], xt[r0 + s][:, :], xt[r0 + s][:, :], 1.0, 0.0,
                                                           ALU.mult, ALU.add, ss[:, s:s + 1]))
                            dve.tensor_scalar(ms[:, s:s + 1], ss[:, s:s + 1], 1.0 / D, EPS, ALU.mult,
                                              ALU.add).then_inc(ms_ready, 1)
                        if r0 == 0:
                            dve.wait_ge(g_in, 16)
                        for s in range(2):
                            t = XR * i + r0 + s
                            dve.wait_ge(rms_ready, t + 1)
                            chain(dve.reciprocal(rstd[:, s:s + 1], rms[:, s:s + 1]))
                            dve.wait_ge(t_free, 2 * t + 2)
                            dve.scalar_tensor_tensor(hh[s][:, :], xt[r0 + s][:, :], rstd[:, s:s + 1], gb[:, :],
                                                     ALU.mult, ALU.mult).then_inc(h_ready, 1)
                    assert chain.n == 2 * XR

            @block.tensor
            def _(pe):
                with pe.Fori(0, NT // 2) as i:
                    for s in range(2):
                        pe.wait_ge(h_ready, 2 * i + s + XR + 1)
                        for h in range(2):
                            for k in range(4):
                                last = pe.transpose(pt[s][h][:, k * P:(k + 1) * P],
                                                    hh[s][:, (4 * h + k) * P:(4 * h + k + 1) * P], ident[:, :])
                            last.then_inc(t_ready, 1)

            @block.scalar
            def _(act):
                act.sem_inc(t_free, 4)
                act.dma_start(gb[:, :], on_rows(g_row, P)).then_inc(g_in, 16)
                with act.Fori(0, NT // 2) as i:
                    for s in range(2):
                        act.wait_ge(ms_ready, 2 * i + s + 1)
                        act.activation(rms[:, s:s + 1], ms[:, s:s + 1], ACT.Sqrt).then_inc(rms_ready, 1)
                    for s in range(2):
                        for h in range(2):
                            act.wait_ge(t_ready, 4 * i + 2 * s + h + 1)
                            act.activation(hT[:, 4 * h:4 * h + 4, ds(i * (2 * P) + s * P, P)],
                                           pt[s][h][:, :].rearrange("p (k n) -> p k n", k=4),
                                           ACT.Copy).then_inc(t_free, 1)


def s5(nc, hT, ident, w_u, prm, y_out):
    a_re, a_im, log_dt, b_re, b_im, c_re, c_im, d_skip = prm
    NP9 = TS + 1
    LEAD = (TS - 1) * SC
    TWO_PI = 2 * np.pi
    C1 = 6.28125
    C2 = float(np.float32(np.round((TWO_PI - C1) * 2 ** 22) / 2 ** 22))
    C3 = float(np.float32(TWO_PI - C1 - C2))
    ROUND = 1.5 * 2.0 ** 23
    HALVINGS = 10
    AHEAD = 4
    with ExitStack() as ctx:
        t_ = Tools(nc, ctx, "s5")
        w = t_.sb("w", [P, KD, SW])
        tok = t_.sb("tok", [P, HC, TS, SW])
        yT = t_.sb("yT", [P, SW // P, S])
        lr, li, dt = (t_.sb(n, [P, PAIRS]) for n in ("lr", "li", "dt"))
        br0, bi0, cr, ci, br, bi = (t_.sb(n, [P, PAIRS, SC]) for n in ("br0", "bi0", "cr", "ci", "br", "bi"))
        d8 = t_.sb("d8", [P, SG])
        v = [t_.sb(f"v{n}", [P, PAIRS]) for n in range(12)]
        t16 = [t_.sb(f"t16{n}", [P, PAIRS, SC]) for n in range(2)]
        pr, pi, npi = (t_.sb(n, [P, PAIRS, NP9]) for n in ("pr", "pi", "npi"))
        rr, ri = (t_.sb(n, [P, PAIRS, TS]) for n in ("rr", "ri"))
        lar, lai, nlai = (t_.sb(n, [P, PAIRS, LEVELS]) for n in ("lar", "lai", "nlai"))
        ust = [t_.sb(f"ust{z}", [P, HC, 2, TS, SC]) for z in range(AHEAD)]
        bpad = [t_.sb(f"bpad{z}", [P, 2, 2 * LEAD + SC]) for z in range(AHEAD)]
        cpad = [t_.sb(f"cpad{z}", [P, 2, LEAD + NP9 * SC]) for z in range(AHEAD)]
        inm = [t_.sb(f"inm{z}", [P, 2, TS * SC]) for z in range(AHEAD)]
        tmp = [t_.sb(f"tmp{n}", [P, NP9 * SC]) for n in range(4)]
        u8 = [t_.sb(f"u8{z}", [P, 2 * NC]) for z in range(2)]
        inT = [t_.sb(f"inT{z}", [P, 2, P]) for z in range(2)]
        intra = [t_.sb(f"intra{z}", [P, 2, P]) for z in range(2)]
        st = [t_.sb(f"st{z}", [P, 2, NC + 1]) for z in range(2)]
        alt = t_.sb("alt", [P, 2, NC + 1])
        ps_u = [t_.ps(f"u{z}") for z in range(2)]
        ps_8, ps_in, ps_it0, ps_x = (t_.ps(n) for n in ("p8", "pin", "pit", "px"))
        ps_it = (ps_it0, ps_u[0])
        ps_y = [t_.ps(f"y{h}") for h in range(2)]
        (w_in, prm_in, dt_ready, chain_v, maps_ready, pads_ready, u_ready, u_saved, chain_p, staged, t8, tin, kin,
         acts, it_saved, x_ready, x_saved, scanned, y_ready, y_saved, chain_s, yt_ready, yt_saved, y_stored) = t_.sems(
            "w_in prm_in dt_ready chain_v maps_ready pads_ready u_ready u_saved chain_p staged t8 tin kin "
            "acts it_saved x_ready x_saved scanned y_ready y_saved chain_s yt_ready yt_saved y_stored")

        with nc.Block() as block:
            @block.sync
            def _(sp):
                sp.dma_start(w[:, :, :], w_u).then_inc(w_in, 16)
                n = 0
                for dst, src in ((lr, a_re), (li, a_im)):
                    sp.dma_start(dst[:, :], src).then_inc(prm_in, 16)
                    n += 1
                for h in range(2):
                    sp.dma_start(dt[SN * h:SN * (h + 1), :], on_rows(log_dt[h], SN)).then_inc(prm_in, 16)
                    n += 1
                for dst, src in ((br0, b_re), (bi0, b_im), (cr, c_re), (ci, c_im)):
                    sp.dma_start(dst[:, :, :], src).then_inc(prm_in, 16)
                    n += 1
                for s in range(TS):
                    sp.dma_start(d8[SC * s:SC * (s + 1), :], d_skip).then_inc(prm_in, 16)
                    n += 1
                for k in range(HC):
                    sp.wait_ge(yt_saved, (k + 1) * TS)
                    part = slice(k * P * TS, (k + 1) * P * TS)
                    sp.dma_start(y_out[:, :, part], yT[:, :, part]).then_inc(y_stored, 16)
                sp.wait_ge(y_stored, 16 * HC)
            PRM = 16 * (8 + TS)

            @block.gpsimd
            def _(pool):
                for z in range(AHEAD):
                    pool.memset(bpad[z][:, :, :], 0.0)
                    last = pool.memset(cpad[z][:, :, :], 0.0)
                last.then_inc(pads_ready, 1)
                pool.wait_ge(pads_ready, 1)
                pool.wait_ge(maps_ready, 1)
                pool.wait_ge(u_saved, HC * TS)

                def build(p, z, free):
                    if free is not None:
                        pool.wait_ge(y_ready, free)
                    chain = Steps(pool, chain_p, 3 * p)
                    for k in range(HC):
                        pool.tensor_copy(ust[z][:, k, :, :, :],
                                         tok[:, k, :, ds(p * 2 * SC, 2 * SC)].rearrange("p j (h c) -> p h j c", h=2))
                    pool.tensor_copy(bpad[z][:, 0, LEAD:LEAD + SC], br[:, ds(p, 1), :].rearrange("p a c -> p (a c)"))
                    pool.tensor_copy(bpad[z][:, 1, LEAD:LEAD + SC], bi[:, ds(p, 1), :].rearrange("p a c -> p (a c)"))

                    def outer(dst, power, factor, n):
                        return pool.tensor_tensor(
                            dst[:, 0:n * SC].rearrange("p (j c) -> p j c", c=SC),
                            power[:, ds(p, 1), :].rearrange("p a j -> p (a j)").unsqueeze(2).to_broadcast([P, n, SC]),
                            factor[:, ds(p, 1), :].to_broadcast([P, n, SC]), ALU.mult)

                    for (a, b, c, d), dst, off, n, op in (
                            (((rr, br), (ri, bi), (rr, bi), (ri, br)), inm, 0, TS, (ALU.subtract, ALU.add)),
                            (((pr, cr), (npi, ci), (npi, cr), (pr, ci)), cpad, LEAD, NP9, (ALU.add, ALU.subtract))):
                        for t, (power, factor) in zip(tmp[:3], (a, b, c)):
                            outer(t, power, factor, n)
                        chain(outer(tmp[3], *d, n))
                        pool.tensor_tensor(dst[z][:, 0, off:off + n * SC], tmp[0][:, 0:n * SC], tmp[1][:, 0:n * SC], op[0])
                        last = pool.tensor_tensor(dst[z][:, 1, off:off + n * SC], tmp[2][:, 0:n * SC],
                                                  tmp[3][:, 0:n * SC], op[1])
                        if dst is inm:
                            chain(last)
                    last.then_inc(staged, 1)
                    pool.wait_ge(staged, p + 1)

                for p in range(AHEAD):
                    build(p, p, None)
                with pool.Fori(1, PAIRS // AHEAD) as i:
                    for z in range(AHEAD):
                        build(AHEAD * i + z, z, AHEAD * (i - 1) + z + 1)

            @block.tensor
            def _(pe):
                pe.wait_ge(w_in, 16)
                for n in range(HC * TS):
                    k, j = divmod(n, TS)
                    if n >= 2:
                        pe.wait_ge(u_saved, n - 1)
                    for c in range(KD):
                        lhs = hT[:, c, k * P * TS + j:(k * P + P - 1) * TS + j + 1:TS]
                        last = pe.matmul(ps_u[n % 2][:, :], lhs, w[:, c, :], start=(c == 0), stop=(c == KD - 1))
                    last.then_inc(u_ready, 1)

                def inputs(p, f):
                    z = f % 2
                    pe.wait_ge(staged, p + 1)
                    pe.wait_ge(acts, 2 * p + 1)
                    for h in range(2):
                        for k in range(HC):
                            last = pe.transpose(ps_8[:, h * NC + k * P:h * NC + (k + 1) * P],
                                                ust[f][:, k, h, :, :].rearrange("p j c -> p (j c)"), ident[:, :])
                    last.then_inc(t8, 1)
                    for r in range(2):
                        last = pe.transpose(ps_in[:, r * P:(r + 1) * P], inm[f][:, r, :], ident[:, :])
                    last.then_inc(tin, 1)
                    pe.wait_ge(it_saved, 2 * p + 2)
                    for h in range(2):
                        q = slice(SN * h, SN * (h + 1))
                        for s in range(TS):
                            for r in range(2):
                                last = pe.matmul(ps_it[h][:, 0:P], bpad[f][q, r, LEAD - SC * s:LEAD - SC * s + P],
                                                 cpad[f][q, r, LEAD - SC * s:LEAD - SC * s + P],
                                                 start=(s == 0 and r == 0), stop=(s == TS - 1 and r == 1))
                    last.then_inc(kin, 1)
                    pe.wait_ge(acts, 2 * p + 3)
                    pe.wait_ge(x_saved, p + 1)
                    for r in range(2):
                        for h in range(2):
                            last = pe.matmul(ps_x[SN * h:SN * (h + 1), r * NC:(r + 1) * NC],
                                             inT[z][:, r, SN * h:SN * (h + 1)], u8[z][:, h * NC:(h + 1) * NC],
                                             start=True, stop=True)
                    last.then_inc(x_ready, 1)

                def outputs(p, f):
                    z = f % 2
                    pe.wait_ge(scanned, p + 1)
                    pe.wait_ge(y_saved, 4 * p + 4)
                    for h in range(2):
                        q = slice(SN * h, SN * (h + 1))
                        for k in range(HC):
                            out = ps_y[h][:, k * P:(k + 1) * P]
                            pe.matmul(out, u8[z][:, h * NC + k * P:h * NC + (k + 1) * P], intra[z][:, h, :],
                                      start=True, stop=False)
                            for r in range(2):
                                last = pe.matmul(out, st[z][q, r, k * P:(k + 1) * P], cpad[f][q, r, LEAD + SC:],
                                                 start=False, stop=(r == 1))
                    last.then_inc(y_ready, 1)

                inputs(0, 0)
                with pe.Fori(0, PAIRS // AHEAD - 1) as i:
                    for f in range(AHEAD):
                        inputs(AHEAD * i + f + 1, (f + 1) % AHEAD)
                        outputs(AHEAD * i + f, f)
                for f in range(AHEAD):
                    if f + 1 < AHEAD:
                        inputs(PAIRS - AHEAD + f + 1, f + 1)
                    outputs(PAIRS - AHEAD + f, f)
                pe.wait_ge(y_saved, 4 * PAIRS + 4)
                for n in range(HC * TS):
                    k, j = divmod(n, TS)
                    if n >= 2:
                        pe.wait_ge(yt_saved, n - 1)
                    for f in range(SW // P):
                        last = pe.transpose(ps_u[n % 2][:, f * P:(f + 1) * P], tok[:, k, j, f * P:(f + 1) * P], ident[:, :])
                    last.then_inc(yt_ready, 1)

            @block.scalar
            def _(act):
                act.sem_inc(acts, 1)
                act.sem_inc(y_saved, 4)
                act.wait_ge(prm_in, PRM)
                act.activation(dt[:, :], dt[:, :], ACT.Exp).then_inc(dt_ready, 1)
                for n in range(HC * TS):
                    k, j = divmod(n, TS)
                    act.wait_ge(u_ready, n + 1)
                    act.activation(tok[:, k, j, :], ps_u[n % 2][:, :], ACT.Copy).then_inc(u_saved, 1)

                def save_inputs(p, z):
                    act.wait_ge(t8, p + 1)
                    act.activation(u8[z][:, :], ps_8[:, :], ACT.Copy).then_inc(acts, 1)
                    act.wait_ge(tin, p + 1)
                    act.activation(inT[z][:, :, :], ps_in[:, 0:2 * P].rearrange("p (r n) -> p r n", r=2),
                                   ACT.Copy).then_inc(acts, 1)

                def save_outputs(p, z):
                    act.wait_ge(y_ready, p + 1)
                    for h in range(2):
                        for k in range(HC):
                            act.activation(tok[:, k, :, ds(p * 2 * SC + h * SC, SC)],
                                           ps_y[h][:, k * P:(k + 1) * P].rearrange(
                                               "p (j c) -> p j c", c=SC), ACT.Gelu_apprx_tanh).then_inc(y_saved, 1)

                save_inputs(0, 0)
                with act.Fori(0, PAIRS // 2 - 1) as i:
                    save_inputs(2 * i + 1, 1)
                    save_outputs(2 * i, 0)
                    save_inputs(2 * i + 2, 0)
                    save_outputs(2 * i + 1, 1)
                save_inputs(PAIRS - 1, 1)
                save_outputs(PAIRS - 2, 0)
                save_outputs(PAIRS - 1, 1)

            @block.vector
            def _(dve):
                for z in range(2):
                    dve.memset(st[z][:, :, 0:1], 0.0)
                dve.sem_inc(it_saved, 2)
                dve.sem_inc(x_saved, 1)
                go = Steps(dve, chain_v)
                tt, tsc, stt = dve.tensor_tensor, dve.tensor_scalar, dve.scalar_tensor_tensor

                def cmul(re, im, ar, ai, b_r, b_i, t):
                    tt(t[0], ar, b_r, ALU.mult)
                    tt(t[1], ai, b_i, ALU.mult)
                    tt(t[2], ar, b_i, ALU.mult)
                    go(tt(t[3], ai, b_r, ALU.mult))
                    tt(re, t[0], t[1], ALU.subtract)
                    go(tt(im, t[2], t[3], ALU.add))

                vv = [x[:, :] for x in v]
                t4 = vv[8:12]
                dve.wait_ge(dt_ready, 1)
                tt(vv[0], lr[:, :], dt[:, :], ALU.mult)
                go(tt(vv[1], li[:, :], dt[:, :], ALU.mult))
                go(tsc(vv[2], vv[1], 1.0 / TWO_PI, None, ALU.mult))
                go(tsc(vv[2], vv[2], ROUND, None, ALU.add))
                go(tsc(vv[2], vv[2], -ROUND, None, ALU.add))
                for c in (C1, C2, C3):
                    go(stt(vv[1], vv[2], -c, vv[1], ALU.mult, ALU.add))
                go(tsc(vv[0], vv[0], -110.0, 100.0, ALU.max, ALU.min))
                tsc(vv[0], vv[0], 0.5 ** HALVINGS, None, ALU.mult)
                go(tsc(vv[1], vv[1], 0.5 ** HALVINGS, None, ALU.mult))
                tsc(vv[2], vv[0], 1 / 6, 1.0, ALU.mult, ALU.add)
                go(tsc(vv[3], vv[1], 1 / 6, None, ALU.mult))
                for k in (5, 4, 3, 2):
                    cmul(vv[4], vv[5], vv[0], vv[1], vv[2], vv[3], t4)
                    tsc(vv[2], vv[4], 1 / k, 1.0, ALU.mult, ALU.add)
                    go(tsc(vv[3], vv[5], 1 / k, None, ALU.mult))
                cmul(vv[4], vv[5], vv[0], vv[1], vv[2], vv[3], t4)
                for _ in range(HALVINGS):
                    stt(t4[0], vv[4], 2.0, vv[4], ALU.add, ALU.mult)
                    tt(t4[1], vv[5], vv[5], ALU.mult)
                    go(stt(t4[2], vv[4], 1.0, vv[5], ALU.add, ALU.mult))
                    tt(vv[4], t4[0], t4[1], ALU.subtract)
                    go(tsc(vv[5], t4[2], 2.0, None, ALU.mult))
                er, ei = vv[4], vv[5]
                tsc(vv[6], li[:, :], -1.0, None, ALU.mult)
                tt(t4[0], lr[:, :], lr[:, :], ALU.mult)
                go(tt(t4[1], li[:, :], li[:, :], ALU.mult))
                go(tt(vv[7], t4[0], t4[1], ALU.add))
                go(dve.reciprocal(vv[7], vv[7]))
                cmul(vv[0], vv[1], er, ei, lr[:, :], vv[6], t4)
                tt(vv[2], vv[0], vv[7], ALU.mult)
                go(tt(vv[3], vv[1], vv[7], ALU.mult))
                fr, fi = (x.unsqueeze(2).to_broadcast([P, PAIRS, SC]) for x in (vv[2], vv[3]))
                for dst, (f0, b0), (f1, b1), op in ((br, (fr, br0), (fi, bi0), ALU.subtract),
                                                    (bi, (fr, bi0), (fi, br0), ALU.add)):
                    tt(t16[0][:, :, :], b0[:, :, :], f0, ALU.mult)
                    go(tt(t16[1][:, :, :], b1[:, :, :], f1, ALU.mult))
                    go(tt(dst[:, :, :], t16[0][:, :, :], t16[1][:, :, :], op))
                dve.memset(pr[:, :, 0:1], 1.0)
                dve.memset(pi[:, :, 0:1], 0.0)
                tsc(pr[:, :, 1], er, 1.0, None, ALU.add)
                go(dve.tensor_copy(pi[:, :, 1], ei))
                for j in range(2, NP9):
                    cmul(pr[:, :, j], pi[:, :, j], pr[:, :, j - 1], pi[:, :, j - 1], pr[:, :, 1], pi[:, :, 1], t4)
                tsc(npi[:, :, :], pi[:, :, :], -1.0, None, ALU.mult)
                for j in range(TS):
                    dve.tensor_copy(rr[:, :, j], pr[:, :, TS - 1 - j])
                    dve.tensor_copy(ri[:, :, j], pi[:, :, TS - 1 - j])
                dve.tensor_copy(lar[:, :, 0], pr[:, :, TS])
                go(dve.tensor_copy(lai[:, :, 0], pi[:, :, TS]))
                for l in range(1, LEVELS):
                    a, b = lar[:, :, l - 1], lai[:, :, l - 1]
                    cmul(lar[:, :, l], lai[:, :, l], a, b, a, b, t4)
                go(tsc(nlai[:, :, :], lai[:, :, :], -1.0, None, ALU.mult))
                dve.sem_inc(maps_ready, 1)

                def scan(p, z):
                    dve.wait_ge(kin, p + 1)
                    for h in range(2):
                        stt(intra[z][:, h, :], ident[:, :], d8[:, ds(2 * p + h, 1)], ps_it[h][:, 0:P],
                            ALU.mult, ALU.add).then_inc(it_saved, 1)
                    dve.wait_ge(x_ready, p + 1)
                    dve.tensor_copy(st[z][:, :, 1:], ps_x[:, :].rearrange("p (r n) -> p r n", r=2)).then_inc(x_saved, 1)
                    dve.wait_ge(x_saved, p + 2)
                    chain = Steps(dve, chain_s, (2 * LEVELS - 1) * p)
                    src, dst = st[z], alt
                    for l in range(LEVELS):
                        s = 1 << l
                        scalar = [x[:, ds(p, 1), l:l + 1].rearrange("p a b -> p (a b)") for x in (lar, nlai, lai)]
                        dve.tensor_copy(dst[:, :, 1:1 + s], src[:, :, 1:1 + s])
                        chain(stt(dst[:, :, 1 + s:], src[:, :, 1:NC + 1 - s], scalar[0], src[:, :, 1 + s:],
                                  ALU.mult, ALU.add))
                        stt(dst[:, 0, 1 + s:], src[:, 1, 1:NC + 1 - s], scalar[1], dst[:, 0, 1 + s:], ALU.mult, ALU.add)
                        last = stt(dst[:, 1, 1 + s:], src[:, 0, 1:NC + 1 - s], scalar[2], dst[:, 1, 1 + s:],
                                   ALU.mult, ALU.add)
                        if l < LEVELS - 1:
                            chain(last)
                        src, dst = dst, src
                    last.then_inc(scanned, 1)
                    dve.wait_ge(scanned, p + 1)

                with dve.Fori(0, PAIRS // 2) as i:
                    for z in range(2):
                        scan(2 * i + z, z)
                for n in range(HC * TS):
                    k, j = divmod(n, TS)
                    dve.wait_ge(yt_ready, n + 1)
                    first = k * P * TS + j
                    dve.tensor_copy(yT[:, :, first:first + (P - 1) * TS + 1:TS],
                                    ps_u[n % 2][:, :].rearrange("p (f n) -> p f n", f=SW // P)).then_inc(yt_saved, 1)


def bucket_onehot():
    hot = np.zeros((BUCKETS + 1, len(GROUPS), STEPS_W), np.float32)
    exact = BUCKETS // 2
    for g, (window, dilation) in enumerate(GROUPS):
        steps = 2 * P - 1 - np.arange(STEPS_W)
        inside = (steps >= 0) & (steps <= window // dilation)
        dist = np.clip(steps, 0, None) * dilation
        far = exact + (np.log(np.maximum(dist, 1).astype(np.float32) / exact) / np.log(MAX_DIST / exact)
                       * (BUCKETS - exact)).astype(np.int32)
        bucket = np.where(dist < exact, dist, np.minimum(far, BUCKETS - 1))
        hot[bucket[inside], g, np.nonzero(inside)[0]] = 1.0
        hot[BUCKETS, g] = np.where(inside, 0.0, MASKED)
    return hot


def bias_tables(nc, rel_bias, onehot, rows_d, bias, jflip):
    NG, NH = len(GROUPS), len(GROUPS) * HG
    with ExitStack() as ctx:
        t_ = Tools(nc, ctx, "bia")
        rel = t_.sb("rel", [BUCKETS + 1, NH])
        hot = t_.sb("hot", [BUCKETS + 1, NG, STEPS_W])
        rows = t_.sb("rows", [HG, NG, STEPS_W])
        hank = t_.sb("hank", [P, NH, 2 * P])
        pr = [t_.ps(f"pr{g}") for g in range(NG)]
        pf = [t_.ps(f"pf{n}") for n in range(4)]
        loaded, negated, rows_ready, rows_saved, rows_out, hank_in, flipped, saved = t_.sems(
            "loaded negated rows_ready rows_saved rows_out hank_in flipped saved")
        with nc.Block() as block:
            @block.sync
            def _(sp):
                sp.dma_start(rel[0:BUCKETS, :], rel_bias).then_inc(loaded, 16)
                sp.dma_start(hot[:, :, :], onehot).then_inc(loaded, 16)
                sp.wait_ge(rows_saved, NG)
                sp.dma_start(rows_d.rearrange("(g h) s -> h g s", g=NG), rows[:, :, :]).then_inc(rows_out, 16)
                sp.wait_ge(rows_out, 16)
                shifted = bass.AP(rows_d.tensor, rows_d.offset, [[1, P], [STEPS_W, NH], [1, 2 * P]])
                sp.dma_start(hank[:, :, :], shifted).then_inc(hank_in, 16)

            @block.vector
            def _(dve):
                dve.memset(rel[BUCKETS:BUCKETS + 1, :], 1.0)
                dve.wait_ge(loaded, 32)
                dve.tensor_scalar(rel[0:BUCKETS, :], rel[0:BUCKETS, :], -1.0, None, ALU.mult).then_inc(negated, 1)
                for g in range(NG):
                    dve.wait_ge(rows_ready, g + 1)
                    dve.tensor_copy(rows[:, g, :], pr[g][0:HG, 0:STEPS_W]).then_inc(rows_saved, 1)
                for n in range(NH // 2):
                    dve.wait_ge(flipped, n + 1)
                    dve.tensor_copy(bias[:, 2 * n:2 * n + 2, :],
                                    pf[n % 4][:, :].rearrange("p (h k) -> p h k", h=2)).then_inc(saved, 1)

            @block.tensor
            def _(pe):
                pe.wait_ge(negated, 1)
                for g in range(NG):
                    pe.matmul(pr[g][0:HG, 0:STEPS_W], rel[:, g * HG:(g + 1) * HG], hot[:, g, :], start=True,
                              stop=True).then_inc(rows_ready, 1)
                pe.wait_ge(hank_in, 16)
                for n in range(NH // 2):
                    if n >= 4:
                        pe.wait_ge(saved, n - 3)
                    pe.matmul(pf[n % 4][:, :], jflip[:, :],
                              hank[:, 2 * n:2 * n + 2, :].rearrange("p h k -> p (h k)"), start=True,
                              stop=True).then_inc(flipped, 1)


def attention(nc, hT, w_in, q_gain, k_gain, bias, ident, att_d):
    UN = NBLK * HG
    with ExitStack() as ctx:
        t_ = Tools(nc, ctx, "att")
        hc = t_.sb("hc", [P, KD, CH])
        w = [t_.sb(f"w{n}", [P, KD, AW]) for n in "qkv"]
        qT = t_.sb("qT", [P, NFT, CH])
        kT = t_.sb("kT", [P, NFT, P + CH])
        v = t_.sb("v", [P, 1 + NBLK, AW])
        same = t_.sb("same", [P, P])
        gains = [t_.sb(f"gain{n}", [P, len(GROUPS)]) for n in "qk"]
        eps = t_.sb("eps", [P, 1])
        tick = t_.sem("tick")
        rt = [t_.sb(f"rt{z}", [P, CH]) for z in range(2)]
        sc = [t_.sb(f"sc{z}", [P, 2 * P]) for z in range(3)]
        probs = t_.sb("probs", [P, 4 * 2 * P])
        pp = [probs[:, z * 2 * P:(z + 1) * 2 * P] for z in range(4)]
        sq = [probs[:, z * CH:(z + 1) * CH] for z in range(2)]
        ppT = [t_.sb(f"ppT{z}", [P, 2 * P]) for z in range(3)]
        ao = [t_.sb(f"ao{z}", [P, HG, RW]) for z in range(NBLK)]
        bank = [t_.ps(f"b{n}") for n in range(8)]
        gm, ssq, tb, ob = (bank[0], bank[1], bank[3], bank[4]), bank[2], bank[4:6], bank[6:8]
        vb = (bank[0], bank[1], bank[3], bank[7])
        sb = (bank[2], bank[0], bank[1], bank[3])
        w_sem = [t_.sem(f"w_in_{n}") for n in "qkv"]
        ao_out = [t_.sem(f"ao_out{z}") for z in range(NBLK)]
        (gain_in, const, gain_ready, hc_ready, qk_mm, v_mm, qk_done, v_done, sq_ready, ssq_ready, root_ready, rec,
         s_ready, s_read, p_ready, t_ready, pt_ready, pv_done, o_saved) = t_.sems(
            "gain_in const gain_ready hc_ready qk_mm v_mm qk_done v_done sq_ready ssq_ready root_ready rec "
            "s_ready s_read p_ready t_ready pt_ready pv_done o_saved")

        def chunks(eng, g, body):
            first = g == 0
            if first:
                body(g, 0, 0, True)
            with eng.Fori(1 if first else 0, NCH) as c:
                body(g, c, c + NCH * g, False)

        def alone(g, b, opening):
            return g == 2 or (b == 0 and (g == 1 or opening))

        def in_group_order(ap, g, c):
            d = GROUPS[g][1]
            if d == 1:
                return ap[:, :, ds(c * CH, CH)].rearrange("p k (r a) -> p k r a", r=1)
            n = d // NCH
            return ap.rearrange("p k (a r) -> p k r a", r=d)[:, :, ds(c * n, n), :]

        def block_rows(g, c, b):
            rows = att_d[g]
            if g == 0:
                return rows[ds(c * CH + b * P, P), :]
            d = GROUPS[g][1]
            r, a = (c, b) if g == 1 else (c * NBLK + b, 0)
            return rows.rearrange("(a r) w -> r a w", r=d)[ds(r, 1), a * P:(a + 1) * P, :].rearrange("o a w -> (o a) w")

        with nc.Block() as block:
            @block.sync
            def _(sp):
                for h in range(2):
                    for dst, src in zip(gains, (q_gain, k_gain)):
                        sp.dma_start(dst[DH * h:DH * (h + 1), :], src).then_inc(gain_in, 16)
                def load(g, i):
                    col = (i * len(GROUPS) + g) * AW
                    sp.dma_start(w[i][:, :, :], w_in[:, col:col + AW].rearrange("(k p) n -> p k n", p=P)).then_inc(
                        w_sem[i], 16)

                def chunk(g, c, n, opening):
                    for b in range(NBLK):
                        sp.wait_ge(o_saved, NBLK * n + b + 1)
                        sp.dma_start(block_rows(g, c, b), ao[b][:, :, :].rearrange("p h w -> p (h w)")).then_inc(
                            ao_out[b], 16)

                for i in range(3):
                    load(0, i)
                chunk(0, 0, 0, True)
                for g in range(len(GROUPS)):
                    with sp.Fori(1 if g == 0 else 0, NCH - 1) as c:
                        chunk(g, c, c + NCH * g, False)
                    if g + 1 < len(GROUPS):
                        for i in range(2):
                            sp.wait_ge(qk_mm, 2 * NFT * (NCH * (g + 1) - 1) + NFT * (i + 1))
                            load(g + 1, i)
                        sp.wait_ge(v_mm, NBLK * NCH * (g + 1))
                        load(g + 1, 2)
                    chunk(g, NCH - 1, NCH * g + NCH - 1, False)
                for z in range(NBLK):
                    sp.wait_ge(ao_out[z], 16 * NCH * len(GROUPS))

            @block.gpsimd
            def _(pool):
                pool.memset(same[:, :], 0.0).then_inc(const, 1)
                pool.memset(eps[:, :], EPS).then_inc(const, 1)
                pool.wait_ge(const, 2)
                for h in range(2):
                    pool.memset(same[DH * h:DH * (h + 1), DH * h:DH * (h + 1)], 1.0).then_inc(const, 1)

                pool.wait_ge(const, 4)

                def stage(g, c, n, opening):
                    if not opening:
                        pool.wait_ge(v_mm, NBLK * n)
                    src = in_group_order(hT[:, :, :], g, c)
                    pool.tensor_copy(hc[:, :, :].rearrange("p k (r a) -> p k r a", r=src.shape[2]),
                                     src).then_inc(hc_ready, 1)
                for g in range(len(GROUPS)):
                    chunks(pool, g, stage)

            @block.tensor
            def _(pe):
                pe.wait_ge(const, 4)

                def chunk(g, c, n, opening):
                    pe.wait_ge(hc_ready, n + 1)
                    if not opening:
                        pe.wait_ge(s_read, UN * n)

                    def square_sums(t):
                        pe.wait_ge(sq_ready, 2 * NFT * n + t + 1)
                        if t or not opening:
                            pe.wait_ge(root_ready, 2 * NFT * n + t)
                        pe.matmul(ssq[:, :], same[:, :], sq[t % 2][:, :], start=True, stop=True).then_inc(ssq_ready, 1)

                    for t in range(2 * NFT):
                        i, f = divmod(t, NFT)
                        if f == 0:
                            pe.wait_ge(w_sem[i], 16 * g + 16)
                        if t >= 4:
                            pe.wait_ge(qk_done, 2 * NFT * n + t - 3)
                        for k in range(KD):
                            last = pe.matmul(gm[t % 4][:, :], w[i][:, k, f * P:(f + 1) * P], hc[:, k, :],
                                             start=(k == 0), stop=(k == KD - 1))
                        last.then_inc(qk_mm, 1)
                        if t:
                            square_sums(t - 1)
                    pe.wait_ge(w_sem[2], 16 * g + 16)

                    def scores(u):
                        b, h = divmod(u, HG)
                        off, rows = (P if alone(g, b, opening) else 0), slice(DH * (h % 2), DH * (h % 2) + DH)
                        pe.matmul(sb[u % 4][:, off:2 * P], qT[rows, h // 2, b * P:(b + 1) * P],
                                  kT[rows, h // 2, b * P + off:(b + 2) * P], start=True, stop=True).then_inc(s_ready, 1)

                    for b in range(NBLK):
                        if b < 3:
                            pe.wait_ge(qk_done, 2 * NFT * n + 2 * NFT - 3 + b)
                        else:
                            pe.wait_ge(qk_done, 2 * NFT * (n + 1))
                            scores(0)
                            pe.wait_ge(v_done, NBLK * n + 1)
                            scores(1)
                            if not opening:
                                pe.wait_ge(o_saved, NBLK * n)
                        for k in range(KD):
                            last = pe.matmul(vb[b][:, :], hc[:, k, b * P:(b + 1) * P], w[2][:, k, :],
                                             start=(k == 0), stop=(k == KD - 1))
                        last.then_inc(v_mm, 1)
                        if b == 0:
                            square_sums(2 * NFT - 1)

                    for step in range(2, UN + 5):
                        if step < UN:
                            if step < 4:
                                pe.wait_ge(v_done, NBLK * n + step)
                            else:
                                pe.wait_ge(s_read, UN * n + step - 3)
                            scores(step)
                        u = step - 3
                        if 0 <= u < UN:
                            b, h = divmod(u, HG)
                            pe.wait_ge(p_ready, UN * n + u + 1)
                            if u >= 2 or not opening:
                                pe.wait_ge(pt_ready, UN * n + u - 1)
                            for k in range(1 if alone(g, b, opening) else 0, 2):
                                last = pe.transpose(tb[u % 2][:, k * P:(k + 1) * P], pp[u % 4][:, k * P:(k + 1) * P],
                                                    ident[:, :])
                            last.then_inc(t_ready, 1)
                        u = step - 5
                        if 0 <= u < UN:
                            b, h = divmod(u, HG)
                            pe.wait_ge(pt_ready, UN * n + u + 1)
                            if u == 0:
                                pe.wait_ge(v_done, NBLK * n + NBLK)
                            if h == 0 and (b >= 2 or not opening):
                                pe.wait_ge(o_saved, NBLK * n + b - 1)
                            k0 = 1 if alone(g, b, opening) else 0
                            for k in range(k0, 2):
                                last = pe.matmul(ob[b % 2][:, h * DH:(h + 1) * DH], ppT[u % 3][:, k * P:(k + 1) * P],
                                                 v[:, b + k, h * DH:(h + 1) * DH], start=(k == k0), stop=(k == 1))
                            last.then_inc(pv_done, 1)
                for g in range(len(GROUPS)):
                    chunks(pe, g, chunk)

            @block.scalar
            def _(act):
                act.wait_ge(const, 4)

                def chunk(g, c, n, opening):
                    def root(t):
                        act.wait_ge(ssq_ready, 2 * NFT * n + t + 1)
                        if t >= 2 or not opening:
                            act.wait_ge(qk_done, 2 * NFT * n + t - 1)
                        act.activation(rt[t % 2][:, :], ssq[:, :], ACT.Sqrt, bias=eps[:, :],
                                       scale=1.0 / DH).then_inc(root_ready, 1)

                    for t in range(2 * NFT):
                        act.wait_ge(qk_mm, 2 * NFT * n + t + 1)
                        act.activation(sq[t % 2][:, :], gm[t % 4][:, :], ACT.Square).then_inc(sq_ready, 1)
                        if t:
                            root(t - 1)
                    root(2 * NFT - 1)
                    if g == 0 and not opening:
                        act.wait_ge(pv_done, UN * n)
                        act.activation(v[:, 0, :], v[:, NBLK, :], ACT.Copy).then_inc(gain_ready, 1)
                        act.wait_ge(gain_ready, n + 1)
                    for b in range(NBLK):
                        act.wait_ge(v_mm, NBLK * n + b + 1)
                        if b == 0 and not opening:
                            act.wait_ge(pv_done, UN * n)
                        act.activation(v[:, 1 + b, :], vb[b][:, :], ACT.Copy).then_inc(v_done, 1)

                    def save(b):
                        act.wait_ge(pv_done, UN * n + HG * (b + 1))
                        act.activation(ao[b][:, :, 0:DH], ob[b % 2][:, :].rearrange("p (h d) -> p h d", h=HG),
                                       ACT.Copy).then_inc(o_saved, 1)

                    for u in range(UN):
                        b, h = divmod(u, HG)
                        off = P if alone(g, b, opening) else 0
                        act.wait_ge(s_read, UN * n + u + 1)
                        if u >= 4 or not opening:
                            act.wait_ge(t_ready, UN * n + u - 3)
                        act.activation(pp[u % 4][:, off:2 * P], sc[u % 3][:, off:2 * P], ACT.Exp,
                                       bias=ao[b][:, h, DH:DH + 1], scale=-1.0,
                                       accum_out=ao[b][:, h, DH + 1:DH + 2]).then_inc(p_ready, 1)
                        if h == 5 and b:
                            save(b - 1)
                    save(NBLK - 1)
                for g in range(len(GROUPS)):
                    chunks(act, g, chunk)

            @block.vector
            def _(dve):
                dve.wait_ge(gain_in, 64)
                dve.tensor_scalar(gains[0][:, :], gains[0][:, :], -(DH ** -0.5), None, ALU.mult).then_inc(gain_ready, 1)
                dve.wait_ge(gain_ready, 1)

                def chunk(g, c, n, opening):
                    if not opening:
                        dve.wait_ge(s_ready, UN * n)
                    if g == 0 and not opening:
                        dve.tensor_copy(kT[:, :, 0:P], kT[:, :, CH:CH + P]).then_inc(rec, 1)
                        dve.wait_ge(rec, (2 * NFT + 1) * n)
                    kept = n if g == 0 else NCH - 1
                    for t in range(2 * NFT):
                        i, f = divmod(t, NFT)
                        dve.wait_ge(root_ready, 2 * NFT * n + t + 1)
                        dve.reciprocal(rt[t % 2][:, :], rt[t % 2][:, :]).then_inc(rec, 1)
                        dve.wait_ge(rec, 2 * NFT * n + kept + t + 1)
                        dst = qT[:, f, :] if i == 0 else kT[:, f, P:P + CH]
                        dve.scalar_tensor_tensor(dst, gm[t % 4][:, :], gains[i][:, g:g + 1], rt[t % 2][:, :], ALU.mult,
                                                 ALU.mult).then_inc(qk_done, 1)
                    for step in range(UN + 3):
                        u = step
                        if u < UN:
                            b, h = divmod(u, HG)
                            off = P if alone(g, b, opening) else 0
                            dve.wait_ge(s_ready, UN * n + u + 1)
                            if u >= 3 or not opening:
                                dve.wait_ge(p_ready, UN * n + u - 2)
                            if h == 0 and not opening:
                                dve.wait_ge(ao_out[b], 16 * n)
                            dve.sem_inc(tick, 1)
                            dve.tensor_tensor_reduce(sc[u % 3][:, off:2 * P], sb[u % 4][:, off:2 * P],
                                                     bias[:, HG * g + h, off:2 * P], 1.0, MASKED, ALU.add, ALU.min,
                                                     ao[b][:, h, DH:DH + 1]).then_inc(s_read, 1)
                        u = step - 3
                        if 0 <= u < UN:
                            b = u // HG
                            off = P if alone(g, b, opening) else 0
                            dve.wait_ge(t_ready, UN * n + u + 1)
                            if u >= 3 or not opening:
                                dve.wait_ge(pv_done, UN * n + u - 2)
                            dve.tensor_copy(ppT[u % 3][:, off:2 * P], tb[u % 2][:, off:2 * P]).then_inc(pt_ready, 1)
                for g in range(len(GROUPS)):
                    chunks(dve, g, chunk)



def mix(nc, hT, ident, yT_d, att_d, w_glu, b_glu, w_tiles, mixed_d):
    KA = AW // P
    KW = 2 * KD + 2 * KA
    NO = D // P
    NG = len(GROUPS)
    STEPS = 8
    assert NO == 2 * NBLK
    with ExitStack() as ctx:
        t_ = Tools(nc, ctx, "mix")
        glu = t_.sb("glu", [P, KA, SW])
        bg = t_.sb("bg", [P, KA])
        w = [t_.sb(f"w{z}", [P, KW, P]) for z in range(2)]
        y, y2 = (t_.sb(n, [P, KA, CH]) for n in ("y", "y2"))
        ga, gb, ta, tb = ([t_.sb(f"{n}{z}", [P, CH]) for z in range(2)] for n in ("ga", "gb", "ta", "tb"))
        mx = t_.sb("mx", [P, NO, CH])
        a = [[t_.sb(f"a{z}{g}", [P, HG, RW]) for g in range(NG)] for z in range(2)]
        low, den, rden = (t_.sb(n, [P, HG]) for n in ("low", "den", "rden"))
        dif, wgt, part = (t_.sb(n, [P, NG, HG]) for n in ("dif", "wgt", "part"))
        comb = [t_.sb(f"comb{z}", [P, AW]) for z in range(2)]
        m1, m2 = (t_.sb(n, [P, AW]) for n in ("m1", "m2"))
        aT = t_.sb("aT", [P, NFT, S])
        bank = [t_.ps(f"b{n}") for n in range(8)]
        pg, pt = bank[4:7], bank[7]
        w_sem = [t_.sem(f"w_in{z}") for z in range(2)]
        a_in = [t_.sem(f"a_in{z}") for z in range(2)]
        (glu_in, y_in, glu_mm, sig, y2_ready, mm, gates, m_b, mx_ready, mx_out, step, added, dif_ready, w_ready,
         combined, turned, saved) = t_.sems(
            "glu_in y_in glu_mm sig y2_ready mm gates m_b mx_ready mx_out step added dif_ready w_ready "
            "combined turned saved")

        def over_chunks(eng, body):
            body(0, True, True)
            with eng.Fori(1, NCH - 1) as c:
                body(c, False, True)
            body(NCH - 1, False, False)

        with nc.Block() as block:
            @block.sync
            def _(sp):
                def load_att(c, j):
                    sp.wait_ge(combined, NBLK * c + j + 1)
                    for g in range(NG):
                        sp.dma_start(a[j % 2][g][:, :, :].rearrange("p h w -> p (h w)"),
                                     att_d[g, ds(c * CH + j * P, P), :]).then_inc(a_in[j % 2], 16)

                def chunk(c, first, more):
                    sp.wait_ge(y2_ready, c * KA + 1)
                    sp.dma_start(y[:, :, :], yT_d[:, :, ds(c * CH, CH)]).then_inc(y_in, 16)
                    for o in range(NO):
                        if first and o == 2:
                            for j in range(NBLK):
                                load_att(0, j)
                            load_att(1, 0)
                        sp.wait_ge(mm, c * (4 * NO) + 4 * o + 4)
                        sp.dma_start(w[o % 2][:, :, :], w_tiles[o]).then_inc(w_sem[o % 2], 16)
                        if more and o % 2 == 0 and not (first and o == 0):
                            load_att(c + 1, o // 2)

                sp.dma_start(glu[:, :, :], w_glu).then_inc(glu_in, 16)
                sp.dma_start(bg[:, :], b_glu).then_inc(glu_in, 16)
                over_chunks(sp, chunk)
                sp.wait_ge(mx_out, 16 * NCH)

            @block.tensor
            def _(pe):
                pe.sem_inc(mm, 8)
                pe.sem_inc(turned, 2)
                pe.wait_ge(glu_in, 32)

                def turn(c, j):
                    n = NBLK * c + j
                    pe.wait_ge(combined, n + 3)
                    pe.wait_ge(saved, n + 1)
                    for f in range(NFT):
                        last = pe.transpose(pt[:, f * P:(f + 1) * P], comb[j % 2][:, f * P:(f + 1) * P], ident[:, :])
                    last.then_inc(turned, 1)

                def chunk(c, first, more):
                    pe.wait_ge(y_in, 16 * c + 16)
                    for f in range(KA):
                        if f < 3:
                            pe.wait_ge(y2_ready, c * KA + 1)
                        else:
                            pe.wait_ge(sig, c * KA + 1)
                        for k in range(KA):
                            last = pe.matmul(pg[f % 3][:, :], glu[:, k, f * P:(f + 1) * P], y[:, k, :], start=(k == 0),
                                             stop=(k == KA - 1))
                        last.then_inc(glu_mm, 1)
                    for o in range(NO):
                        z = o % 2
                        t = c * NO + o
                        pe.wait_ge(w_sem[z], c * (16 * NO // 2) + 16 * (o // 2) + 16)
                        pe.wait_ge(gates, 2 * t + 1)
                        for j in range(2):
                            for k in range(KD):
                                last = pe.matmul(bank[j][:, :], w[z][:, j * KD + k, :], hT[:, k, ds(c * CH, CH)],
                                                 start=(k == 0), stop=(k == KD - 1))
                            last.then_inc(mm, 1)
                        if first and o == 0:
                            for j in range(NBLK):
                                turn(0, j)
                        if more and o % 2:
                            turn(c + 1, o // 2)
                        if o == 0:
                            pe.wait_ge(saved, NBLK * c + NBLK + 1)
                            pe.wait_ge(y2_ready, c * KA + KA + 1)
                        pe.wait_ge(m_b, t + 2)
                        for j in range(2):
                            for k in range(KA):
                                src = (aT[:, k, ds(c * CH, CH)], y2[:, k, :])[j]
                                last = pe.matmul(bank[2 + j][:, :], w[z][:, 2 * KD + j * KA + k, :], src,
                                                 start=(k == 0), stop=(k == KA - 1))
                            last.then_inc(mm, 1)
                over_chunks(pe, chunk)

            @block.scalar
            def _(act):
                act.sem_inc(gates, 1)
                act.sem_inc(saved, 1)
                act.wait_ge(glu_in, 32)

                def weigh(c, j):
                    act.wait_ge(dif_ready, NBLK * c + j + 1)
                    act.activation(wgt[:, :, :], dif[:, :, :], ACT.Exp).then_inc(w_ready, 1)

                def save(c, j):
                    act.wait_ge(turned, NBLK * c + j + 3)
                    act.activation(aT[:, :, ds(c * CH + j * P, P)], pt[:, :].rearrange("p (f n) -> p f n", f=NFT),
                                   ACT.Copy).then_inc(saved, 1)

                def chunk(c, first, more):
                    act.wait_ge(mm, c * (4 * NO) + 8)
                    for f in range(KA):
                        act.wait_ge(glu_mm, c * KA + f + 1)
                        act.activation(y2[:, f, :], pg[f % 3][:, :], ACT.Sigmoid, bias=bg[:, f:f + 1]).then_inc(sig, 1)
                    if first:
                        for j in range(NBLK):
                            weigh(0, j)
                            if j:
                                save(0, j - 1)
                        save(0, NBLK - 1)
                    for o in range(NO):
                        t = c * NO + o
                        for j, dst in enumerate((ga, gb)):
                            act.wait_ge(mm, 4 * t + 8 + j + 1)
                            act.wait_ge(m_b, t + 1)
                            act.activation(dst[o % 2][:, :], bank[j][:, :], ACT.Sigmoid).then_inc(gates, 1)
                        if more:
                            (weigh, save)[o % 2](c + 1, o // 2)
                over_chunks(act, chunk)

            @block.vector
            def _(dve):
                tt = dve.tensor_tensor
                dve.sem_inc(m_b, 2)
                dve.sem_inc(y2_ready, 1)
                dve.sem_inc(combined, 2)

                def combine(c, j):
                    n, z = NBLK * c + j, j % 2
                    chain = Steps(dve, step, STEPS * n)
                    dve.wait_ge(a_in[z], 16 * NG * (NBLK // 2 * c + j // 2) + 16 * NG)
                    m = [x[:, :, DH] for x in a[z]]
                    chain(tt(low[:, :], m[0], m[1], ALU.min))
                    chain(tt(low[:, :], low[:, :], m[2], ALU.min))
                    for g in range(NG):
                        last = tt(dif[:, g, :], low[:, :], m[g], ALU.subtract)
                    last.then_inc(dif_ready, 1)
                    dve.wait_ge(w_ready, n + 1)
                    for g in range(NG):
                        last = tt(part[:, g, :], wgt[:, g, :], a[z][g][:, :, DH + 1], ALU.mult)
                    chain(last)
                    chain(tt(den[:, :], part[:, 0, :], part[:, 1, :], ALU.add))
                    chain(tt(den[:, :], den[:, :], part[:, 2, :], ALU.add))
                    chain(dve.reciprocal(rden[:, :], den[:, :]))
                    chain(tt(part[:, :, :], wgt[:, :, :], rden[:, :].unsqueeze(1).to_broadcast([P, NG, HG]), ALU.mult))

                    def weighted(dst, g):
                        return tt(dst[:, :].rearrange("p (h d) -> p h d", h=HG), a[z][g][:, :, 0:DH],
                                  part[:, g, :].unsqueeze(2).to_broadcast([P, HG, DH]), ALU.mult)
                    weighted(m1, 0)
                    weighted(m2, 1)
                    dve.wait_ge(turned, n + 1)
                    chain(weighted(comb[z], 2))
                    tt(m1[:, :], m1[:, :], m2[:, :], ALU.add).then_inc(added, 1)
                    dve.wait_ge(added, n + 1)
                    tt(comb[z][:, :], comb[z][:, :], m1[:, :], ALU.add).then_inc(combined, 1)
                    dve.wait_ge(combined, n + 3)
                    assert chain.n == STEPS

                def chunk(c, first, more):
                    for f in range(KA):
                        dve.wait_ge(sig, c * KA + f + 1)
                        tt(y2[:, f, :], y[:, f, :], y2[:, f, :], ALU.mult).then_inc(y2_ready, 1)
                    if first:
                        for j in range(NBLK):
                            combine(0, j)
                    for o in range(NO):
                        t = c * NO + o
                        z = o % 2
                        dve.wait_ge(gates, 2 * t + 3)
                        dve.wait_ge(mm, 4 * t + 8 + 4)
                        dve.wait_ge(mx_ready, t + 1)
                        tt(ta[z][:, :], bank[2][:, :], ga[z][:, :], ALU.mult)
                        tt(tb[z][:, :], bank[3][:, :], gb[z][:, :], ALU.mult).then_inc(m_b, 1)
                        if more and z == 0:
                            combine(c + 1, o // 2)
                over_chunks(dve, chunk)

            @block.gpsimd
            def _(pool):
                pool.sem_inc(mx_ready, 2)
                with pool.Fori(0, NCH) as c:
                    for o in range(NO):
                        t = c * NO + o
                        pool.wait_ge(m_b, t + 3)
                        pool.tensor_tensor(mx[:, o, :], ta[o % 2][:, :], tb[o % 2][:, :], ALU.add).then_inc(mx_ready, 1)
                    pool.wait_ge(mx_ready, c * NO + NO + 2)
                    pool.dma_start(mixed_d[:, :, ds(c * CH, CH)], mx[:, :, :]).then_inc(mx_out, 16)
                    pool.wait_ge(mx_out, 16 * c + 16)


def route(nc, x, mixed_d, w_out, g_row, w_router, b_router, empty_slots, ident, upper, ones, acc_d, h2_d, slots_d,
          table_d):
    with ExitStack() as ctx:
        t_ = Tools(nc, ctx, "rt")
        w = t_.sb("w", [P, KD, D])
        wh, wl = (t_.sb(n, [P, KD, D], F32R) for n in ("wh", "wl"))
        mh, ml = ([t_.sb(f"{n}{z}", [P, D], F32R) for z in range(2)] for n in ("mh", "ml"))
        gb = t_.sb("gb", [P, D])
        wr = t_.sb("wr", [P, KD, NE])
        br = t_.sb("br", [1, NE])
        xt, mt, x1, h2 = ([t_.sb(f"{n}{z}", [P, D]) for z in range(2)] for n in ("x", "m", "x1", "h2"))
        h2T = t_.sb("h2T", [P, KD, P])
        zero = t_.sb("zero", [P, D])
        junk = t_.sb("junk", [P, D])
        ss, ms, rms, rstd, top, nbest, esum, resum, tok = (t_.sb(n, [P, 1]) for n in (
            "ss", "ms", "rms", "rstd", "top", "nbest", "esum", "resum", "tok"))
        lg, mask, chosen = (t_.sb(n, [P, NE]) for n in ("lg", "mask", "chosen"))
        v8 = t_.sb("v8", [P, 8])
        i8 = t_.sb("i8", [P, 8], U32)
        idx, ex, rsel, slot = (t_.sb(n, [P, TOPK]) for n in ("idx", "ex", "rsel", "slot"))
        ecol = t_.sb("ecol", [P, NE])
        hot, rk = (t_.sb(n, [P, TOPK, NE]) for n in ("hot", "rk"))
        slot_i = [t_.sb(f"slot_i{z}", [P, TOPK], U32) for z in range(2)]
        pay = [t_.sb(f"pay{z}", [P, TOPK, 2], I32) for z in range(2)]
        cnt, full, part, upto, before = (t_.sb(n, [P, NE]) for n in ("cnt", "full", "part", "upto", "before"))
        row, ei, nth = (t_.sb(n, [P, 1]) for n in ("row", "ei", "nth"))
        tab = t_.sb("tab", [P, 2, 4])
        tab_i = t_.sb("tab_i", [P, 2, 4], I32)
        po = [[t_.ps(f"o{z}{h}") for h in range(2)] for z in range(2)]
        pt = [t_.ps(f"t{h}") for h in range(2)]
        pl, pr = t_.ps("l"), t_.ps("r")
        x_in = [t_.sem(f"x_in{z}") for z in range(2)]
        x1_out = [t_.sem(f"x1_out{z}") for z in range(2)]
        h2_out = [t_.sem(f"h2_out{z}") for z in range(2)]
        w_in = [t_.sem(f"w_in{n}") for n in range(2)]
        tick = t_.sem("tick")
        (wh_ready, wl_ready, mh_ready, ml_ready, c_in, pre, pad_out, iot, mm, x1_ready, step, ms_ready, rms_ready, h2_ready, turned, h2T_ready, lg_mm, ex_in,
         ex_ready, mask_ready, rank_mm, rank_read, pay_ready, pay_free, sc_out, cnt_mm, fin, tab_out) = t_.sems(
            "wh_ready wl_ready mh_ready ml_ready c_in pre pad_out iot mm x1_ready step ms_ready rms_ready h2_ready turned h2T_ready lg_mm ex_in "
            "ex_ready mask_ready rank_mm rank_read pay_ready pay_free sc_out cnt_mm fin tab_out")
        rows = lambda ap, t: ap[ds(t * P, P), :]
        half = [slice(n * KD // 2, (n + 1) * KD // 2) for n in range(2)]
        with nc.Block() as block:
            @block.sync
            def _(sp):
                for n in range(2):
                    sp.dma_start(w[:, half[n], :], w_out[:, half[n], :]).then_inc(w_in[n], 16)
                sp.dma_start(gb[:, :], on_rows(g_row, P)).then_inc(c_in, 16)
                sp.dma_start(wr[:, :, :], w_router).then_inc(c_in, 16)
                sp.dma_start(br[:, :], on_rows(b_router, 1)).then_inc(c_in, 16)
                sp.dma_start(slots_d, empty_slots).then_inc(pre, 16)
                with sp.Fori(0, NT // 2) as i:
                    for z in range(2):
                        t = 2 * i + z
                        sp.wait_ge(h2_ready, t + 1)
                        sp.dma_start(xt[z][:, :], rows(x, t)).then_inc(x_in[z], 16)
                        sp.dma_start(mt[z][:, :].rearrange("p (k n) -> p k n", k=KD),
                                     mixed_d[:, :, ds(t * P, P)]).then_inc(x_in[z], 16)

            @block.scalar
            def _(act):
                act.sem_inc(h2T_ready, 2)
                for z in range(2):
                    act.sem_inc(x1_out[z], 16)
                    act.sem_inc(h2_out[z], 16)
                act.wait_ge(pad_out, 1)
                for g in range(NGT):
                    act.dma_start(h2_d[S + g * P:S + (g + 1) * P, :], zero[:, :]).then_inc(pre, 16)
                    act.dma_start(acc_d[S + g * P:S + (g + 1) * P, :], zero[:, :]).then_inc(pre, 16)

                def normalise(t, z):
                    act.wait_ge(ms_ready, t + 1)
                    act.activation(rms[:, :], ms[:, :], ACT.Sqrt).then_inc(rms_ready, 1)
                    act.dma_start(rows(acc_d, t), x1[z][:, :]).then_inc(x1_out[z], 16)
                    act.wait_ge(h2_ready, t + 3)
                    act.dma_start(rows(h2_d, t), h2[z][:, :]).then_inc(h2_out[z], 16)

                def save(t):
                    for h in range(2):
                        act.wait_ge(turned, 2 * t + h + 3)
                        if h == 0:
                            act.wait_ge(lg_mm, t + 1)
                        act.activation(h2T[:, 4 * h:4 * h + 4, :], pt[h][:, :].rearrange("p (k n) -> p k n", k=4),
                                       ACT.Copy).then_inc(h2T_ready, 1)

                def gates(t):
                    act.wait_ge(ex_in, t + 2)
                    act.activation(ex[:, :], v8[:, 0:TOPK], ACT.Exp, bias=nbest[:, :],
                                   accum_out=esum[:, :]).then_inc(ex_ready, 1)

                def split(t, i, z, first=False):
                    if not first:
                        act.wait_ge(mm, 2 * t - 2)
                    act.wait_ge(x_in[z], 32 * i + 32)
                    act.activation(mh[z][:, :], mt[z][:, :], ACT.Copy).then_inc(mh_ready, 1)

                def tile(i, z, more):
                    t = 2 * i + z
                    normalise(t + 1, 1 - z)
                    gates(t)
                    save(t + 1)
                    if more:
                        split(t + 3, i + 1 + z, 1 - z)

                for n in range(2):
                    act.wait_ge(w_in[n], 16)
                    act.activation(wh[:, half[n], :].rearrange("p k n -> p (k n)"),
                                   w[:, half[n], :].rearrange("p k n -> p (k n)"), ACT.Copy).then_inc(wh_ready, 1)
                    split(n, 0, n, True)
                normalise(0, 0)
                save(0)
                split(2, 1, 0)
                with act.Fori(0, NT // 2 - 2) as i:
                    for z in range(2):
                        tile(i, z, True)
                tile(NT // 2 - 2, 0, True)
                tile(NT // 2 - 2, 1, False)
                tile(NT // 2 - 1, 0, False)
                gates(NT - 1)
                for z in range(2):
                    act.wait_ge(x1_out[z], 16 * (NT // 2) + 16)
                    act.wait_ge(h2_out[z], 16 * (NT // 2) + 16)
                act.wait_ge(fin, 1)
                act.dma_start(table_d.rearrange("k p c -> p k c"), tab_i[:, :, :]).then_inc(tab_out, 16)
                act.wait_ge(tab_out, 16)

            @block.tensor
            def _(pe):
                pe.sem_inc(lg_mm, 1)
                pe.sem_inc(turned, 2)
                pe.wait_ge(c_in, 48)
                pe.wait_ge(wl_ready, 2)

                def project(t, z, h):
                    if h == 0:
                        pe.wait_ge(ml_ready, t + 1)
                        pe.wait_ge(x1_ready, 2 * t + 2)
                    for k in range(KD):
                        for m, wp in ((mh, wh), (mh, wl), (ml, wh)):
                            last = pe.matmul(po[z][h][:, :], m[z][:, k * P:(k + 1) * P], wp[:, k, h * 512:(h + 1) * 512],
                                             start=(k == 0 and m is mh and wp is wh), stop=(k == KD - 1 and m is ml))
                    last.then_inc(mm, 1)

                def turn(t, z):
                    pe.wait_ge(h2_ready, t + 3)
                    for h in range(2):
                        if h == 0:
                            pe.wait_ge(h2T_ready, 2 * t + 2)
                        for k in range(4):
                            last = pe.transpose(pt[h][:, k * P:(k + 1) * P],
                                                h2[z][:, (4 * h + k) * P:(4 * h + k + 1) * P], ident[:, :])
                        last.then_inc(turned, 1)

                def logits(t):
                    pe.wait_ge(h2T_ready, 2 * t + 4)
                    pe.wait_ge(ex_in, t + 1)
                    for k in range(KD):
                        pe.matmul(pl[:, 0:NE], h2T[:, k, :], wr[:, k, :], start=(k == 0), stop=False)
                    pe.matmul(pl[:, 0:NE], ones[0:1, :], br[:, :], start=False, stop=True).then_inc(lg_mm, 1)

                def rank(t):
                    pe.wait_ge(mask_ready, t + 1)
                    pe.matmul(pr[:, 0:NE], upper[:, :], mask[:, :], start=True, stop=False)
                    pe.matmul(pr[:, 0:NE], ones[:, :], chosen[:, :], start=False, stop=True).then_inc(rank_mm, 1)

                project(0, 0, 0)
                project(0, 0, 1)
                project(1, 1, 0)
                turn(0, 0)
                project(1, 1, 1)
                logits(0)
                with pe.Fori(0, NT // 2 - 1) as i:
                    for z in range(2):
                        t = 2 * i + z
                        project(t + 2, z, 0)
                        turn(t + 1, 1 - z)
                        project(t + 2, z, 1)
                        rank(t)
                        logits(t + 1)
                turn(NT - 1, 1)
                rank(NT - 2)
                logits(NT - 1)
                rank(NT - 1)
                pe.wait_ge(rank_read, NT)
                pe.matmul(pr[:, 0:NE], ones[:, :], chosen[:, :], start=True, stop=True).then_inc(cnt_mm, 1)

            @block.gpsimd
            def _(pool):
                pool.sem_inc(pay_free, 2)
                pool.memset(zero[:, :], 0.0).then_inc(pad_out, 1)
                pool.iota(ecol[:, :], [[1, NE]], base=0, channel_multiplier=0,
                          allow_small_or_imprecise_dtypes=True).then_inc(iot, 1)
                pool.iota(tok[:, :], [[1, 1]], base=0, channel_multiplier=1,
                          allow_small_or_imprecise_dtypes=True).then_inc(iot, 1)
                pool.iota(row[:, :], [[1, 1]], base=0, channel_multiplier=1,
                          allow_small_or_imprecise_dtypes=True).then_inc(iot, 1)
                pool.wait_ge(pre, 16 + 32 * NGT)
                with pool.Fori(0, NT // 2) as i:
                    for z in range(2):
                        stop_until(pool, pay_ready, 2 * i + z + 1, tick)
                        for s in range(TOPK):
                            pool.indirect_dma_start(
                                out=slots_d, out_offset=bass.IndirectOffsetOnAxis(ap=slot_i[z][:, s:s + 1], axis=0),
                                in_=pay[z][:, s, :], in_offset=None).then_inc(sc_out, 16)
                        pool.wait_ge(sc_out, 16 * TOPK * (2 * i + z + 1))
                        pool.sem_inc(pay_free, 1)

            @block.vector
            def _(dve):
                tt, tsc, stt = dve.tensor_tensor, dve.tensor_scalar, dve.scalar_tensor_tensor
                dve.sem_inc(x1_ready, 4)
                dve.sem_inc(h2_ready, 2)
                dve.sem_inc(ex_in, 1)
                dve.memset(chosen[:, :], 0.0)
                dve.wait_ge(c_in, 48)
                dve.wait_ge(iot, 3)
                FRONT, PER = 2, 13

                def normalise(t, z, i, chain):
                    dve.wait_ge(x1_out[z], 16 * i + 16)
                    dve.wait_ge(h2_out[z], 16 * i + 16)
                    dve.wait_ge(x_in[z], 32 * i + 32)
                    for h in range(2):
                        dve.wait_ge(mm, 2 * t + h + 1)
                        tt(x1[z][:, h * 512:(h + 1) * 512], po[z][h][:, :], xt[z][:, h * 512:(h + 1) * 512],
                           ALU.add).then_inc(x1_ready, 1)
                    dve.wait_ge(x1_ready, 2 * t + 6)
                    chain(dve.tensor_tensor_reduce(junk[:, :], x1[z][:, :], x1[z][:, :], 1.0, 0.0, ALU.mult, ALU.add,
                                                   ss[:, :]))
                    tsc(ms[:, :], ss[:, :], 1.0 / D, EPS, ALU.mult, ALU.add).then_inc(ms_ready, 1)
                    dve.wait_ge(rms_ready, t + 1)
                    chain(dve.reciprocal(rstd[:, :], rms[:, :]))
                    dve.wait_ge(turned, 2 * t + 2)
                    stt(h2[z][:, :], x1[z][:, :], rstd[:, :], gb[:, :], ALU.mult, ALU.mult).then_inc(h2_ready, 1)

                def split(t, z):
                    dve.wait_ge(mh_ready, t + 1)
                    tt(ml[z][:, :], mt[z][:, :], mh[z][:, :].bitcast(F32), ALU.subtract).then_inc(ml_ready, 1)

                def choose(t, z, chain, more=False):
                    dve.wait_ge(lg_mm, t + 2)
                    chain(dve.tensor_copy(lg[:, :], pl[:, 0:NE]))
                    dve.sem_inc(tick, 1)
                    chain(dve.max(v8[:, :], lg[:, :]))
                    dve.sem_inc(tick, 1)
                    dve.max_index(i8[:, :], v8[:, :], lg[:, :])
                    tsc(nbest[:, :], v8[:, 0:1], -1.0, None, ALU.mult).then_inc(ex_in, 1)
                    dve.wait_ge(ex_in, t + 2)
                    chain(dve.tensor_copy(idx[:, :], i8[:, 0:TOPK]))
                    chain(tt(hot[:, :, :], ecol[:, :].unsqueeze(1).to_broadcast([P, TOPK, NE]),
                             idx[:, :].unsqueeze(2).to_broadcast([P, TOPK, NE]), ALU.is_equal))
                    dve.tensor_reduce(mask[:, :], hot[:, :, :].rearrange("p s e -> p e s"), AX.X,
                                      ALU.add).then_inc(mask_ready, 1)
                    dve.wait_ge(ex_ready, t + 1)
                    chain(dve.reciprocal(resum[:, :], esum[:, :]))
                    dve.wait_ge(pay_free, t + 1)
                    chain(tsc(pay[z][:, :, 1].bitcast(F32), ex[:, :], resum[:, :], None, ALU.mult))
                    chain(dve.tensor_copy(pay[z][:, :, 0], tok[:, :].to_broadcast([P, TOPK])))
                    if more:
                        split(t + 3, 1 - z)
                    dve.wait_ge(rank_mm, t + 1)
                    chain(tt(rk[:, :, :], hot[:, :, :], pr[:, 0:NE].unsqueeze(1).to_broadcast([P, TOPK, NE]), ALU.mult))
                    tt(chosen[:, :], chosen[:, :], mask[:, :], ALU.add).then_inc(rank_read, 1)
                    chain(dve.tensor_reduce(rsel[:, :], rk[:, :, :], AX.X, ALU.add))
                    chain(stt(slot[:, :], idx[:, :], float(REGION), rsel[:, :], ALU.mult, ALU.add))
                    dve.tensor_copy(slot_i[z][:, :], slot[:, :]).then_inc(pay_ready, 1)
                    dve.wait_ge(pay_ready, t + 1)
                    chain(tsc(tok[:, :], tok[:, :], float(P), None, ALU.add))

                def tile(i, z, more):
                    t = 2 * i + z
                    chain = Steps(dve, step, FRONT + PER * t)
                    normalise(t + 1, 1 - z, i + z, chain)
                    choose(t, z, chain, more)
                    assert chain.n == PER

                for n in range(2):
                    dve.wait_ge(wh_ready, n + 1)
                    tt(wl[:, half[n], :].rearrange("p k n -> p (k n)"), w[:, half[n], :].rearrange("p k n -> p (k n)"),
                       wh[:, half[n], :].rearrange("p k n -> p (k n)").bitcast(F32), ALU.subtract).then_inc(wl_ready, 1)
                    split(n, n)
                normalise(0, 0, 0, Steps(dve, step))
                split(2, 0)
                with dve.Fori(0, NT // 2 - 2) as i:
                    for z in range(2):
                        tile(i, z, True)
                tile(NT // 2 - 2, 0, True)
                tile(NT // 2 - 2, 1, False)
                tile(NT // 2 - 1, 0, False)
                choose(NT - 1, 1, Steps(dve, step, FRONT + PER * (NT - 1)))
                chain = Steps(dve, step, PER * NT)
                dve.wait_ge(cnt_mm, 1)
                dve.memset(junk[:, 0:NE], 1.0)
                chain(dve.tensor_copy(cnt[:, :], pr[:, 0:NE]))
                chain(tsc(full[:, :], cnt[:, :], float(SMALL), None, ALU.is_gt))
                for j in range(1, REGION // LARGE):
                    chain(stt(full[:, :], cnt[:, :], float(SMALL + j * LARGE), full[:, :], ALU.is_gt, ALU.add))
                chain(stt(part[:, :], full[:, :], -float(LARGE), cnt[:, :], ALU.mult, ALU.add))
                chain(tsc(part[:, :], part[:, :], 0.0, None, ALU.is_gt))
                for kind, tiles in enumerate((full, part)):
                    chain(dve.tensor_tensor_scan(upto[:, :], junk[:, 0:NE], tiles[:, :], 0.0, ALU.mult, ALU.add))
                    chain(tsc(before[:, :], upto[:, :], row[:, :], None, ALU.is_le))
                    chain(dve.tensor_reduce(ei[:, :], before[:, :], AX.X, ALU.add))
                    if kind == 0:
                        chain(tt(before[:, :], before[:, :], upto[:, :], ALU.mult))
                        chain(dve.tensor_reduce(nth[:, :], before[:, :], AX.X, ALU.max))
                        chain(tt(nth[:, :], row[:, :], nth[:, :], ALU.subtract))
                    else:
                        chain(tsc(before[:, :], ecol[:, :], ei[:, :], None, ALU.is_equal))
                        chain(tt(before[:, :], before[:, :], full[:, :], ALU.mult))
                        chain(dve.tensor_reduce(nth[:, :], before[:, :], AX.X, ALU.add))
                    tsc(tab[:, kind, 0:1], ei[:, :], float(NE - 1), None, ALU.min)
                    chain(tsc(nth[:, :], nth[:, :], float(LARGE), None, ALU.mult))
                    chain(stt(tab[:, kind, 1:2], ei[:, :], float(REGION), nth[:, :], ALU.mult, ALU.add))
                    chain(tsc(tab[:, kind, 1:2], tab[:, kind, 1:2], float(NE * REGION), None, ALU.min))
                    chain(tsc(tab[:, kind, 2:4], upto[:, NE - 1:NE].to_broadcast([P, 2]), 1.0, None, ALU.max))
                dve.tensor_copy(tab_i[:, :, :], tab[:, :, :]).then_inc(fin, 1)


def experts(nc, size, ident, w_gu, b_gu, w_down, b_down, h2_d, acc_d, slots_d, table_d):
    RAW = 4
    NG = size // P
    NB = 2 * NG
    with ExitStack() as ctx:
        t_ = Tools(nc, ctx, f"ex{size}")
        tab = t_.sb("tab", [1, P * 4], I32)
        wg = [t_.sb(f"wg{r}", [P, KD, 2, P]) for r in range(RAW)]
        wd = [t_.sb(f"wd{r}", [P, D]) for r in range(RAW)]
        wgh, wgl = ([t_.sb(f"{n}{z}", [P, KD, 2, P], F32R) for z in range(2)] for n in ("wgh", "wgl"))
        wdh, wdl = ([t_.sb(f"{n}{z}", [P, D], F32R) for z in range(2)] for n in ("wdh", "wdl"))
        nxt, cur = (t_.sb(n, [P, NG, 2], I32) for n in ("nxt", "cur"))
        xg = t_.sb("xg", [P, NG, D])
        xh, xl = (t_.sb(n, [P, KD, size], F32R) for n in ("xh", "xl"))
        bin_, bgu = (t_.sb(n, [P, 2 * NF]) for n in ("bin", "bgu"))
        bd = t_.sb("bd", [P, D])
        t1, sg, t2, t4, at = ([t_.sb(f"{n}{z}", [P, size]) for z in range(2)] for n in ("t1", "sg", "t2", "t4", "at"))
        ath, atl = ([t_.sb(f"{n}{z}", [P, size], F32R) for z in range(2)] for n in ("ath", "atl"))
        y = t_.sb("y", [P, NG, D])
        down = [t_.ps(f"d{n}") for n in range(NB)]
        gu = [t_.ps(f"g{j}") for j in range(2)]
        wg_in = [t_.sem(f"wg_in{r}") for r in range(RAW)]
        wd_in = [t_.sem(f"wd_in{r}") for r in range(RAW)]
        (tab_in, b_in, bd_in, wgh_ready, wgl_ready, wdh_ready, wdl_ready, gu_mm, down_mm, gu_read, act_ready, clip, sig,
         prod, at_step, turned, xh_ready, xl_ready, sl_in, g_in, cur_ready, b_ready, y_ready, y_scaled, y_out,
         y_free) = t_.sems(
            "tab_in b_in bd_in wgh_ready wgl_ready wdh_ready wdl_ready gu_mm down_mm gu_read act_ready clip sig "
            "prod at_step turned xh_ready xl_ready sl_in g_in cur_ready b_ready y_ready y_scaled y_out "
            "y_free")
        tick = t_.sem("tick")

        def number(eng):
            eng.wait_ge(tab_in, 16)
            return eng.value_load(tab[0:1, 2:3], min_val=1, max_val=NE)

        def flat(w):
            return w if len(w.shape) == 2 else w.rearrange("p k j n -> p (k j n)")

        with nc.Block() as block:
            @block.sync
            def _(sp):
                def expert(i):
                    return sp.value_load(tab[0:1, ds(i * 4, 1)], min_val=0, max_val=NE - 1)

                def weights(e, f):
                    r = f % RAW
                    sp.dma_start(wg[r][:, :, :, :], w_gu[ds(e, 1), f].rearrange("o p k j n -> (o p) k j n")).then_inc(
                        wg_in[r], 16)
                    sp.dma_start(wd[r][:, :], w_down[ds(e, 1), f * P:(f + 1) * P, :].rearrange("o p n -> (o p) n")).then_inc(
                        wd_in[r], 16)

                def biases(e):
                    sp.dma_start(bin_[:, :], b_gu[ds(e, 1)].rearrange("o p n -> (o p) n")).then_inc(b_in, 16)

                sp.dma_start(tab[:, :], table_d.rearrange("a b -> (a b)").rearrange("(o n) -> o n", o=1)).then_inc(tab_in, 16)
                n = number(sp)
                e = expert(0)
                weights(e, 0)
                biases(e)
                sp.wait_ge(g_in, 16 * NG)
                for f in range(1, RAW):
                    weights(e, f)
                with sp.Fori(0, n) as i:
                    e = expert(i)
                    for f in range(NF - RAW):
                        sp.wait_ge(wgl_ready, NF * i + f + 1)
                        sp.wait_ge(wdl_ready, NF * i + f + 1)
                        weights(e, f + RAW)
                    sp.wait_ge(y_ready, NB * i + NB)
                    sp.dma_start(bd[:, :], b_down[ds(e, 1), :].to_broadcast([P, D])).then_inc(bd_in, 16)
                    e = expert(i + 1)
                    sp.wait_ge(b_ready, i + 1)
                    biases(e)
                    for f in range(RAW):
                        sp.wait_ge(wgl_ready, NF * i + NF - RAW + f + 1)
                        sp.wait_ge(wdl_ready, NF * i + NF - RAW + f + 1)
                        weights(e, f)
                for r in range(RAW):
                    sp.wait_ge(wg_in[r], n * (16 * NF // RAW) + 16)
                    sp.wait_ge(wd_in[r], n * (16 * NF // RAW) + 16)
                stop_until(sp, b_in, n * 16 + 16, tick)

            @block.gpsimd
            def _(pool):
                pool.sem_inc(y_free, 1)
                n = number(pool)

                def fetch(i, first=False):
                    base = pool.value_load(tab[0:1, ds(i * 4 + 1, 1)], min_val=0, max_val=NE * REGION)
                    pool.dma_start(nxt[:, :, :], slots_d[ds(base, size), :].rearrange("(g p) w -> p g w", p=P)).then_inc(
                        sl_in, 16)
                    stop_until(pool, sl_in, 16 * i + 16, tick)
                    if not first:
                        stop_until(pool, turned, NB * i, tick)
                    for g in range(NG):
                        pool.indirect_dma_start(
                            out=xg[:, g, :], out_offset=None, in_=h2_d,
                            in_offset=bass.IndirectOffsetOnAxis(ap=nxt[:, g, 0:1].bitcast(U32), axis=0)).then_inc(g_in, 16)

                def split_down(s, z, r):
                    stop_until(pool, wdh_ready, s + 1, tick)
                    pool.tensor_tensor(wdl[z][:, :], wd[r][:, :], wdh[z][:, :].bitcast(F32),
                                       ALU.subtract).then_inc(wdl_ready, 1)

                fetch(0, True)
                split_down(0, 0, 0)
                with pool.Fori(0, n) as i:
                    stop_until(pool, g_in, 16 * NG * i + 16 * NG, tick)
                    pool.tensor_copy(cur[:, :, 0], nxt[:, :, 0])
                    pool.tensor_copy(cur[:, :, 1].bitcast(F32), nxt[:, :, 1].bitcast(F32)).then_inc(cur_ready, 1)
                    for f in range(NF):
                        split_down(NF * i + f + 1, (f + 1) % 2, (f + 1) % RAW)
                        if f == 0:
                            stop_until(pool, cur_ready, i + 1, tick)
                            fetch(i + 1)
                    for g in range(NG):
                        stop_until(pool, y_ready, NB * i + NB + 2 * g + 2, tick)
                        pool.tensor_scalar(y[:, g, :], y[:, g, :], cur[:, g, 1:2].bitcast(F32), None,
                                           ALU.mult).then_inc(y_scaled, 1)
                        stop_until(pool, y_scaled, NG * i + g + 1, tick)
                        pool.indirect_dma_start(
                            out=acc_d, out_offset=bass.IndirectOffsetOnAxis(ap=cur[:, g, 0:1].bitcast(U32), axis=0),
                            in_=y[:, g, :], in_offset=None, compute_op=ALU.add).then_inc(y_out, 16)
                    pool.wait_ge(y_out, 16 * NG * i + 16 * NG)
                    pool.sem_inc(y_free, 1)
                pool.wait_ge(g_in, n * (16 * NG) + 16 * NG)

            @block.tensor
            def _(pe):
                pe.sem_inc(down_mm, 1)
                n = number(pe)

                def turn(i, b):
                    g, h = divmod(b, 2)
                    if b >= 2:
                        pe.wait_ge(xl_ready, NB * i + b - 1)
                    for k in range(4):
                        last = pe.transpose(gu[b % 2][:, k * P:(k + 1) * P],
                                            xg[:, g, (4 * h + k) * P:(4 * h + k + 1) * P], ident[:, :])
                    last.then_inc(turned, 1)

                def gate_up(i, f):
                    pe.wait_ge(wgl_ready, NF * i + f + 1)
                    if f == 0:
                        pe.wait_ge(xl_ready, NB * i + NB)
                    h, l = wgh[f % 2], wgl[f % 2]
                    for j in range(2):
                        if f:
                            pe.wait_ge((clip, gu_read)[j], NF * i + f)
                        for k in range(KD):
                            for w, x in ((h, xh), (h, xl), (l, xh)):
                                last = pe.matmul(gu[j][:, 0:size], w[:, k, j, :], x[:, k, :], start=(k == 0 and x is xh and w is h),
                                                 stop=(k == KD - 1 and w is l))
                        last.then_inc(gu_mm, 1)

                def down_product(i, f, g):
                    if g == 0:
                        pe.wait_ge(wdl_ready, NF * i + f + 1)
                        pe.wait_ge(act_ready, NF * i + f + 1)
                        if f == 0:
                            pe.wait_ge(y_ready, NB * i + NB)
                    z = f % 2
                    for h in range(2):
                        for a, w in ((ath, wdh), (ath, wdl), (atl, wdh)):
                            last = pe.matmul(down[2 * g + h][:, :], a[z][:, g * P:(g + 1) * P],
                                             w[z][:, h * 512:(h + 1) * 512], start=(f == 0 and a is ath and w is wdh),
                                             stop=(f == NF - 1 and a is atl))
                    if g == NG - 1:
                        last.then_inc(down_mm, 1)

                pe.wait_ge(g_in, 16 * NG)
                for b in range(NB):
                    turn(0, b)
                with pe.Fori(0, n) as i:
                    gate_up(i, 0)
                    for f in range(1, NF):
                        gate_up(i, f)
                        for g in range(NG):
                            down_product(i, f - 1, g)
                    pe.wait_ge(g_in, 16 * NG * i + 32 * NG)
                    pe.wait_ge(gu_read, NF * i + NF)
                    for g in range(NG):
                        turn(i + 1, 2 * g)
                        turn(i + 1, 2 * g + 1)
                        down_product(i, NF - 1, g)

            @block.scalar
            def _(act):
                n = number(act)

                def split_gate_up(i, f, free=None):
                    if free is not None:
                        act.wait_ge(gu_mm, free)
                    act.wait_ge(wg_in[f % RAW], 16 * (NF // RAW) * i + 16 * (f // RAW) + 16)
                    act.activation(flat(wgh[f % 2][:, :, :, :]), flat(wg[f % RAW][:, :, :, :]), ACT.Copy).then_inc(
                        wgh_ready, 1)

                def split_down(i, f, free=None):
                    if free is not None:
                        act.wait_ge(down_mm, free)
                    act.wait_ge(wd_in[f % RAW], 16 * (NF // RAW) * i + 16 * (f // RAW) + 16)
                    act.activation(wdh[f % 2][:, :], wd[f % RAW][:, :], ACT.Copy).then_inc(wdh_ready, 1)

                def save_x(i):
                    for b in range(NB):
                        g, h = divmod(b, 2)
                        act.wait_ge(turned, NB * i + b + 1)
                        act.activation(xh[:, 4 * h:4 * h + 4, g * P:(g + 1) * P],
                                       gu[b % 2][:, :].rearrange("p (k n) -> p k n", k=4), ACT.Copy).then_inc(xh_ready, 1)
                split_gate_up(0, 0)
                save_x(0)
                split_down(0, 0)
                split_gate_up(0, 1)
                with act.Fori(0, n) as i:
                    for f in range(NF):
                        act.wait_ge(clip, NF * i + f + 1)
                        act.activation(sg[f % 2][:, :], t1[f % 2][:, :], ACT.Sigmoid, scale=ALPHA).then_inc(sig, 1)
                        if f == NF - 1:
                            save_x(i + 1)
                        di, nf = divmod(f + 2, NF)
                        split_gate_up(i + di, nf, 2 * NF * i + 2 * f + 2)
                        di, nf = divmod(f + 1, NF)
                        split_down(i + di, nf, NF * i + f + 1)

            @block.vector
            def _(dve):
                tt, tsc, stt = dve.tensor_tensor, dve.tensor_scalar, dve.scalar_tensor_tensor
                dve.sem_inc(y_ready, NB)
                n = number(dve)

                def split_gate_up(s, z, r):
                    dve.wait_ge(wgh_ready, s + 1)
                    tt(flat(wgl[z][:, :, :, :]), flat(wg[r][:, :, :, :]), flat(wgh[z][:, :, :, :]).bitcast(F32),
                       ALU.subtract).then_inc(wgl_ready, 1)

                def save_x(i):
                    for b in range(NB):
                        g, h = divmod(b, 2)
                        part = (slice(None), slice(4 * h, 4 * h + 4), slice(g * P, (g + 1) * P))
                        dve.wait_ge(xh_ready, NB * i + b + 1)
                        tt(xl[part], gu[b % 2][:, :].rearrange("p (k n) -> p k n", k=4), xh[part].bitcast(F32),
                           ALU.subtract).then_inc(xl_ready, 1)
                split_gate_up(0, 0, 0)
                save_x(0)
                split_gate_up(1, 1, 1)
                with dve.Fori(0, n) as i:
                    chain = Steps(dve, at_step, 2 * NF * i)
                    dve.wait_ge(b_in, 16 * i + 16)
                    dve.tensor_copy(bgu[:, 0:NF], bin_[:, 0:NF])
                    tsc(bgu[:, NF:], bin_[:, NF:], 1.0, None, ALU.add).then_inc(b_ready, 1)
                    dve.wait_ge(b_ready, i + 1)
                    for f in range(NF):
                        z = f % 2
                        dve.wait_ge(gu_mm, 2 * NF * i + 2 * f + 1)
                        tsc(t1[z][:, :], gu[0][:, 0:size], bgu[:, f:f + 1], LIMIT, ALU.add, ALU.min).then_inc(clip, 1)
                        dve.wait_ge(gu_mm, 2 * NF * i + 2 * f + 2)
                        tsc(t2[z][:, :], gu[1][:, 0:size], bgu[:, NF + f:NF + f + 1], LIMIT + 1.0, ALU.add,
                            ALU.min).then_inc(gu_read, 1)
                        dve.wait_ge(sig, NF * i + f + 1)
                        tt(t4[z][:, :], t1[z][:, :], sg[z][:, :], ALU.mult).then_inc(prod, 1)
                        dve.wait_ge(prod, NF * i + f + 1)
                        chain(stt(at[z][:, :], t2[z][:, :], 1.0 - LIMIT, t4[z][:, :], ALU.max, ALU.mult))
                        if f:
                            dve.wait_ge(down_mm, NF * i + f)
                        chain(dve.tensor_copy(ath[z][:, :], at[z][:, :]))
                        tt(atl[z][:, :], at[z][:, :], ath[z][:, :].bitcast(F32), ALU.subtract).then_inc(act_ready, 1)
                        if f == NF - 1:
                            save_x(i + 1)
                        split_gate_up(NF * i + f + 2, z, (f + 2) % RAW)
                    dve.wait_ge(bd_in, 16 * i + 16)
                    dve.wait_ge(y_free, i + 1)
                    dve.wait_ge(down_mm, NF * i + NF + 1)
                    for b in range(NB):
                        g, h = divmod(b, 2)
                        tt(y[:, g, h * 512:(h + 1) * 512], down[b][:, :], bd[:, h * 512:(h + 1) * 512],
                           ALU.add).then_inc(y_ready, 1)


def hybrid_layer(nc, a, acc_d):
    scratch = lambda name, shape, dt=F32: nc.dram_tensor(name, list(shape), dt, kind="Internal").ap()
    att_d = scratch("att_d", [len(GROUPS), S, HG * RW])
    yT_d = scratch("yT_d", [P, SW // P, S])
    mixed_d = scratch("mixed_d", [P, KD, S])
    rows_d = scratch("rows_d", [len(GROUPS) * HG, STEPS_W])
    h2_d = scratch("h2_d", [DUMP, D])
    slots_d = scratch("slots_d", [SLOTS, 2], I32)
    table_d = scratch("table_d", [2, P, 4], I32)
    with ExitStack() as outer:
        keep = Tools(nc, outer, "k")
        ident, jflip, upper, ones = (keep.sb(n, [P, P]) for n in ("ident", "jflip", "upper", "ones"))
        make_constants(nc, ident, jflip, upper, ones)
        with ExitStack() as ctx:
            hT = Tools(nc, ctx, "k").sb("hT", [P, KD, S])
            normalise_input(nc, a["x"], a["g_mix"], hT, ident)
            s5(nc, hT, ident, a["w_in"][:, QKV:QKV + SW].rearrange("(k p) n -> p k n", p=P),
               [a[k] for k in ("a_re", "a_im", "log_dt", "b_re", "b_im", "c_re", "c_im", "d_skip")], yT_d)
            with ExitStack() as inner:
                bias = Tools(nc, inner, "k").sb("bias", [P, len(GROUPS) * HG, 2 * P])
                bias_tables(nc, a["rel_bias"], a["onehot"], rows_d, bias, jflip)
                attention(nc, hT, a["w_in"], a["q_gain"], a["k_gain"], bias, ident, att_d)
            mix(nc, hT, ident, yT_d, att_d, a["w_glu"], a["b_glu"], a["mix_w"], mixed_d)
        route(nc, a["x"], mixed_d, a["w_out"], a["g_ffn"], a["w_router"], a["b_router"], a["empty_slots"], ident,
              upper, ones, acc_d, h2_d, slots_d, table_d)
        for kind, size in enumerate((LARGE, SMALL)):
            experts(nc, size, ident, a["w_gu"], a["b_gu"], a["w_down"], a["b_down"], h2_d, acc_d, slots_d,
                    table_d[kind])


def by_state(w):
    w = w.reshape(PAIRS, 2, SN, *w.shape[2:])
    return np.moveaxis(w, 0, 2).reshape(2 * SN, PAIRS, *w.shape[3:])


def out_tiles(w):
    return w.reshape(-1, P, w.shape[1] // P, P).transpose(2, 1, 0, 3)


def k_tiles(w):
    return w.reshape(-1, P, w.shape[1]).transpose(1, 0, 2)


def kernel(x, g_mix, w_in, q_gain, k_gain, rel_bias, ssm_a_re, ssm_a_im, ssm_log_dt, ssm_b_re, ssm_b_im, ssm_c_re,
           ssm_c_im, ssm_d, w_glu, b_glu, w_attn_proj, w_ssm_proj, w_out, g_ffn, w_router, b_router, w_gate_up,
           b_gate_up, w_down, b_down):
    import concourse.bacc as bacc
    from concourse.bass_utils import run_bass_kernel_spmd

    w_in0 = np.asarray(w_in)[0]
    gates = QKV + SW
    slots = np.zeros((SLOTS, 2), np.int32)
    slots[:, 0] = S + np.arange(SLOTS) % LARGE
    arrays = {
        "x": np.asarray(x)[0], "g_mix": np.asarray(g_mix)[0], "w_in": w_in0,
        "q_gain": np.asarray(q_gain)[0].T, "k_gain": np.asarray(k_gain)[0].T,
        "rel_bias": np.asarray(rel_bias), "onehot": bucket_onehot(),
        "a_re": by_state(np.asarray(ssm_a_re)[0]), "a_im": by_state(np.asarray(ssm_a_im)[0]),
        "log_dt": np.asarray(ssm_log_dt)[0].reshape(PAIRS, 2).T,
        "b_re": by_state(np.asarray(ssm_b_re)[0]), "b_im": by_state(np.asarray(ssm_b_im)[0]),
        "c_re": by_state(np.asarray(ssm_c_re)[0].transpose(0, 2, 1)),
        "c_im": by_state(np.asarray(ssm_c_im)[0].transpose(0, 2, 1)),
        "d_skip": np.asarray(ssm_d)[0].reshape(SG, SC).T,
        "w_glu": k_tiles(np.asarray(w_glu)[0]), "b_glu": np.asarray(b_glu)[0].reshape(-1, P).T,
        "mix_w": np.concatenate([out_tiles(m) for m in (
            w_in0[:, gates:gates + D], w_in0[:, gates + D:], np.asarray(w_attn_proj)[0], np.asarray(w_ssm_proj)[0])],
            axis=2),
        "w_out": k_tiles(np.asarray(w_out)[0]), "g_ffn": np.asarray(g_ffn)[0],
        "w_router": k_tiles(np.asarray(w_router)[0]), "b_router": np.asarray(b_router)[0], "empty_slots": slots,
        "w_gu": np.asarray(w_gate_up)[0].reshape(NE, KD, P, 2, NF, P).transpose(0, 4, 2, 1, 3, 5),
        "b_gu": np.asarray(b_gate_up)[0].reshape(NE, 2 * NF, P).transpose(0, 2, 1),
        "w_down": np.asarray(w_down)[0], "b_down": np.asarray(b_down)[0],
    }
    arrays = {k: np.ascontiguousarray(v) for k, v in arrays.items()}
    nc = bacc.Bacc("TRN2", target_bir_lowering=False, num_devices=1)
    a = {k: nc.dram_tensor(f"in_{k}", v.shape, mybir.dt.from_np(v.dtype), kind="ExternalInput").ap()
         for k, v in arrays.items()}
    out = nc.dram_tensor("out", [DUMP, D], F32, kind="ExternalOutput").ap()
    hybrid_layer(nc, a, out)
    r = run_bass_kernel_spmd(nc, [{f"in_{k}": v for k, v in arrays.items()}], core_ids=[0])
    return r.results[0]["out"][:S].reshape(1, S, D)
```
